# Optimizing a Trainium2 kernel written in Bass

```python
import jax, jax.numpy as jnp
from jax import lax
import numpy as np

D_MODEL = 1024
BATCH = 1
SEQ = 1024
DEPTH = 1
DEC_BATCH = 8
DEC_SEQ = 1
PAST_LEN = 8192
PAGE_SIZE = 128

H_RET = 8
DK_RET = 64
DV_RET = 64
RET_WIDTH = H_RET * DV_RET
RET_CHUNK = 128
RET_ROPE_BASE = 10000.0
H_ATT = 8
HD_ATT = 64
ATT_WIDTH = H_ATT * HD_ATT
ATT_ROPE_THETA = 500000.0
ROT_DIMS = HD_ATT // 4
DILATIONS = ((128, 1), (512, 4), (2048, 16))
WINDOW_MAX = 2048
Q_BLOCK = 128
MIX_WIDTH = RET_WIDTH + ATT_WIDTH
PROJ_WIDTH = 4 * RET_WIDTH + 3 * ATT_WIDTH
PROJ_SPLITS = (RET_WIDTH, 2 * RET_WIDTH, 3 * RET_WIDTH, 4 * RET_WIDTH,
               4 * RET_WIDTH + ATT_WIDTH, 4 * RET_WIDTH + 2 * ATT_WIDTH)
D_FF = 2816
CONV_W = 3
PLE_DIM = 256
LN_EPS = 1e-5
ALPHA = (2 * DEPTH) ** 0.25
BETA = (8 * DEPTH) ** -0.25

kernel_name = "hymba_retnet_dilated_convffn_step"

def layer_norm(x, g, b):
    xf = x.astype(jnp.float32)
    mu = jnp.mean(xf, axis=-1, keepdims=True)
    var = jnp.mean(jnp.square(xf - mu), axis=-1, keepdims=True)
    return ((xf - mu) * lax.rsqrt(var + LN_EPS)).astype(x.dtype) * g + b

def head_norm(x):
    mu = jnp.mean(x, axis=-1, keepdims=True)
    var = jnp.mean(jnp.square(x - mu), axis=-1, keepdims=True)
    return (x - mu) * lax.rsqrt(var + LN_EPS)

def rotary(x, pos, n_rot, base):
    half = n_rot // 2
    inv = base ** (-jnp.arange(half, dtype=jnp.float32) / half)
    ang = pos.astype(jnp.float32)[:, None] * inv[None, :]
    cos = jnp.cos(ang)[:, None, :]
    sin = jnp.sin(ang)[:, None, :]
    xr = x[..., :n_rot].astype(jnp.float32)
    x1, x2 = xr[..., :half], xr[..., half:]
    rot = jnp.concatenate([x1 * cos - x2 * sin, x2 * cos + x1 * sin], axis=-1).astype(x.dtype)
    return jnp.concatenate([rot, x[..., n_rot:]], axis=-1)

def project(h, w_in, pos):
    B, T, _ = h.shape
    q_r, k_r, v_r, g_r, q_a, k_a, v_a = jnp.split(h @ w_in, PROJ_SPLITS, axis=-1)
    q_r = rotary(q_r.reshape(B, T, H_RET, DK_RET), pos, DK_RET, RET_ROPE_BASE)
    k_r = rotary(k_r.reshape(B, T, H_RET, DK_RET), pos, DK_RET, RET_ROPE_BASE) * (DK_RET ** -0.5)
    v_r = v_r.reshape(B, T, H_RET, DV_RET)
    q_a = rotary(q_a.reshape(B, T, H_ATT, HD_ATT), pos, ROT_DIMS, ATT_ROPE_THETA)
    k_a = rotary(k_a.reshape(B, T, H_ATT, HD_ATT), pos, ROT_DIMS, ATT_ROPE_THETA)
    v_a = v_a.reshape(B, T, H_ATT, HD_ATT)
    return q_r, k_r, v_r, g_r, q_a, k_a, v_a

def _log_gamma():
    return jnp.log(1.0 - 2.0 ** (-5.0 - jnp.arange(H_RET, dtype=jnp.float32)))

def retention_chunk(state, qkv):
    q, k, v = qkv
    C = q.shape[1]
    lg = _log_gamma()
    idx = jnp.arange(C, dtype=jnp.float32)
    rel = idx[:, None] - idx[None, :]
    decay = jnp.where(rel >= 0, jnp.exp(lg[:, None, None] * jnp.maximum(rel, 0.0)), 0.0)
    inner = jnp.einsum('bhij,bjhe->bihe', jnp.einsum('bihd,bjhd->bhij', q, k) * decay, v)
    cross = jnp.einsum('bihd,bhde->bihe', q, state) * jnp.exp(lg[None, :] * (idx[:, None] + 1.0))[None, :, :, None]
    k_dec = k * jnp.exp(lg[None, :] * (C - 1.0 - idx[:, None]))[None, :, :, None]
    new_state = jnp.exp(lg * C)[None, :, None, None] * state + jnp.einsum('bjhd,bjhe->bhde', k_dec, v)
    return new_state, inner + cross

def retention_prompt(q, k, v):
    B, S, H, _ = q.shape
    n = S // RET_CHUNK

    def chunks(t):
        return jnp.moveaxis(t.astype(jnp.float32).reshape(B, n, RET_CHUNK, H, t.shape[-1]), 1, 0)

    s0 = jnp.zeros((B, H, DK_RET, DV_RET), jnp.float32)
    fin, o = lax.scan(retention_chunk, s0, (chunks(q), chunks(k), chunks(v)))
    return jnp.moveaxis(o, 0, 1).reshape(B, S, H, DV_RET), fin

def _masked_softmax_stats(s, valid):
    s = jnp.where(valid, s, -jnp.inf)
    m = jnp.max(s, axis=-1, keepdims=True)
    pr = jnp.exp(s - m)
    den = jnp.sum(pr, axis=-1, keepdims=True)
    return pr / den, (m + jnp.log(den))[..., 0]

def _to_strided(x, d):
    B, S, H, E = x.shape
    return x.reshape(B, S // d, d, H, E).transpose(0, 2, 1, 3, 4).reshape(B * d, S // d, H, E)

def _from_strided(x, B, d):
    L = x.shape[1]
    rest = x.shape[2:]
    x = jnp.moveaxis(x.reshape((B, d, L) + rest), 1, 2)
    return x.reshape((B, L * d) + rest)

def _banded_dilated(q, k, v, span, d):
    B, S, H, E = q.shape
    L = S // d
    nb = -(-L // Q_BLOCK)
    Lp = nb * Q_BLOCK
    qs = jnp.pad(_to_strided(q, d), ((0, 0), (0, Lp - L), (0, 0), (0, 0))).reshape(B * d, nb, Q_BLOCK, H, E)

    def band(t):
        t = jnp.pad(_to_strided(t, d), ((0, 0), (Q_BLOCK, Lp - L), (0, 0), (0, 0)))
        t = t.reshape(B * d, nb + 1, Q_BLOCK, H, E)
        return jnp.concatenate([t[:, :-1], t[:, 1:]], axis=2)

    kw, vw = band(k), band(v)
    s = jnp.einsum('znqhe,znkhe->znhqk', qs, kw, preferred_element_type=jnp.float32) * (E ** -0.5)
    qi = jnp.arange(Q_BLOCK)[:, None]
    ki = jnp.arange(2 * Q_BLOCK)[None, :]
    dist = Q_BLOCK + qi - ki
    kpos = jnp.arange(nb)[:, None, None] * Q_BLOCK + ki[None] - Q_BLOCK
    valid = ((dist >= 0) & (dist <= span))[None] & (kpos >= 0)
    pr, lse = _masked_softmax_stats(s, valid[None, :, None])
    o = jnp.einsum('znhqk,znkhe->znqhe', pr, vw.astype(jnp.float32)).reshape(B * d, Lp, H, E)[:, :L]
    lse = jnp.swapaxes(lse, 2, 3).reshape(B * d, Lp, H)[:, :L]
    return _from_strided(o, B, d), _from_strided(lse, B, d)

def _gathered_dilated(q, k_all, v_all, span, d, n_past):
    E = q.shape[-1]
    T = q.shape[1]
    idx = n_past + jnp.arange(T)[:, None] - d * jnp.arange(span + 1)[None, :]
    valid = idx >= 0
    idc = jnp.clip(idx, 0)
    kg = k_all[:, idc]
    vg = v_all[:, idc]
    s = jnp.einsum('bthe,btjhe->bthj', q, kg, preferred_element_type=jnp.float32) * (E ** -0.5)
    pr, lse = _masked_softmax_stats(s, valid[None, :, None, :])
    return jnp.einsum('bthj,btjhe->bthe', pr, vg.astype(jnp.float32)), lse

def combine_by_denominator(outs, lses):
    w = jax.nn.softmax(jnp.stack(lses, axis=0), axis=0)
    return jnp.einsum('pbth,pbthe->bthe', w, jnp.stack(outs, axis=0))

def dilated_attention_prompt(q, k, v):
    outs, lses = [], []
    for window, dil in DILATIONS:
        o, l = _banded_dilated(q, k, v, window // dil, dil)
        outs.append(o)
        lses.append(l)
    return combine_by_denominator(outs, lses).astype(q.dtype)

def dilated_attention_sample(q, k_new, v_new, k_buf, v_buf):
    n_past = k_buf.shape[1]
    k_all = jnp.concatenate([k_buf.astype(k_new.dtype), k_new], axis=1)
    v_all = jnp.concatenate([v_buf.astype(v_new.dtype), v_new], axis=1)
    outs, lses = [], []
    for window, dil in DILATIONS:
        o, l = _gathered_dilated(q, k_all, v_all, window // dil, dil, n_past)
        outs.append(o)
        lses.append(l)
    return combine_by_denominator(outs, lses).astype(q.dtype)

def merge_heads(ret_o, g_r, att_o, w_out):
    B, T = ret_o.shape[:2]
    r = head_norm(ret_o).reshape(B, T, RET_WIDTH).astype(g_r.dtype) * jax.nn.silu(g_r)
    a = att_o.reshape(B, T, ATT_WIDTH)
    return jnp.concatenate([r, a], axis=-1) @ w_out

def conv_ffn(h, prefix, w_up, conv_w, conv_b, w_down):
    T = h.shape[1]
    u = h @ w_up
    up = jnp.concatenate([prefix.astype(u.dtype), u], axis=1)
    c = conv_b + sum(conv_w[j] * up[:, j:j + T] for j in range(CONV_W))
    a, g = jnp.split(c, 2, axis=-1)
    return (a * jax.nn.gelu(g)) @ w_down, up[:, T:]

def channel_and_embed(h, mix, p, prefix, ln1_g, ln1_b, w_up, conv_w, conv_b, w_down,
                      w_ple_gate, w_ple_proj, ln2_g, ln2_b):
    h1 = layer_norm(ALPHA * h + mix, ln1_g, ln1_b)
    f, conv_state = conv_ffn(h1, prefix, w_up, conv_w, conv_b, w_down)
    e = jax.nn.sigmoid(h1 @ w_ple_gate) * (p @ w_ple_proj)
    return layer_norm(ALPHA * h1 + f + e, ln2_g, ln2_b), conv_state

def setup_inputs(seed: int = 0) -> dict:
    key = jax.random.key(seed)
    ks = jax.random.split(key, 22)
    f32 = jnp.float32
    win_buf = min(WINDOW_MAX, PAST_LEN)
    two_f = 2 * D_FF

    def nrm(k, shape, scale):
        return jax.random.normal(k, shape, f32) * scale

    return {
        'x_prompt': nrm(ks[0], (BATCH, SEQ, D_MODEL), 1.0),
        'x_sample': nrm(ks[1], (DEC_BATCH, DEC_SEQ, D_MODEL), 1.0),
        'cache_k_win': nrm(ks[2], (DEPTH, DEC_BATCH, win_buf, H_ATT, HD_ATT), 1.0),
        'cache_v_win': nrm(ks[3], (DEPTH, DEC_BATCH, win_buf, H_ATT, HD_ATT), 1.0),
        'state_ret': nrm(ks[4], (DEPTH, DEC_BATCH, H_RET, DK_RET, DV_RET), 0.5),
        'state_conv': nrm(ks[5], (DEPTH, DEC_BATCH, CONV_W - 1, two_f), 1.0),
        'p_prompt': nrm(ks[6], (DEPTH, BATCH, SEQ, PLE_DIM), 1.0),
        'p_sample': nrm(ks[7], (DEPTH, DEC_BATCH, DEC_SEQ, PLE_DIM), 1.0),
        'ln_in_g': 1.0 + nrm(ks[8], (D_MODEL,), 0.02),
        'ln_in_b': nrm(ks[9], (D_MODEL,), 0.02),
        'w_in': nrm(ks[10], (DEPTH, D_MODEL, PROJ_WIDTH), D_MODEL ** -0.5),
        'w_out': nrm(ks[11], (DEPTH, MIX_WIDTH, D_MODEL), BETA * MIX_WIDTH ** -0.5),
        'ln1_g': 1.0 + nrm(ks[12], (DEPTH, D_MODEL), 0.02),
        'ln1_b': nrm(ks[13], (DEPTH, D_MODEL), 0.02),
        'w_up': nrm(ks[14], (DEPTH, D_MODEL, two_f), D_MODEL ** -0.5),
        'conv_w': nrm(ks[15], (DEPTH, CONV_W, two_f), CONV_W ** -0.5),
        'conv_b': nrm(ks[16], (DEPTH, two_f), 0.02),
        'w_down': nrm(ks[17], (DEPTH, D_FF, D_MODEL), BETA * D_FF ** -0.5),
        'w_ple_gate': nrm(ks[18], (DEPTH, D_MODEL, D_MODEL), D_MODEL ** -0.5),
        'w_ple_proj': nrm(ks[19], (DEPTH, PLE_DIM, D_MODEL), BETA * PLE_DIM ** -0.5),
        'ln2_g': 1.0 + nrm(ks[20], (DEPTH, D_MODEL), 0.02),
        'ln2_b': nrm(ks[21], (DEPTH, D_MODEL), 0.02),
    }

def reference(x_prompt, x_sample, cache_k_win, cache_v_win, state_ret, state_conv, p_prompt, p_sample,
              ln_in_g, ln_in_b, w_in, w_out, ln1_g, ln1_b, w_up, conv_w, conv_b, w_down,
              w_ple_gate, w_ple_proj, ln2_g, ln2_b):
    B, S, _ = x_prompt.shape
    T = x_sample.shape[1]
    pos_p = jnp.arange(S, dtype=jnp.int32)
    pos_s = PAST_LEN + jnp.arange(T, dtype=jnp.int32)
    keep = min(WINDOW_MAX, S)
    hp = layer_norm(x_prompt, ln_in_g, ln_in_b)
    hs = layer_norm(x_sample, ln_in_g, ln_in_b)
    kp_l, vp_l, rp_l, cp_l, ks_l, vs_l, rs_l, cs_l = [], [], [], [], [], [], [], []
    for i in range(DEPTH):
        q_r, k_r, v_r, g_r, q_a, k_a, v_a = project(hp, w_in[i], pos_p)
        ret_o, ret_fin = retention_prompt(q_r, k_r, v_r)
        att_o = dilated_attention_prompt(q_a, k_a, v_a)
        mix = merge_heads(ret_o, g_r, att_o, w_out[i])
        hp, conv_p = channel_and_embed(hp, mix, p_prompt[i], jnp.zeros((B, CONV_W - 1, 2 * D_FF), hp.dtype),
                                       ln1_g[i], ln1_b[i], w_up[i], conv_w[i], conv_b[i], w_down[i],
                                       w_ple_gate[i], w_ple_proj[i], ln2_g[i], ln2_b[i])
        kp_l.append(k_a[:, S - keep:])
        vp_l.append(v_a[:, S - keep:])
        rp_l.append(ret_fin.astype(state_ret.dtype))
        cp_l.append(conv_p)
        q_r, k_r, v_r, g_r, q_a, k_a, v_a = project(hs, w_in[i], pos_s)
        ret_new, ret_o = retention_chunk(state_ret[i].astype(jnp.float32),
                                         (q_r.astype(jnp.float32), k_r.astype(jnp.float32), v_r.astype(jnp.float32)))
        att_o = dilated_attention_sample(q_a, k_a, v_a, cache_k_win[i], cache_v_win[i])
        mix = merge_heads(ret_o, g_r, att_o, w_out[i])
        hs, conv_s = channel_and_embed(hs, mix, p_sample[i], state_conv[i],
                                       ln1_g[i], ln1_b[i], w_up[i], conv_w[i], conv_b[i], w_down[i],
                                       w_ple_gate[i], w_ple_proj[i], ln2_g[i], ln2_b[i])
        ks_l.append(k_a)
        vs_l.append(v_a)
        rs_l.append(ret_new.astype(state_ret.dtype))
        cs_l.append(conv_s)
    return (hp, hs, jnp.stack(kp_l), jnp.stack(vp_l), jnp.stack(rp_l), jnp.stack(cp_l),
            jnp.stack(ks_l), jnp.stack(vs_l), jnp.stack(rs_l), jnp.stack(cs_l))


_drawn_inputs = setup_inputs


def setup_inputs(seed=0):
    import zlib

    import numpy as np

    out = dict(_drawn_inputs(seed))
    spreads = {}
    factors = {'ln1_g': 2.824, 'ln1_b': 2.692, 'conv_b': 6.469, 'ln2_g': 2.943, 'ln2_b': 2.748}
    for name, (base, spread) in spreads.items():
        noise = np.random.default_rng([zlib.crc32(name.encode()), seed]).standard_normal(out[name].shape)
        drawn = base * np.exp(spread * noise) if base else spread * noise
        out[name] = __import__('jax').numpy.asarray(drawn.astype(out[name].dtype))
    for name, factor in factors.items():
        out[name] = (out[name] * factor).astype(out[name].dtype)
    return out
```

```python
from contextlib import ExitStack

import numpy as np
import concourse.bass as bass
from concourse import mybir

F32 = mybir.dt.float32
F16 = mybir.dt.float16
ALU = mybir.AluOpType
ACT = mybir.ActivationFunctionType
AX_X = mybir.AxisListType.X
ds = bass.ds

P = 128
D = 1024
SEQ = 1024
NB = 8
NT = SEQ // P
KD = D // P
H = 8
E = 64
HP = H // 2
HW = H * E
PAST = 8192
WIN = 2048
D_FF = 2816
NCH = D_FF // P
PLE = 256
EPS = 1e-5
ALPHA = 2.0 ** 0.25
S_ACT = 16.0
S_W = 64.0
UNSCALE = 1.0 / (S_ACT * S_W)
ATT_SCALE = E ** -0.5
NEG = -1e30
BASE = 4
PASSES = ((0, 0), (0, 1), (1, 0))


Q_ORDER = [(h, q) for h in range(2) for q in (7, 0, 6, 1, 5, 2, 4, 3)]


def build(nc, x_prompt, x_sample, cache_k, cache_v, state_ret, state_conv, p_prompt, p_sample,
          ln_in_g, ln_in_b, w_in, w_out, ln1_g, ln1_b, w_up, conv_w, conv_b, w_down,
          w_ple_gate, w_ple_proj, ln2_g, ln2_b,
          c_ident, c_rope_ret, c_rope_att, c_decay, c_gq, c_kdec, c_gchunk, c_mask, c_gsample, c_own,
          y_prompt, y_sample, kwin_p, vwin_p, ret_p, conv_p, kwin_s, vwin_s, ret_s, conv_s, debug=None):
    outer = ExitStack()
    with outer:
        stage = ["all"]

        def sb(stack, name, shape, dt=F32):
            return stack.enter_context(nc.sbuf_tensor(f"{stage[0]}_{name}", shape, dt))

        own, before = [], []

        def sems(names):
            made = [nc.alloc_semaphore(name=f"{stage[0]}_{n}") for n in names.split()]
            own.extend(made)
            return made

        def count_from_base(pool):
            for s in own:
                pool.sem_inc(s, BASE)

        def clear_before(sp):
            for s in before:
                sp.sem_clear(s)

        def end_stage():
            for s in before:
                nc.release_semaphore(s)
            before[:] = own
            own.clear()

        PS = outer.enter_context(nc.psum_tensor("PS", [P, 8, 512], F32))
        HRES = sb(outer, "HRES", [P, NT + 1, D])
        HT = sb(outer, "HT", [P, 2, KD, SEQ + NB], F16)
        IDENT = sb(outer, "IDENT", [P, P])
        EPSC = sb(outer, "EPSC", [P, 2])
        MTS = sb(outer, "MTS", [P, 2, KD, NB], F16)
        CW = sb(outer, "CW", [P, 4, 2 * NCH])
        CWS = sb(outer, "CWS", [P, 3, 2 * NCH])
        ST = sb(outer, "ST", [P, 2 * NB, 2 * NCH])
        scratch = nc.dram_tensor("scratch", (7, NB, HW), F32, kind="Internal").ap()

        WS = sb(outer, "WS", [P, 2, 2, KD, 512], F16)

        mid = outer.enter_context(ExitStack())
        MT = sb(mid, "MT", [P, 2, KD, SEQ], F16)

        w_in_v = w_in.rearrange("a (k p) (j h n) -> p (a k) j h n", p=P, j=7, n=P)

        proj = outer.enter_context(ExitStack())
        STG = sb(proj, "STG", [P, 2, 2, 512])
        stage[0] = "norm_in"
        with ExitStack() as st:
            XS = sb(st, "XS", [P, 2, D])
            HS = sb(st, "HS", [P, 2, D])
            XN = sb(st, "XN", [P, 2, D])
            LNP = sb(st, "LNP", [P, 2, D])
            BST = sb(st, "BST", [P, 2, 6])
            MV = sb(st, "MV", [P, 2])
            VE = sb(st, "VE", [P, 1])
            RSTD = sb(st, "RSTD", [P, 1])
            (const_in, x_free, half_ready, stats_done, aggr_done, var_ready, rstd_ready, xn_ready, gained,
             h_ready, h_copied, turned, hi_ready, lo_ready, w_free, whi, wlo) = sems(
                "const_in x_free half_ready stats_done aggr_done var_ready rstd_ready xn_ready gained "
                    "h_ready h_copied turned hi_ready lo_ready w_free whi wlo")
            stats_seen, = sems("stats_seen")
            CRAW = sb(st, "CRAW", [P, 4, P])
            SRAW = sb(st, "SRAW", [P, 2 * NB, P])
            par_in, par_turned = sems("par_in par_turned")
            x_in = sems("x_in0 x_in1 x_in2")
            w_in_s = sems("w_in_s0 w_in_s1")
            with nc.Block() as block:
                @block.sync
                def _(sp):
                    sp.sem_inc(x_free, 2)
                    sp.sem_inc(w_free, 2)
                    sp.dma_start(LNP[:, 0], ln_in_g.rearrange("(a n) -> a n", a=1).broadcast_to([P, D])).then_inc(const_in, 16)
                    sp.dma_start(LNP[:, 1], ln_in_b.rearrange("(a n) -> a n", a=1).broadcast_to([P, D])).then_inc(const_in, 16)
                    sp.dma_start(IDENT[:], c_ident).then_inc(const_in, 16)
                    with sp.Fori(0, NT // 2) as i:
                        for u in range(2):
                            sp.wait_ge(x_free, BASE + 2 * i + u + 1)
                            sp.dma_start(XS[:, u], x_prompt[0, ds((2 * i + u) * P, P), :]).then_inc(x_in[u], 16)
                    sp.wait_ge(x_free, BASE + NT + 1)
                    sp.dma_start(XS[:NB, 0], x_sample[:, 0, :]).then_inc(x_in[2], 16)
                    sp.dma_start(CRAW[:2 * NCH, 0:3], conv_w.rearrange("a j (c f) -> c (a j) f", f=P)).then_inc(par_in, 16)
                    sp.dma_start(CRAW[:2 * NCH, 3], conv_b.rearrange("a (c f) -> (a c) f", f=P)).then_inc(par_in, 16)
                    sp.dma_start(SRAW[:2 * NCH], state_conv.rearrange("a b j (c f) -> c (a b j) f", f=P)).then_inc(par_in, 16)
                    for c in range(4):
                        sp.wait_ge(w_free, BASE + c + 1)
                        for k in range(2):
                            sp.dma_start(STG[:, c % 2, k].rearrange("p (j n) -> p j n", j=4),
                                         w_in_v[:, 2 * c + k, 0:4, 0, :]).then_inc(w_in_s[c % 2], 16)
                    clear_before(sp)

                @block.vector
                def _(dve):
                    nc.vector.memset(EPSC[:], -0.5).then_inc(stats_seen, 1)
                    dve.wait_ge(const_in, BASE + 48)

                    def norm(t, u, n, sem, count, free=True):
                        dve.wait_ge(sem, BASE + count)
                        for c in range(2):
                            nc.vector.bn_stats(BST[:n, c], XS[:n, u, c * 512:(c + 1) * 512]).then_inc(stats_done, 1)
                        dve.wait_ge(stats_done, BASE + 2 * t + 2)
                        dve.sem_inc(stats_seen, 1)
                        nc.vector.bn_aggr(MV[:n], BST[:n].rearrange("p a b -> p (a b)")).then_inc(aggr_done, 1)
                        dve.wait_ge(aggr_done, BASE + t + 1)
                        nc.vector.tensor_scalar(VE[:n], MV[:n, 1:2], EPS, None, ALU.add).then_inc(var_ready, 1)
                        dve.wait_ge(rstd_ready, BASE + t + 1)
                        if free:
                            dve.wait_ge(h_ready, BASE + t - 1)
                        nc.vector.tensor_scalar(XN[:n, u], XS[:n, u], MV[:n, 0:1], RSTD[:n], ALU.subtract,
                                                ALU.mult).then_inc(xn_ready, 1)
                        dve.wait_ge(xn_ready, BASE + t + 1)
                        nc.vector.tensor_tensor(XN[:n, u], XN[:n, u], LNP[:n, 0], ALU.mult).then_inc(gained, 1)
                        dve.sem_inc(x_free, 1)

                    def low(t, n, b):
                        dve.wait_ge(hi_ready, BASE + t + 1)
                        nc.vector.scalar_tensor_tensor(
                            HT[:, 1, :, ds(t * P, n)], PS[:, b:b + 2].rearrange("p b (k n) -> p (b k) n", k=4)[:, :, :n],
                            S_ACT, HT[:, 0, :, ds(t * P, n)], ALU.mult, ALU.subtract).then_inc(lo_ready, 1)

                    norm(0, 0, P, x_in[0], 16, False)
                    norm(1, 1, P, x_in[1], 16, False)
                    low(0, P, 0)
                    with dve.Fori(0, NT // 2 - 1) as i:
                        for u in range(2):
                            norm(2 * i + u + 2, u, P, x_in[u], 16 * i + 32)
                            low(2 * i + u + 1, P, 2 * (1 - u))
                    norm(NT, 0, NB, x_in[2], 16)
                    low(NT - 1, P, 2)
                    low(NT, NB, 0)
                    for c in range(4):
                        dve.wait_ge(whi, BASE + c + 1)
                        nc.vector.scalar_tensor_tensor(WS[:, 0, 1, 2 * c:2 * c + 2], STG[:, c % 2], S_W,
                                                       WS[:, 0, 0, 2 * c:2 * c + 2], ALU.mult, ALU.subtract).then_inc(w_free, 1)

                @block.gpsimd
                def _(pool):
                    count_from_base(pool)
                    pool.wait_ge(const_in, BASE + 48)
                    pool.wait_ge(stats_seen, BASE + 1)

                    def scale(t, u, n):
                        pool.wait_ge(var_ready, BASE + t + 1)
                        nc.gpsimd.tensor_tensor(RSTD[:n], VE[:n], EPSC[:n, 0:1], ALU.pow).then_inc(rstd_ready, 1)

                    def shift(t, u, n):
                        pool.wait_ge(gained, BASE + t + 1)
                        nc.gpsimd.tensor_tensor(HS[:n, u], XN[:n, u], LNP[:n, 1], ALU.add).then_inc(h_ready, 1)

                    for u in range(2):
                        scale(u, u, P)
                        shift(u, u, P)
                    with pool.Fori(0, NT // 2 - 1) as i:
                        for u in range(2):
                            t = 2 * i + u + 2
                            scale(t, u, P)
                            pool.wait_ge(turned, BASE + t - 1)
                            pool.wait_ge(h_copied, BASE + t - 1)
                            shift(t, u, P)
                    scale(NT, 0, NB)
                    pool.wait_ge(turned, BASE + NT - 1)
                    pool.wait_ge(h_copied, BASE + NT - 1)
                    shift(NT, 0, NB)

                @block.tensor
                def _(pe):
                    pe.wait_ge(const_in, BASE + 48)

                    def turn(t, u, n):
                        pe.wait_ge(h_ready, BASE + t + 1)
                        for k in range(KD):
                            last = nc.tensor.transpose(PS[:, 2 * u + k // 4, (k % 4) * P:(k % 4) * P + n],
                                                       HS[:n, u, k * P:(k + 1) * P], IDENT[:n, :n])
                        last.then_inc(turned, 1)

                    turn(0, 0, P)
                    turn(1, 1, P)
                    with pe.Fori(0, NT // 2 - 1) as i:
                        for u in range(2):
                            pe.wait_ge(lo_ready, BASE + 2 * i + u + 1)
                            turn(2 * i + u + 2, u, P)
                    pe.wait_ge(lo_ready, BASE + NT - 1)
                    turn(NT, 0, NB)
                    pe.wait_ge(par_in, BASE + 48)
                    for j in range(4 + 2 * NB):
                        src = CRAW[:2 * NCH, j] if j < 4 else SRAW[:2 * NCH, j - 4]
                        mm = nc.tensor.transpose(PS[:, 4 + j // 10, (j % 10) * 2 * NCH:(j % 10 + 1) * 2 * NCH],
                                                 src, IDENT[:2 * NCH, :2 * NCH])
                    mm.then_inc(par_turned, 1)

                @block.scalar
                def _(act):
                    def high(t, u, n):
                        act.wait_ge(h_ready, BASE + t + 1)
                        nc.scalar.activation(HRES[:n, t], HS[:n, u], ACT.Copy).then_inc(h_copied, 1)
                        act.wait_ge(turned, BASE + t + 1)
                        nc.scalar.activation(HT[:, 0, :, ds(t * P, n)],
                                             PS[:, 2 * u:2 * u + 2].rearrange("p b (k n) -> p (b k) n", k=4)[:, :, :n],
                                             ACT.Copy, scale=S_ACT).then_inc(hi_ready, 1)

                    with act.Fori(0, NT // 2) as i:
                        for u in range(2):
                            high(2 * i + u, u, P)
                    high(NT, 0, NB)
                    act.wait_ge(par_turned, BASE + 1)
                    n = 2 * NCH
                    nc.scalar.activation(CW[:].rearrange("p j c -> p (j c)"), PS[:, 4, 0:4 * n], ACT.Copy)
                    nc.scalar.activation(CWS[:].rearrange("p j c -> p (j c)"), PS[:, 4, 0:3 * n], ACT.Copy, scale=UNSCALE)
                    st_rows = ST[:].rearrange("p j c -> p (j c)")
                    nc.scalar.activation(st_rows[:, 0:6 * n], PS[:, 4, 4 * n:10 * n], ACT.Copy)
                    nc.scalar.activation(st_rows[:, 6 * n:16 * n], PS[:, 5, 0:10 * n], ACT.Copy)
                    for c in range(4):
                        act.wait_ge(w_in_s[c % 2], BASE + 32 * (c // 2) + 32)
                        nc.scalar.activation(WS[:, 0, 0, 2 * c:2 * c + 2], STG[:, c % 2], ACT.Copy,
                                             scale=S_W).then_inc(whi, 1)
        end_stage()
        stage[0] = "retention"
        with ExitStack() as st:
            ROPE = sb(st, "ROPE", [P, NT + 1, 2, E // 2])
            DEC = sb(st, "DEC", [P, H, P])
            GQ = sb(st, "GQ", [P, HP, P])
            KDEC = sb(st, "KDEC", [P, HW])
            GCH = sb(st, "GCH", [P, HP])
            STATE = sb(st, "STATE", [P, HP, P])
            T1 = sb(st, "T1", [P, 256])
            T2 = sb(st, "T2", [P, 256])
            QK = sb(st, "QK", [P, 2, 256])
            QKT = sb(st, "QKT", [P, 2, 256])
            V = sb(st, "V", [P, NT, P])
            G = sb(st, "G", [P, NT, P])
            QG = sb(st, "QG", [P, 4, P])
            KG = sb(st, "KG", [P, 4, P])
            SD = sb(st, "SD", [P, 2, 2, P])
            BST = sb(st, "BST", [P, 2, 6])
            MV = sb(st, "MV", [P, 2, 2])
            VE = sb(st, "VE", [P, 2])
            RSTD = sb(st, "RSTD", [P, 2])
            RN = sb(st, "RN", [P, P])
            R = sb(st, "R", [P, 2, P])
            ZS = sb(st, "ZS", [P, 512])
            Z, TB, SB, OB, UB, RB = (PS[:, 0:2], PS[:, 2, 0:256], PS[:, 3:5, 0:P], PS[:, 7, 0:P], PS[:, 5, 0:P],
                                     PS[:, 6, 0:P])
            (tab_in, z_ready, z_turned, v_ready, halves, rotated, qkt_ready, qg_ready, kg_ready, scored, sd_ready,
             out_ready, stats, stats_seen, aggr, var_ready, rstd_ready, state_ready, normed, r_ready, r_turned, rhi,
             rlo, pe_go, zs_out, w_free, whi, state_zero) = sems(
                "tab_in z_ready z_turned v_ready halves rotated qkt_ready qg_ready kg_ready scored sd_ready "
                    "out_ready stats stats_seen aggr var_ready rstd_ready state_ready normed r_ready r_turned rhi "
                    "rlo pe_go zs_out w_free whi state_zero")
            w_in_s = sems("w_in_s0 w_in_s1")

            def steps(body):
                def run(eng):
                    with eng.Fori(0, HP - 1) as p:
                        body(eng, p, False)
                    body(eng, HP - 1, True)
                return run

            with nc.Block() as block:
                @block.sync
                def _(sp):
                    sp.sem_inc(w_free, 2)
                    for dst, src in ((ROPE, c_rope_ret), (DEC, c_decay), (GQ, c_gq), (KDEC, c_kdec), (GCH, c_gchunk)):
                        sp.dma_start(dst[:], src).then_inc(tab_in, 16)

                    def body(sp, p, last):
                        for c in range(4):
                            sp.wait_ge(w_free, BASE + 4 * p + c + 1)
                            for k in range(2):
                                if last:
                                    sp.dma_start(STG[:, c % 2, k, 0:384].rearrange("p (j n) -> p j n", j=3),
                                                 w_in_v[:, 2 * c + k, 4:7, 0, :]).then_inc(w_in_s[c % 2], 16)
                                else:
                                    sp.dma_start(STG[:, c % 2, k].rearrange("p (j n) -> p j n", j=4),
                                                 w_in_v[:, 2 * c + k, 0:4, p + 1, :]).then_inc(w_in_s[c % 2], 16)
                        sp.wait_ge(rotated, BASE + 18 * p + 18)
                        sp.wait_ge(v_ready, BASE + 9 * p + 9)
                        sp.dma_start(scratch[0:4, :, ds(p * P, P)].rearrange("j b n -> b j n"),
                                     ZS[:NB].rearrange("b (j n) -> b j n", j=4)).then_inc(zs_out, 16)
                    steps(body)(sp)
                    sp.wait_ge(state_ready, BASE + HP * NT)
                    for hh in range(2):
                        sp.dma_start(ret_p.rearrange("a b (p t) d e -> (a b t) d p e", t=2)[hh],
                                     STATE[hh * E:(hh + 1) * E, :, hh * E:(hh + 1) * E]).then_inc(zs_out, 16)
                    sp.wait_ge(zs_out, BASE + 16 * HP + 32)
                    clear_before(sp)

                @block.tensor
                def _(pe):
                    pe.wait_ge(tab_in, BASE + 80)

                    def body(pe, p, last):
                        slot = p % 2
                        for s in range(NT + 5):
                            if s <= NT:
                                n = P if s < NT else NB
                                if s == 0:
                                    pe.wait_ge(rlo, BASE + 8 * p)
                                    pe.wait_ge(w_free, BASE + 4 * p + 2)
                                if s >= 2:
                                    pe.wait_ge(halves, BASE + 18 * p + 2 * s - 2)
                                    pe.wait_ge(v_ready, BASE + 9 * p + s - 1)
                                    if s == NT:
                                        pe.sem_inc(pe_go, 1)
                                elif last is not None:
                                    pe.wait_ge(halves, BASE + 18 * p)
                                    pe.wait_ge(v_ready, BASE + 9 * p)
                                for k in range(KD):
                                    for a, b in PASSES:
                                        mm = nc.tensor.matmul(Z[:n, s % 2], HT[:, a, k, s * P:s * P + n],
                                                              WS[:, slot, b, k, :], start=(k == 0 and (a, b) == (0, 0)),
                                                              stop=(k == KD - 1 and (a, b) == (1, 0)))
                                mm.then_inc(z_ready, 1)
                            t = s - 1
                            if 0 <= t < NT:
                                pe.wait_ge(rotated, BASE + 18 * p + 2 * t + 2)
                                pe.wait_ge(qkt_ready, BASE + 8 * p + t)
                                for j in range(2):
                                    mm = nc.tensor.transpose(TB[:, j * P:(j + 1) * P], QK[:, t % 2, j * P:(j + 1) * P], IDENT[:])
                                mm.then_inc(z_turned, 1)
                            t = s - 2
                            if 0 <= t < NT:
                                pe.wait_ge(qkt_ready, BASE + 8 * p + t + 1)
                                pe.wait_ge(sd_ready, BASE + 8 * p + t)
                                for h in range(2):
                                    r = slice(h * E, (h + 1) * E)
                                    mm = nc.tensor.matmul(SB[:, h], QKT[r, t % 2, P:2 * P],
                                                          QKT[r, t % 2, 0:P], start=True, stop=True)
                                mm.then_inc(scored, 1)
                            t = s - 3
                            if 0 <= t < NT:
                                pe.wait_ge(sd_ready, BASE + 8 * p + t + 1)
                                pe.wait_ge(qg_ready, BASE + 8 * p + t + 1)
                                pe.wait_ge(kg_ready, BASE + 8 * p + t + 1)
                                pe.wait_ge(state_ready, BASE + 8 * p + t)
                                pe.wait_ge(normed, BASE + 16 * p + 2 * t)
                                if t == 0:
                                    pe.wait_ge(state_zero, BASE + 1)
                                nc.tensor.matmul(OB, QG[:, t % 4], STATE[:, p, :], start=True, stop=False)
                                for h in range(2):
                                    nc.tensor.matmul(OB[:, h * E:(h + 1) * E], SD[:, t % 2, h], V[:, t, h * E:(h + 1) * E],
                                                     start=False, stop=(h == 1))
                                nc.tensor.matmul(UB, KG[:, t % 4], V[:, t], start=True, stop=True).then_inc(out_ready, 1)
                            t = s - 4
                            if 0 <= t < NT:
                                pe.wait_ge(r_ready, BASE + 8 * p + t + 1)
                                pe.wait_ge(rlo, BASE + 8 * p + t)
                                nc.tensor.transpose(RB, R[:, t % 2], IDENT[:]).then_inc(r_turned, 1)
                    steps(body)(pe)

                @block.scalar
                def _(act):
                    def body(act, p, last):
                        cols = 384 if last else 512
                        for s in range(NT + 5):
                            if s <= NT:
                                act.wait_ge(halves, BASE + 18 * p + 2 * s + 2)
                                if s < NT:
                                    act.wait_ge(out_ready, BASE + 8 * p)
                                    act.wait_ge(r_ready, BASE + 8 * p)
                                    nc.scalar.activation(V[:, s], Z[:, s % 2, 256:384], ACT.Copy, scale=UNSCALE)
                                    nc.scalar.activation(G[:, s], Z[:, s % 2, 384:512], ACT.Silu, scale=UNSCALE).then_inc(v_ready, 1)
                                else:
                                    act.wait_ge(zs_out, BASE + 16 * p)
                                    nc.scalar.activation(ZS[:NB, 256:384], Z[:NB, s % 2, 256:384], ACT.Copy, scale=UNSCALE)
                                    nc.scalar.activation(ZS[:NB, 384:512], Z[:NB, s % 2, 384:512], ACT.Silu,
                                                         scale=UNSCALE).then_inc(v_ready, 1)
                            t = s - 1
                            if 0 <= t < NT:
                                act.wait_ge(z_turned, BASE + 8 * p + t + 1)
                                if t >= 2:
                                    act.wait_ge(scored, BASE + 8 * p + t - 1)
                                    act.wait_ge(qg_ready, BASE + 8 * p + t - 1)
                                else:
                                    act.wait_ge(scored, BASE + 8 * p)
                                    act.wait_ge(qg_ready, BASE + 8 * p)
                                nc.scalar.activation(QKT[:, t % 2], TB, ACT.Copy).then_inc(qkt_ready, 1)
                            t = s - 4
                            if 0 <= t < NT:
                                act.wait_ge(r_turned, BASE + 8 * p + t + 1)
                                nc.scalar.activation(MT[:, 0, p, t * P:(t + 1) * P], RB, ACT.Copy, scale=S_ACT).then_inc(rhi, 1)
                            if s in (1, 3, 5, 7):
                                c = s // 2
                                act.wait_ge(w_in_s[c % 2], BASE + 64 * p + 32 * (c // 2) + 32)
                                if c == 0:
                                    act.wait_ge(z_ready, BASE + 9 * p)
                                nc.scalar.activation(WS[:, (p + 1) % 2, 0, 2 * c:2 * c + 2, 0:cols], STG[:, c % 2, :, 0:cols],
                                                     ACT.Copy, scale=S_W).then_inc(whi, 1)
                    steps(body)(act)

                @block.vector
                def _(dve):
                    nc.vector.memset(STATE[:], 0.0).then_inc(state_zero, 1)
                    dve.wait_ge(tab_in, BASE + 80)
                    dve.wait_ge(state_zero, BASE + 1)

                    def turn_pairs(p, s, n, out):
                        dve.wait_ge(z_ready, BASE + 9 * p + s + 1)
                        dve.wait_ge(rotated, BASE + 18 * p + 2 * s)
                        z = Z[:n, s % 2, 0:256].rearrange("p (g e) -> p g e", e=E // 2)
                        for j, dst in ((0, T1), (1, T2)):
                            nc.vector.tensor_tensor(dst[:n].rearrange("p (g e) -> p g e", e=E // 2), z,
                                                    ROPE[:n, s, j].unsqueeze(1).broadcast_to([n, 8, E // 2]),
                                                    ALU.mult).then_inc(halves, 1)
                        dve.wait_ge(halves, BASE + 18 * p + 2 * s + 2)
                        c, d, o = (x[:n].rearrange("p (g a e) -> p g a e", a=2, e=E // 2) for x in (T1, T2, out))
                        nc.vector.tensor_tensor(o[:, :, 0], c[:, :, 0], d[:, :, 1], ALU.subtract).then_inc(rotated, 1)
                        nc.vector.tensor_tensor(o[:, :, 1], c[:, :, 1], d[:, :, 0], ALU.add).then_inc(rotated, 1)

                    def body(dve, p, last):
                        cols = 384 if last else 512
                        for s in range(NT + 5):
                            if s < NT:
                                if s >= 2:
                                    dve.wait_ge(z_turned, BASE + 8 * p + s - 1)
                                turn_pairs(p, s, P, QK[:, s % 2])
                            elif s == NT:
                                dve.wait_ge(zs_out, BASE + 16 * p)
                                turn_pairs(p, s, NB, ZS[:, 0:256])
                            t = s - 1
                            if 0 <= t < NT:
                                if t >= 4:
                                    dve.wait_ge(out_ready, BASE + 8 * p + t - 3)
                                dve.wait_ge(qkt_ready, BASE + 8 * p + t + 1)
                                dve.wait_ge(rotated, BASE + 18 * p + 2 * t + 2)
                                nc.vector.tensor_tensor(QG[:, t % 4], QKT[:, t % 2, 0:P], GQ[:, p, :], ALU.mult).then_inc(qg_ready, 1)
                                nc.vector.tensor_tensor(KG[:, t % 4], QK[:, t % 2, P:2 * P], KDEC[:, ds(p * P, P)],
                                                        ALU.mult).then_inc(kg_ready, 1)
                            t = s - 2
                            if 0 <= t < NT:
                                dve.wait_ge(scored, BASE + 8 * p + t + 1)
                                if t >= 2:
                                    dve.wait_ge(out_ready, BASE + 8 * p + t - 1)
                                nc.vector.tensor_tensor(SD[:, t % 2], SB,
                                                        DEC[:, ds(2 * p, 2), :], ALU.mult).then_inc(sd_ready, 1)
                            t = s - 3
                            if 0 <= t < NT:
                                dve.wait_ge(out_ready, BASE + 8 * p + t + 1)
                                for h in range(2):
                                    r = slice(h * E, (h + 1) * E)
                                    mm = nc.vector.scalar_tensor_tensor(STATE[r, p, h * E:(h + 1) * E], STATE[r, p, h * E:(h + 1) * E],
                                                                        GCH[r, p:p + 1] if isinstance(p, int) else GCH[r, ds(p, 1)],
                                                                        UB[r, h * E:(h + 1) * E], ALU.mult, ALU.add)
                                mm.then_inc(state_ready, 1)
                                for h in range(2):
                                    nc.vector.bn_stats(BST[:, h], OB[:, h * E:(h + 1) * E]).then_inc(stats, 1)
                                dve.wait_ge(stats, BASE + 16 * p + 2 * t + 2)
                                dve.sem_inc(stats_seen, 1)
                                for h in range(2):
                                    nc.vector.bn_aggr(MV[:, h], BST[:, h]).then_inc(aggr, 1)
                                dve.wait_ge(aggr, BASE + 16 * p + 2 * t + 2)
                                nc.vector.tensor_scalar(VE[:], MV[:, :, 1], EPS, None, ALU.add).then_inc(var_ready, 1)
                            u = s - 4
                            if 0 <= u < NT:
                                dve.wait_ge(rhi, BASE + 8 * p + u + 1)
                                nc.vector.scalar_tensor_tensor(MT[:, 1, p, u * P:(u + 1) * P], RB, S_ACT,
                                                               MT[:, 0, p, u * P:(u + 1) * P], ALU.mult, ALU.subtract).then_inc(rlo, 1)
                            if s in (1, 3, 5, 7):
                                c = s // 2
                                dve.wait_ge(whi, BASE + 4 * p + c + 1)
                                nc.vector.scalar_tensor_tensor(WS[:, (p + 1) % 2, 1, 2 * c:2 * c + 2, 0:cols], STG[:, c % 2, :, 0:cols],
                                                               S_W, WS[:, (p + 1) % 2, 0, 2 * c:2 * c + 2, 0:cols],
                                                               ALU.mult, ALU.subtract).then_inc(w_free, 1)
                            if 0 <= t < NT:
                                dve.wait_ge(rstd_ready, BASE + 8 * p + t + 1)
                                for h in range(2):
                                    nc.vector.tensor_scalar(RN[:, h * E:(h + 1) * E], OB[:, h * E:(h + 1) * E], MV[:, h, 0:1],
                                                            RSTD[:, h:h + 1], ALU.subtract, ALU.mult).then_inc(normed, 1)
                                dve.wait_ge(normed, BASE + 16 * p + 2 * t + 2)
                                if t >= 2:
                                    dve.wait_ge(r_turned, BASE + 8 * p + t - 1)
                                nc.vector.tensor_tensor(R[:, t % 2], RN[:], G[:, t], ALU.mult).then_inc(r_ready, 1)
                    steps(body)(dve)

                @block.gpsimd
                def _(pool):
                    count_from_base(pool)
                    def body(pool, p, last):
                        for t in range(NT):
                            pool.wait_ge(var_ready, BASE + 8 * p + t + 1)
                            nc.gpsimd.tensor_tensor(RSTD[:], VE[:], EPSC[:], ALU.pow).then_inc(rstd_ready, 1)
                    steps(body)(pool)
        end_stage()
        stage[0] = "attention"
        with ExitStack() as st:
            ROPE = sb(st, "ROPE", [P, NT + 1, 2, E // 8])
            MASK = sb(st, "MASK", [P, SEQ])
            T1 = sb(st, "T1", [P, 64])
            T2 = sb(st, "T2", [P, 64])
            QKV = sb(st, "QKV", [P, NT + 1, 384])
            QKT = sb(st, "QKT", [P, 2, SEQ])
            PR = sb(st, "PR", [P, 3, SEQ])
            PRT = sb(st, "PRT", [P, 2, NT, P])
            MX = sb(st, "MX", [P, 2])
            NMX = sb(st, "NMX", [P, 3])
            SUM = sb(st, "SUM", [P, 4])
            RCP = sb(st, "RCP", [P, 2])
            ATT = sb(st, "ATT", [P, NT, P])
            Z, TB, PT, OB = PS[:, 0:2], PS[:, 4, 0:256], PS[:, 4:6], PS[:, 6:8, 0:E]
            NQ = len(Q_ORDER)
            (tab_in, z_ready, z_turned, copied, halves, rotated, qkt_ready, scored, masked, neg_ready, exp_ready,
             p_turned, prt_ready, o_ready, rcp_ready, att_ready, att_turned, mhi, mlo, out_st, w_free, whi,
             pe_go, dve_go) = sems(
                "tab_in z_ready z_turned copied halves rotated qkt_ready scored masked neg_ready exp_ready "
                    "p_turned prt_ready o_ready rcp_ready att_ready att_turned mhi mlo out_st w_free whi pe_go dve_go")
            w_in_s = sems("w_in_s0 w_in_s1")

            with nc.Block() as block:
                @block.sync
                def _(sp):
                    sp.sem_inc(w_free, 2)
                    for dst, src in ((ROPE, c_rope_att), (MASK, c_mask)):
                        sp.dma_start(dst[:], src).then_inc(tab_in, 16)

                    def body(sp, p, last):
                        for c in range(0 if last else 4):
                            sp.wait_ge(w_free, BASE + 4 * p + c + 1)
                            for k in range(2):
                                sp.dma_start(STG[:, c % 2, k, 0:384].rearrange("p (j n) -> p j n", j=3),
                                             w_in_v[:, 2 * c + k, 4:7, p + 1, :]).then_inc(w_in_s[c % 2], 16)
                        for k in range(KD if last else 0):
                            sp.wait_ge(w_free, BASE + 4 * p + k + 1)
                            sp.dma_start(STG[:, k % 2], w_out[0, k * P:(k + 1) * P].rearrange("p (c n) -> p c n", c=2)).then_inc(w_in_s[k % 2], 16)
                        sp.wait_ge(rotated, BASE + 18 * p + 18)
                        for j, pr, sm in ((1, kwin_p, kwin_s), (2, vwin_p, vwin_s)):
                            cols = slice(j * P, (j + 1) * P)
                            sp.dma_start(pr.rearrange("a b (t p) h e -> p (a b t) (h e)", p=P)[:, :, ds(p * P, P)],
                                         QKV[:, 0:NT, cols]).then_inc(out_st, 16)
                            sp.dma_start(sm.rearrange("a b t h e -> (a b t) (h e)")[:, ds(p * P, P)],
                                         QKV[:NB, NT, cols]).then_inc(out_st, 16)
                        sp.dma_start(scratch[4:7, :, ds(p * P, P)].rearrange("j b n -> b j n"),
                                     QKV[:NB, NT].rearrange("b (j n) -> b j n", j=3)).then_inc(out_st, 16)
                    steps(body)(sp)
                    sp.wait_ge(out_st, BASE + 80 * HP)
                    clear_before(sp)

                @block.gpsimd
                def _(pool):
                    count_from_base(pool)

                @block.tensor
                def _(pe):
                    def body(pe, p, last):
                        slot = p % 2
                        pe.wait_ge(masked, BASE + NQ * p)
                        pe.wait_ge(w_free, BASE + 4 * p + 2)
                        for s in range(NT + 2):
                            if s <= NT:
                                n = P if s < NT else NB
                                if s >= 2:
                                    pe.wait_ge(rotated, BASE + 18 * p + 2 * s - 2)
                                if s == NT:
                                    pe.sem_inc(pe_go, 1)
                                for k in range(KD):
                                    for a, b in PASSES:
                                        mm = nc.tensor.matmul(Z[:n, s % 2, 0:384], HT[:, a, k, s * P:s * P + n],
                                                              WS[:, slot, b, k, 0:384], start=(k == 0 and (a, b) == (0, 0)),
                                                              stop=(k == KD - 1 and (a, b) == (1, 0)))
                                mm.then_inc(z_ready, 1)
                            t = s - 1
                            if 0 <= t < NT:
                                pe.wait_ge(rotated, BASE + 18 * p + 2 * t + 2)
                                if t == 0:
                                    pe.wait_ge(mlo, BASE + p)
                                pe.wait_ge(qkt_ready, BASE + 8 * p + t)
                                for j in range(2):
                                    mm = nc.tensor.transpose(TB[:, j * P:(j + 1) * P], QKV[:, t, j * P:(j + 1) * P], IDENT[:])
                                mm.then_inc(z_turned, 1)
                        for n in range(NQ + 3):
                            if n < NQ:
                                h, q = Q_ORDER[n]
                                r = slice(h * E, (h + 1) * E)
                                if n == 0:
                                    pe.wait_ge(qkt_ready, BASE + 8 * p + 8)
                                    pe.wait_ge(rotated, BASE + 18 * p + 18)
                                if n >= 2:
                                    pe.wait_ge(masked, BASE + NQ * p + n - 1)
                                for c in range(q // 4 + 1):
                                    w = min(512, (q + 1) * P - c * 512)
                                    mm = nc.tensor.matmul(PS[:, 2 * (n % 2) + c, 0:w], QKT[r, 0, q * P:(q + 1) * P],
                                                          QKT[r, 1, c * 512:c * 512 + w], start=True, stop=True)
                                mm.then_inc(scored, 1)
                            m = n - 2
                            if 0 <= m < NQ:
                                pe.wait_ge(exp_ready, BASE + NQ * p + m + 1)
                                pe.wait_ge(prt_ready, BASE + NQ * p + m)
                                q = Q_ORDER[m][1]
                                for kb in range(q + 1):
                                    mm = nc.tensor.transpose(PT[:, kb // 4, (kb % 4) * P:(kb % 4 + 1) * P],
                                                             PR[:, m % 3, kb * P:(kb + 1) * P], IDENT[:])
                                mm.then_inc(p_turned, 1)
                            m = n - 3
                            if 0 <= m < NQ:
                                h, q = Q_ORDER[m]
                                pe.wait_ge(prt_ready, BASE + NQ * p + m + 1)
                                if m >= 2:
                                    pe.wait_ge(att_ready, BASE + NQ * p + m - 1)
                                for kb in range(q + 1):
                                    mm = nc.tensor.matmul(OB[:, m % 2], PRT[:, m % 2, kb], QKV[:, kb, 256 + h * E:256 + (h + 1) * E],
                                                          start=(kb == 0), stop=(kb == q))
                                mm.then_inc(o_ready, 1)
                        pe.wait_ge(att_ready, BASE + NQ * p + NQ)
                        for t in range(NT):
                            mm = nc.tensor.transpose(PT[:, t // 4, (t % 4) * P:(t % 4 + 1) * P], ATT[:, t], IDENT[:])
                        mm.then_inc(att_turned, 1)
                    steps(body)(pe)

                @block.scalar
                def _(act):
                    def split_out(k):
                        act.wait_ge(w_in_s[k % 2], BASE + 64 * (HP - 1) + 16 * (k // 2) + 16)
                        if k == 4:
                            act.wait_ge(z_ready, BASE + 9 * HP)
                        nc.scalar.activation(WS[:, k // 4, 0, 2 * (k % 4):2 * (k % 4) + 2], STG[:, k % 2], ACT.Copy,
                                             scale=S_W).then_inc(whi, 1)

                    def body(act, p, last):
                        act.wait_ge(out_st, BASE + 80 * p)
                        act.wait_ge(o_ready, BASE + NQ * p)
                        for s in range(NT + 2):
                            if s <= NT:
                                n = P if s < NT else NB
                                act.wait_ge(halves, BASE + 18 * p + 2 * s + 2)
                                nc.scalar.activation(QKV[:n, s], Z[:n, s % 2, 0:384], ACT.Copy, scale=UNSCALE).then_inc(copied, 1)
                            t = s - 1
                            if 0 <= t < NT:
                                act.wait_ge(z_turned, BASE + 8 * p + t + 1)
                                nc.scalar.activation(QKT[:, :, t * P:(t + 1) * P], TB.rearrange("p (j n) -> p j n", j=2),
                                                     ACT.Copy).then_inc(qkt_ready, 1)
                            if not last and s in (1, 3, 5, 7):
                                c = s // 2
                                act.wait_ge(w_in_s[c % 2], BASE + 64 * p + 32 * (c // 2) + 32)
                                nc.scalar.activation(WS[:, (p + 1) % 2, 0, 2 * c:2 * c + 2, 0:384], STG[:, c % 2, :, 0:384],
                                                     ACT.Copy, scale=S_W).then_inc(whi, 1)
                            if last and s in (1, 3, 5, 7):
                                split_out(s // 2)
                        for n in range(NQ + 2):
                            if last and n % 4 == 2 and n < NQ:
                                split_out(4 + n // 4)
                            if n < NQ:
                                w = (Q_ORDER[n][1] + 1) * P
                                act.wait_ge(neg_ready, BASE + NQ * p + n + 1)
                                if n >= 4:
                                    act.wait_ge(rcp_ready, BASE + NQ * p + n - 3)
                                else:
                                    act.wait_ge(rcp_ready, BASE + NQ * p)
                                nc.scalar.activation(PR[:, n % 3, 0:w], PR[:, n % 3, 0:w], ACT.Exp, scale=ATT_SCALE,
                                                     bias=NMX[:, n % 3:n % 3 + 1], accum_out=SUM[:, n % 4:n % 4 + 1]).then_inc(exp_ready, 1)
                            m = n - 2
                            if 0 <= m < NQ:
                                q = Q_ORDER[m][1]
                                act.wait_ge(p_turned, BASE + NQ * p + m + 1)
                                if m >= 2:
                                    act.wait_ge(o_ready, BASE + NQ * p + m - 1)
                                nc.scalar.activation(PRT[:, m % 2, 0:q + 1], PT.rearrange("p b (k n) -> p (b k) n", k=4)[:, 0:q + 1],
                                                     ACT.Copy).then_inc(prt_ready, 1)
                        act.wait_ge(att_turned, BASE + p + 1)
                        nc.scalar.activation(MT[:, 0, HP + p, :], PT.rearrange("p b n -> p (b n)"), ACT.Copy,
                                             scale=S_ACT).then_inc(mhi, 1)
                    steps(body)(act)

                @block.vector
                def _(dve):
                    dve.wait_ge(tab_in, BASE + 32)

                    def split_out(k):
                        dve.wait_ge(whi, BASE + 4 * (HP - 1) + k + 1)
                        w = WS[:, k // 4, :, 2 * (k % 4):2 * (k % 4) + 2]
                        nc.vector.scalar_tensor_tensor(w[:, 1], STG[:, k % 2], S_W, w[:, 0], ALU.mult,
                                                       ALU.subtract).then_inc(w_free, 1)

                    def body(dve, p, last):
                        for s in range(NT + 1):
                            n = P if s < NT else NB
                            dve.wait_ge(z_ready, BASE + 9 * p + s + 1)
                            dve.wait_ge(rotated, BASE + 18 * p + 2 * s)
                            z = Z[:n, s % 2, 0:256].rearrange("p (g e) -> p g e", g=4)[:, :, 0:16].rearrange("p g (a e) -> p g a e", a=2)
                            c, d = (x[:n].rearrange("p (g a e) -> p g a e", a=2, e=8) for x in (T1, T2))
                            for j, dst in ((0, c), (1, d)):
                                nc.vector.tensor_tensor(dst, z, ROPE[:n, s, j].unsqueeze(1).unsqueeze(1).broadcast_to([n, 4, 2, 8]),
                                                        ALU.mult).then_inc(halves, 1)
                            dve.wait_ge(halves, BASE + 18 * p + 2 * s + 2)
                            dve.wait_ge(copied, BASE + 9 * p + s + 1)
                            o = QKV[:n, s, 0:256].rearrange("p (g e) -> p g e", g=4)
                            nc.vector.tensor_tensor(o[:, :, 0:8], c[:, :, 0], d[:, :, 1], ALU.subtract).then_inc(rotated, 1)
                            nc.vector.tensor_tensor(o[:, :, 8:16], c[:, :, 1], d[:, :, 0], ALU.add).then_inc(rotated, 1)
                            if not last and s in (1, 3, 5, 7):
                                k = s // 2
                                dve.wait_ge(whi, BASE + 4 * p + k + 1)
                                w = WS[:, (p + 1) % 2, :, 2 * k:2 * k + 2, 0:384]
                                nc.vector.scalar_tensor_tensor(w[:, 1], STG[:, k % 2, :, 0:384], S_W, w[:, 0],
                                                               ALU.mult, ALU.subtract).then_inc(w_free, 1)
                            if last and s in (1, 3, 5, 7):
                                split_out(s // 2)
                        for n in range(NQ + 3):
                            if n < NQ:
                                q = Q_ORDER[n][1]
                                w = (q + 1) * P
                                dve.wait_ge(scored, BASE + NQ * p + n + 1)
                                if n >= 3:
                                    dve.wait_ge(p_turned, BASE + NQ * p + n - 2)
                                if n >= 2:
                                    dve.wait_ge(neg_ready, BASE + NQ * p + n - 1)
                                dve.sem_inc(dve_go, 1)
                                b = 2 * (n % 2)
                                nc.vector.tensor_tensor_reduce(
                                    out=PR[:, n % 3, 0:w], in0=PS[:, b:b + 2].rearrange("p b n -> p (b n)")[:, 0:w],
                                    in1=MASK[:, SEQ - w:SEQ], scale=1.0, scalar=3 * NEG, op0=ALU.add, op1=ALU.max,
                                    accum_out=MX[:, n % 2:n % 2 + 1]).then_inc(masked, 1)
                                dve.wait_ge(masked, BASE + NQ * p + n + 1)
                                nc.vector.tensor_scalar(NMX[:, n % 3:n % 3 + 1], MX[:, n % 2:n % 2 + 1], -ATT_SCALE, None,
                                                        ALU.mult).then_inc(neg_ready, 1)
                            m = n - 3
                            if 0 <= m < NQ:
                                h, q = Q_ORDER[m]
                                nc.vector.reciprocal(RCP[:, m % 2:m % 2 + 1], SUM[:, m % 4:m % 4 + 1]).then_inc(rcp_ready, 1)
                                dve.wait_ge(rcp_ready, BASE + NQ * p + m + 1)
                                dve.wait_ge(o_ready, BASE + NQ * p + m + 1)
                                nc.vector.tensor_scalar(ATT[:, q, h * E:(h + 1) * E], OB[:, m % 2], RCP[:, m % 2:m % 2 + 1], None,
                                                        ALU.mult).then_inc(att_ready, 1)
                            if last and n % 4 == 2 and n < NQ:
                                split_out(4 + n // 4)
                        dve.wait_ge(mhi, BASE + p + 1)
                        nc.vector.scalar_tensor_tensor(MT[:, 1, HP + p, :], PT.rearrange("p b n -> p (b n)"), S_ACT,
                                                       MT[:, 0, HP + p, :], ALU.mult, ALU.subtract).then_inc(mlo, 1)
                    steps(body)(dve)
        proj.close()
        end_stage()
        stage[0] = "samples"
        mix_scratch = nc.dram_tensor("mix_scratch", (2, NB * H, E), F32, kind="Internal").ap()
        R8 = NB * H
        PAT = 3
        LOG3 = float(np.log(3.0)) / ATT_SCALE
        with ExitStack() as st:
            ROW = sb(st, "ROW", [P, 7, E])
            GAM = sb(st, "GAM", [P, 1])
            OWN = sb(st, "OWN", [P, H])
            QKH = sb(st, "QKH", [P, 2, E // 2])
            SS = sb(st, "SS", [P, E // 2, E])
            OUTER = sb(st, "OUTER", [P, E // 2, E])
            RO = sb(st, "RO", [P, E])
            BST = sb(st, "BST", [P, 6])
            MV = sb(st, "MV", [P, 2])
            VE = sb(st, "VE", [P, 1])
            RSTD = sb(st, "RSTD", [P, 1])
            QB = sb(st, "QB", [P, NB, HW])
            KC = sb(st, "KC", [P, 2, PAT, HW])
            VC = sb(st, "VC", [P, 2, PAT, HW])
            PRD = sb(st, "PRD", [P, PAT, HW])
            SC = sb(st, "SC", [P, PAT, R8])
            SR = sb(st, "SR", [P, PAT * P + 1])
            QN = sb(st, "QN", [P, E])
            MX = sb(st, "MX", [P, 2])
            SUM = sb(st, "SUM", [P, 2])
            PBD = PRD[:].rearrange("p a (b r) -> p (a b r)", b=NB).rearrange("p (b a r) -> p b a r", a=PAT, r=R8)
            AO = sb(st, "AO", [P, E])
            MS = SS[:].rearrange("p d e -> p (d e)")[:, 0:D]
            OM = OUTER[:, 0:H]
            (tab_in, row_in, qb_in, ss_in, k_free, v_free, prods, s_done, s_turned, sr_ready, chain, exp_done, p_turned, pbd_ready,
             pv_done, var_ready, rstd_ready, ret_done, att_done, mix_out, ms_in, ms_turned, mhi, new_ready,
             half_sums, summed, pbd_zero, pool_c) = sems(
                "tab_in row_in qb_in ss_in k_free v_free prods s_done s_turned sr_ready chain exp_done p_turned pbd_ready "
                    "pv_done var_ready rstd_ready ret_done att_done mix_out ms_in ms_turned mhi new_ready "
                    "half_sums summed pbd_zero pool_c")
            k_in = sems("k_in0 k_in1")
            v_in = sems("v_in0 v_in1")
            RPS = PS[:R8, 4, 0:E]
            SPS, PTS, OPS, MPS = PS[:R8, 0, 0:PAT * P], PS[:, 1, 0:PAT * R8], PS[:R8, 2], PS[:, 3, 0:KD * NB]

            def cached(src, b, pat):
                step = (1, 4, 16)[pat]
                return src[0, b, WIN - P * step:WIN].rearrange("(i d) h e -> i d (h e)", d=step)[:, 0]

            with nc.Block() as block:
                @block.sync
                def _(sp):
                    sp.dma_start(OWN[:R8], c_own).then_inc(tab_in, 16)
                    sp.dma_start(QB[:], scratch[4:5].rearrange("a b n -> a b n").broadcast_to([P, NB, HW])).then_inc(qb_in, 16)
                    for half in range(2):
                        r = slice(half * R8, (half + 1) * R8)
                        d = slice(half * E // 2, (half + 1) * E // 2)
                        sp.dma_start(GAM[r], c_gsample, allow_slow_non_contiguous=True).then_inc(ss_in, 16)
                        sp.dma_start(ROW[r], scratch.rearrange("j b (h e) -> (b h) j e", e=E)).then_inc(row_in, 16)
                        sp.dma_start(QKH[r], scratch[0:2].rearrange("j b (h e) -> (b h) j e", e=E)[:, :, d]).then_inc(ss_in, 16)
                        sp.dma_start(SS[r], state_ret.rearrange("a b h d e -> (a b h) d e")[:, d]).then_inc(ss_in, 16)
                    for b in range(NB):
                        if b >= 2:
                            sp.wait_ge(k_free, BASE + b - 1)
                        for pat in range(PAT):
                            sp.dma_start(KC[:, b % 2, pat], cached(cache_k, b, pat)).then_inc(k_in[b % 2], 16)
                        if b < 2:
                            for pat in range(PAT):
                                sp.dma_start(VC[:, b % 2, pat], cached(cache_v, b, pat)).then_inc(v_in[b % 2], 16)
                    for b in range(2, NB):
                        sp.wait_ge(v_free, BASE + b - 1)
                        for pat in range(PAT):
                            sp.dma_start(VC[:, b % 2, pat], cached(cache_v, b, pat)).then_inc(v_in[b % 2], 16)
                    sp.wait_ge(new_ready, BASE + 1)
                    for half in range(2):
                        sp.dma_start(ret_s.rearrange("a b h d e -> (a b h) d e")[:, half * E // 2:(half + 1) * E // 2],
                                     SS[half * R8:(half + 1) * R8]).then_inc(mix_out, 16)
                    sp.wait_ge(ret_done, BASE + 1)
                    sp.dma_start(mix_scratch[0], RO[:R8]).then_inc(mix_out, 16)
                    sp.wait_ge(att_done, BASE + 1)
                    sp.dma_start(mix_scratch[1], AO[:R8]).then_inc(mix_out, 16)
                    sp.wait_ge(mix_out, BASE + 64)
                    sp.dma_start(MS[:NB].rearrange("b (j n) -> b j n", j=2),
                                 mix_scratch.rearrange("j (b h) e -> b j (h e)", h=H)).then_inc(ms_in, 16)
                    clear_before(sp)

                @block.gpsimd
                def _(pool):
                    count_from_base(pool)
                    done = [0]

                    def then(ins):
                        done[0] += 1
                        ins.then_inc(pool_c, 1)
                        pool.wait_ge(pool_c, BASE + done[0])

                    pool.wait_ge(row_in, BASE + 32)
                    pool.wait_ge(ss_in, BASE + 96)
                    whole = [P, E // 2, E]
                    then(nc.gpsimd.tensor_scalar(QKH[:, 1], QKH[:, 1], E ** -0.5, None, ALU.mult))
                    then(nc.gpsimd.tensor_tensor(OUTER[:], QKH[:, 1].unsqueeze(2).broadcast_to(whole),
                                                 ROW[:, 2].unsqueeze(1).broadcast_to(whole), ALU.mult))
                    then(nc.gpsimd.tensor_tensor(SS[:], SS[:], GAM[:].unsqueeze(2).broadcast_to(whole), ALU.mult))
                    nc.gpsimd.tensor_tensor(SS[:], SS[:], OUTER[:], ALU.add).then_inc(new_ready, 1)
                    pool.wait_ge(new_ready, BASE + 1)
                    then(nc.gpsimd.tensor_tensor(OUTER[:], SS[:], QKH[:, 0].unsqueeze(2).broadcast_to(whole), ALU.mult))
                    w = E // 4
                    while w > 1:
                        then(nc.gpsimd.tensor_tensor(OUTER[:, 0:w], OUTER[:, 0:w], OUTER[:, w:2 * w], ALU.add))
                        w //= 2
                    nc.gpsimd.tensor_tensor(OUTER[:, 0], OUTER[:, 0], OUTER[:, 1], ALU.add).then_inc(half_sums, 1)
                    pool.wait_ge(s_done, BASE + NB)
                    nc.gpsimd.memset(PBD, 0.0).then_inc(pbd_zero, 1)
                    pool.wait_ge(var_ready, BASE + 1)
                    nc.gpsimd.tensor_tensor(RSTD[:R8], VE[:R8], EPSC[:R8, 0:1], ALU.pow).then_inc(rstd_ready, 1)

                @block.vector
                def _(dve):
                    done = [0]

                    def then(ins):
                        done[0] += 1
                        ins.then_inc(chain, 1)
                        dve.wait_ge(chain, BASE + done[0])

                    dve.wait_ge(qb_in, BASE + 16)
                    for b in range(NB):
                        dve.wait_ge(k_in[b % 2], BASE + 48 * (b // 2 + 1))
                        dve.wait_ge(s_done, BASE + b)
                        nc.vector.tensor_tensor(PRD[:], KC[:, b % 2], QB[:, b].unsqueeze(1).broadcast_to([P, PAT, HW]),
                                                ALU.mult).then_inc(k_free, 1)
                        dve.wait_ge(k_free, BASE + b + 1)
                        nc.vector.reduce_sum(SC[:, :, b * H:(b + 1) * H], PRD[:].rearrange("p a (h e) -> p a h e", e=E),
                                             AX_X).then_inc(s_done, 1)
                    dve.wait_ge(row_in, BASE + 32)
                    then(nc.vector.tensor_tensor(QN[:R8], ROW[:R8, 4], ROW[:R8, 5], ALU.mult))
                    then(nc.vector.reduce_sum(MX[:R8, 1:2], QN[:R8], AX_X))
                    then(nc.vector.tensor_scalar(SR[:R8, PAT * P:], MX[:R8, 1:2], LOG3, None, ALU.add))
                    dve.wait_ge(s_turned, BASE + 1)
                    then(nc.vector.tensor_copy(SR[:R8, 0:PAT * P], SPS))
                    then(nc.vector.reduce_max(MX[:R8, 0:1], SR[:R8], AX_X))
                    nc.vector.tensor_scalar(SUM[:R8, 1:2], MX[:R8, 0:1], -ATT_SCALE, None, ALU.mult).then_inc(sr_ready, 1)
                    dve.wait_ge(exp_done, BASE + 1)
                    then(nc.vector.reciprocal(MX[:R8, 0:1], SUM[:R8, 0:1]))
                    nc.vector.tensor_scalar(SR[:R8], SR[:R8], MX[:R8, 0:1], None, ALU.mult).then_inc(sr_ready, 1)
                    dve.wait_ge(p_turned, BASE + 1)
                    dve.wait_ge(pbd_zero, BASE + 1)
                    for b in range(NB):
                        nc.vector.tensor_copy(PBD[:, b, :, b * H:(b + 1) * H],
                                              PTS.rearrange("p (a r) -> p a r", a=PAT)[:, :, b * H:(b + 1) * H]).then_inc(pbd_ready, 1)
                    dve.wait_ge(summed, BASE + 1)
                    then(nc.vector.bn_stats(BST[:R8], RPS))
                    then(nc.vector.bn_aggr(MV[:R8], BST[:R8]))
                    nc.vector.tensor_scalar(VE[:R8], MV[:R8, 1:2], EPS, None, ALU.add).then_inc(var_ready, 1)
                    dve.wait_ge(rstd_ready, BASE + 1)
                    then(nc.vector.tensor_scalar(RO[:R8], RPS, MV[:R8, 0:1], RSTD[:R8], ALU.subtract, ALU.mult))
                    nc.vector.tensor_tensor(RO[:R8], RO[:R8], ROW[:R8, 3], ALU.mult).then_inc(ret_done, 1)
                    dve.wait_ge(pv_done, BASE + 1)
                    dve.wait_ge(tab_in, BASE + 16)
                    then(nc.vector.tensor_tensor(OM[:R8], OPS.rearrange("p (h e) -> p h e", h=H),
                                                 OWN[:R8].unsqueeze(2).broadcast_to([R8, H, E]), ALU.mult))
                    then(nc.vector.reduce_sum(AO[:R8], OM[:R8].rearrange("p h e -> p e h"), AX_X))
                    nc.vector.scalar_tensor_tensor(AO[:R8], ROW[:R8, 6], SR[:R8, PAT * P:], AO[:R8], ALU.mult,
                                                   ALU.add).then_inc(att_done, 1)
                    dve.wait_ge(mhi, BASE + 1)
                    nc.vector.scalar_tensor_tensor(MTS[:, 1], MPS.rearrange("p (k b) -> p k b", b=NB), S_ACT, MTS[:, 0],
                                                   ALU.mult, ALU.subtract)

                @block.scalar
                def _(act):
                    act.wait_ge(sr_ready, BASE + 1)
                    nc.scalar.activation(SR[:R8], SR[:R8], ACT.Exp, scale=ATT_SCALE, bias=SUM[:R8, 1:2],
                                         accum_out=SUM[:R8, 0:1]).then_inc(exp_done, 1)
                    act.wait_ge(ms_turned, BASE + 1)
                    nc.scalar.activation(MTS[:, 0], MPS.rearrange("p (k b) -> p k b", b=NB), ACT.Copy, scale=S_ACT).then_inc(mhi, 1)

                @block.tensor
                def _(pe):
                    pe.wait_ge(half_sums, BASE + 1)
                    for half in range(2):
                        mm = nc.tensor.matmul(RPS, IDENT[:, half * R8:(half + 1) * R8], OUTER[:, 0], start=(half == 0), stop=(half == 1))
                    mm.then_inc(summed, 1)
                    pe.wait_ge(s_done, BASE + NB)
                    for a in range(PAT):
                        mm = nc.tensor.transpose(SPS[:, a * P:(a + 1) * P], SC[:, a], IDENT[:])
                    mm.then_inc(s_turned, 1)
                    pe.wait_ge(sr_ready, BASE + 2)
                    for a in range(PAT):
                        mm = nc.tensor.transpose(PTS[:, a * R8:(a + 1) * R8], SR[:R8, a * P:(a + 1) * P], IDENT[:R8, :R8])
                    mm.then_inc(p_turned, 1)
                    for b in range(NB):
                        pe.wait_ge(pbd_ready, BASE + b + 1)
                        pe.wait_ge(v_in[b % 2], BASE + 48 * (b // 2 + 1))
                        for a in range(PAT):
                            mm = nc.tensor.matmul(OPS, PBD[:, b, a], VC[:, b % 2, a], start=(b == 0 and a == 0),
                                                  stop=(b == NB - 1 and a == PAT - 1))
                        mm.then_inc(v_free, 1)
                    pe.wait_ge(v_free, BASE + NB)
                    pe.sem_inc(pv_done, 1)
                    pe.wait_ge(ms_in, BASE + 16)
                    for k in range(KD):
                        mm = nc.tensor.transpose(MPS[:, k * NB:(k + 1) * NB], MS[:NB, k * P:(k + 1) * P], IDENT[:NB, :NB])
                    mm.then_inc(ms_turned, 1)
        end_stage()
        stage[0] = "mixer"
        UW = WS[:, 0].rearrange("p a (c k) (d n) -> p c a (k d) n", c=2, d=2)
        w_up_v = w_up.rearrange("a (k p) (x n) -> p (a k) x n", p=P, x=2)
        with ExitStack() as st:
            WG = sb(st, "WG", [P, 2, KD + PLE // P, D], F16)
            STG = sb(st, "STG", [P, 2, D])
            LNP = sb(st, "LNP", [P, 2, D])
            R = sb(st, "R", [P, D])
            H1 = sb(st, "H1", [P, D])
            PR = sb(st, "PR", [P, 2, PLE])
            PT = sb(st, "PT", [P, 2, 2, PLE // P, P], F16)
            BST = sb(st, "BST", [P, 2, 6])
            MV = sb(st, "MV", [P, 2])
            VE = sb(st, "VE", [P, 1])
            RSTD = sb(st, "RSTD", [P, 1])
            (ln_in, w_free, whi, wlo, mixed, r_ready, stats, stats_go, aggr, var_ready, rstd_ready, xn_ready, gained,
             h1_ready, h1_kept, turned, hi_ready, lo_ready, p_turned, phi, plo, gated, embedded, sig_ready,
             e_ready, row_ready, pe_go, up_in, up_hi) = sems(
                "ln_in w_free whi wlo mixed r_ready stats stats_go aggr var_ready rstd_ready xn_ready gained "
                    "h1_ready h1_kept turned hi_ready lo_ready p_turned phi plo gated embedded sig_ready "
                    "e_ready row_ready pe_go up_in up_hi")
            w_in_s = sems("w_in_s0 w_in_s1")
            p_in = sems("p_in0 p_in1 p_in2")
            M, TB, GB, EB, PB = PS[:, 0:2], PS[:, 4:6], PS[:, 0:2], PS[:, 2:4], PS[:, 6, 0:PLE]
            chunks = [w_ple_gate[0, k * P:(k + 1) * P] for k in range(KD)] + [w_ple_proj[0, k * P:(k + 1) * P] for k in range(PLE // P)]
            NW = len(chunks)
            UP = STG[:].rearrange("p a (k n) -> p (a k) n", n=2 * P)

            with nc.Block() as block:
                @block.sync
                def _(sp):
                    for j, v in ((0, ln1_g), (1, ln1_b)):
                        sp.dma_start(LNP[:, j], v.broadcast_to([P, D])).then_inc(ln_in, 16)
                    for c, src in enumerate(chunks):
                        if c >= 2:
                            sp.wait_ge(wlo, BASE + c - 1)
                        sp.dma_start(STG[:, c % 2], src).then_inc(w_in_s[c % 2], 16)
                    for u in range(2):
                        sp.dma_start(PR[:, u], p_prompt[0, 0, u * P:(u + 1) * P]).then_inc(p_in[u], 16)
                    sp.wait_ge(wlo, BASE + NW)
                    for x in range(2):
                        sp.dma_start(UP[:, :, x * P:(x + 1) * P], w_up_v[:, :, x, 0:P]).then_inc(up_in, 16)
                    with sp.Fori(1, NT // 2) as i:
                        for u in range(2):
                            sp.wait_ge(p_turned, BASE + 2 * i + u - 1)
                            sp.dma_start(PR[:, u], p_prompt[0, 0, ds((2 * i + u) * P, P)]).then_inc(p_in[u], 16)
                    sp.wait_ge(p_turned, BASE + NT - 1)
                    sp.dma_start(PR[:NB, 0], p_sample[0, :, 0]).then_inc(p_in[2], 16)
                    clear_before(sp)

                @block.tensor
                def _(pe):
                    def product(out, n, lhs, w, c, kd):
                        for k in range(kd):
                            for a, b in PASSES:
                                mm = nc.tensor.matmul(out[:n], lhs(a, k), w(b, k, c), start=(k == 0 and (a, b) == (0, 0)),
                                                      stop=(k == kd - 1 and (a, b) == (1, 0)))
                        return mm

                    def mix(t, n):
                        pe.wait_ge(r_ready, BASE + t)
                        pe.sem_inc(pe_go, 1)
                        for c in range(2):
                            mm = product(M[:, c], n, (lambda a, k: MT[:, a, k, ds(t * P, P)]) if n == P else (lambda a, k: MTS[:, a, k]),
                                         lambda b, k, c: WS[:, k // 4, b, 2 * (k % 4) + c], c, KD)
                        mm.then_inc(mixed, 1)

                    def turn(t, n):
                        pe.wait_ge(h1_ready, BASE + t + 1)
                        pe.wait_ge(lo_ready, BASE + t)
                        for k in range(KD):
                            mm = nc.tensor.transpose(TB[:, k // 4, (k % 4) * P:(k % 4) * P + n], H1[:n, k * P:(k + 1) * P],
                                                     IDENT[:n, :n])
                        mm.then_inc(turned, 1)

                    def turn_p(t, u, n, sem, count):
                        pe.wait_ge(sem, BASE + count)
                        pe.wait_ge(plo, BASE + t)
                        for k in range(PLE // P):
                            mm = nc.tensor.transpose(PB[:, k * P:k * P + n], PR[:n, u, k * P:(k + 1) * P], IDENT[:n, :n])
                        mm.then_inc(p_turned, 1)

                    def embed(t, u, n):
                        pe.wait_ge(sig_ready, BASE + t)
                        pe.sem_inc(pe_go, 1)
                        for c in range(2):
                            mm = product(GB[:, c], n, lambda a, k: HT[:, a, k, ds(t * P, n)],
                                         lambda b, k, c: WG[:, b, k, c * 512:(c + 1) * 512], c, KD)
                        mm.then_inc(gated, 1)
                        pe.wait_ge(plo, BASE + t + 1)
                        pe.wait_ge(e_ready, BASE + t)
                        pe.sem_inc(pe_go, 1)
                        for c in range(2):
                            mm = product(EB[:, c], n, lambda a, k: PT[:, u, a, k, 0:n],
                                         lambda b, k, c: WG[:, b, KD + k, c * 512:(c + 1) * 512], c, PLE // P)
                        mm.then_inc(embedded, 1)

                    mix(0, P)
                    with pe.Fori(1, NT) as t:
                        mix(t, P)
                        turn(t - 1, P)
                    mix(NT, NB)
                    turn(NT - 1, P)
                    turn_p(0, 0, P, p_in[0], 16)
                    turn(NT, NB)
                    pe.wait_ge(lo_ready, BASE + NT + 1)
                    pe.wait_ge(r_ready, BASE + NT + 1)
                    pe.wait_ge(wlo, BASE + NW)
                    with pe.Fori(0, NT // 2 - 1) as i:
                        for u in range(2):
                            turn_p(2 * i + u + 1, 1 - u, P, p_in[1 - u], 16 * i + 16 + 16 * u)
                            embed(2 * i + u, u, P)
                    turn_p(NT - 1, 1, P, p_in[1], 16 * (NT // 2))
                    embed(NT - 2, 0, P)
                    turn_p(NT, 0, NB, p_in[2], 16)
                    embed(NT - 1, 1, P)
                    embed(NT, 0, NB)

                @block.scalar
                def _(act):
                    def split(c, u, i):
                        act.wait_ge(w_in_s[u], BASE + 16 * i + 16)
                        nc.scalar.activation(WG[:, 0, c], STG[:, u], ACT.Copy, scale=S_W).then_inc(whi, 1)

                    def high(t, n):
                        act.wait_ge(h1_ready, BASE + t + 1)
                        nc.scalar.activation(HRES[:n, t], H1[:n], ACT.Copy).then_inc(h1_kept, 1)
                        act.wait_ge(turned, BASE + t + 1)
                        nc.scalar.activation(HT[:, 0, :, ds(t * P, n)], TB.rearrange("p b (k n) -> p (b k) n", k=4)[:, :, :n],
                                             ACT.Copy, scale=S_ACT).then_inc(hi_ready, 1)

                    def high_p(t, u, n):
                        act.wait_ge(p_turned, BASE + t + 1)
                        nc.scalar.activation(PT[:, u, 0, :, 0:n], PB.rearrange("p (k n) -> p k n", k=2)[:, :, :n], ACT.Copy,
                                             scale=S_ACT).then_inc(phi, 1)

                    def gate(t, n):
                        act.wait_ge(gated, BASE + t + 1)
                        act.wait_ge(e_ready, BASE + t)
                        nc.scalar.activation(R[:n], GB[:n].rearrange("p b n -> p (b n)"), ACT.Sigmoid, scale=UNSCALE).then_inc(sig_ready, 1)

                    split(0, 0, 0)
                    split(1, 1, 0)
                    with act.Fori(0, NT // 2) as i:
                        for u in range(2):
                            high(2 * i + u, P)
                            split(2 * i + u + 2, u, i + 1)
                    high_p(0, 0, P)
                    high(NT, NB)
                    act.wait_ge(up_in, BASE + 32)
                    nc.scalar.activation(UW[:, 0, 0], UP, ACT.Copy, scale=S_W).then_inc(up_hi, 1)
                    with act.Fori(0, NT // 2 - 1) as i:
                        for u in range(2):
                            high_p(2 * i + u + 1, 1 - u, P)
                            gate(2 * i + u, P)
                    high_p(NT - 1, 1, P)
                    gate(NT - 2, P)
                    high_p(NT, 0, NB)
                    gate(NT - 1, P)
                    gate(NT, NB)

                @block.gpsimd
                def _(pool):
                    count_from_base(pool)
                    pool.wait_ge(ln_in, BASE + 32)

                    def shift(t, n):
                        pool.wait_ge(var_ready, BASE + t + 1)
                        nc.gpsimd.tensor_tensor(RSTD[:n], VE[:n], EPSC[:n, 0:1], ALU.pow).then_inc(rstd_ready, 1)
                        pool.wait_ge(gained, BASE + t + 1)
                        pool.wait_ge(turned, BASE + t)
                        pool.wait_ge(h1_kept, BASE + t)
                        nc.gpsimd.tensor_tensor(H1[:n], R[:n], LNP[:n, 1], ALU.add).then_inc(h1_ready, 1)

                    with pool.Fori(0, NT) as t:
                        shift(t, P)
                    shift(NT, NB)

                @block.vector
                def _(dve):
                    def split(c):
                        dve.wait_ge(whi, BASE + c + 1)
                        nc.vector.scalar_tensor_tensor(WG[:, 1, c], STG[:, c % 2], S_W, WG[:, 0, c], ALU.mult,
                                                       ALU.subtract).then_inc(wlo, 1)

                    def norm(t, n):
                        dve.wait_ge(mixed, BASE + t + 1)
                        dve.wait_ge(h1_ready, BASE + t)
                        nc.vector.scalar_tensor_tensor(R[:n], HRES[:n, t], ALPHA / UNSCALE, M[:n].rearrange("p b n -> p (b n)"),
                                                       ALU.mult, ALU.add).then_inc(r_ready, 1)
                        dve.wait_ge(r_ready, BASE + t + 1)
                        for c in range(2):
                            nc.vector.bn_stats(BST[:n, c], R[:n, c * 512:(c + 1) * 512]).then_inc(stats, 1)
                        dve.wait_ge(stats, BASE + 2 * t + 2)
                        dve.sem_inc(stats_go, 1)
                        nc.vector.bn_aggr(MV[:n], BST[:n].rearrange("p a b -> p (a b)")).then_inc(aggr, 1)
                        dve.wait_ge(aggr, BASE + t + 1)
                        nc.vector.tensor_scalar(VE[:n], MV[:n, 1:2], EPS / UNSCALE ** 2, None, ALU.add).then_inc(var_ready, 1)
                        dve.wait_ge(rstd_ready, BASE + t + 1)
                        nc.vector.tensor_scalar(R[:n], R[:n], MV[:n, 0:1], RSTD[:n], ALU.subtract, ALU.mult).then_inc(xn_ready, 1)
                        dve.wait_ge(xn_ready, BASE + t + 1)
                        nc.vector.tensor_tensor(R[:n], R[:n], LNP[:n, 0], ALU.mult).then_inc(gained, 1)

                    def low(t, n):
                        dve.wait_ge(hi_ready, BASE + t + 1)
                        nc.vector.scalar_tensor_tensor(HT[:, 1, :, ds(t * P, n)], TB.rearrange("p b (k n) -> p (b k) n", k=4)[:, :, :n],
                                                       S_ACT, HT[:, 0, :, ds(t * P, n)], ALU.mult, ALU.subtract).then_inc(lo_ready, 1)

                    def low_p(t, u, n):
                        dve.wait_ge(phi, BASE + t + 1)
                        nc.vector.scalar_tensor_tensor(PT[:, u, 1, :, 0:n], PB.rearrange("p (k n) -> p k n", k=2)[:, :, :n],
                                                       S_ACT, PT[:, u, 0, :, 0:n], ALU.mult, ALU.subtract).then_inc(plo, 1)

                    def add(t, n):
                        dve.wait_ge(embedded, BASE + t + 1)
                        dve.wait_ge(sig_ready, BASE + t + 1)
                        nc.vector.scalar_tensor_tensor(R[:n], EB[:n].rearrange("p b n -> p (b n)"), UNSCALE, R[:n],
                                                       ALU.mult, ALU.mult).then_inc(row_ready, 1)
                        dve.wait_ge(row_ready, BASE + t + 1)
                        nc.vector.scalar_tensor_tensor(HRES[:n, t], HRES[:n, t], ALPHA, R[:n], ALU.mult, ALU.add).then_inc(e_ready, 1)

                    dve.wait_ge(ln_in, BASE + 32)
                    norm(0, P)
                    split(0)
                    split(1)
                    with dve.Fori(1, NT) as t:
                        low(t - 1, P)
                        norm(t, P)
                        split(t + 1)
                    low(NT - 1, P)
                    split(NW - 1)
                    norm(NT, NB)
                    low_p(0, 0, P)
                    low(NT, NB)
                    dve.wait_ge(up_hi, BASE + 1)
                    nc.vector.scalar_tensor_tensor(UW[:, 0, 1], UP, S_W, UW[:, 0, 0], ALU.mult, ALU.subtract)
                    dve.wait_ge(h1_ready, BASE + NT + 1)
                    with dve.Fori(0, NT // 2 - 1) as i:
                        for u in range(2):
                            low_p(2 * i + u + 1, 1 - u, P)
                            add(2 * i + u, P)
                    low_p(NT - 1, 1, P)
                    add(NT - 2, P)
                    low_p(NT, 0, NB)
                    add(NT - 1, P)
                    add(NT, NB)
        mid.close()
        end_stage()
        stage[0] = "ffn"
        GROUP = 6
        FULL = NCH // GROUP
        S_G = 8.0
        UNDOWN = 1.0 / (S_G * S_W)
        T = SEQ + NB
        with ExitStack() as st:
            SU = sb(st, "SU", [P, 2, KD, 2 * P])
            SD = sb(st, "SD", [P, 2, D])
            WD = (WS[:, 1].rearrange("p a (k c) n -> p (a k) (c n)", c=2)[:, 0:GROUP], sb(st, "WD", [P, GROUP, D], F16))
            HG = sb(st, "HG", [P, 2, GROUP, T], F16)
            C = sb(st, "C", [P, 2, T])
            PRD = sb(st, "PRD", [P, T])
            UC = sb(st, "UC", [P, 2 + NB, 2 * NCH])
            UO = sb(st, "UO", [P, 2 + NB, P])
            LNP = sb(st, "LNP", [P, 2, D])
            R = sb(st, "R", [P, D])
            Y = sb(st, "Y", [P, D])
            BST = sb(st, "BST", [P, 2, 6])
            MV = sb(st, "MV", [P, 2])
            VE = sb(st, "VE", [P, 1])
            RSTD = sb(st, "RSTD", [P, 1])
            (ln_in, su_free, sd_free, uhi, dhi, a_ready, g_ready, first_tap, tap1, conved, kept, s_tap1, s_conved, gelu_done, prod_ready,
             hi_ready, lo_ready, downed, added, stats, stats_go, aggr, var_ready, rstd_ready, xn_ready, gained,
             y_ready, y_out, last_turned, last_read, pe_go, dve_go) = sems(
                "ln_in su_free sd_free uhi dhi a_ready g_ready first_tap tap1 conved kept s_tap1 s_conved gelu_done prod_ready "
                    "hi_ready lo_ready downed added stats stats_go aggr var_ready rstd_ready xn_ready gained "
                    "y_ready y_out last_turned last_read pe_go dve_go")
            u_in = sems("u_in0 u_in1")
            d_in = sems("d_in0 d_in1")
            DB = (PS[:, 6:8], PS[:, 4:6])

            def groups(eng, body):
                with eng.Fori(0, FULL) as g:
                    body(g, GROUP, False)
                body(FULL, NCH - GROUP * FULL, True)

            def chunk_loop(eng, g, n, last, body):
                if last:
                    for l in range(n):
                        body(GROUP * g + l, l % 2, l, l == n - 1)
                else:
                    with eng.Fori(0, n // 2) as i:
                        for u in range(2):
                            body(GROUP * g + 2 * i + u, u, 2 * i + u, False)

            def tile_loop(eng, g, body, between=None):
                base = (NT + 1) * g
                with eng.Fori(0, NT // 2) as i:
                    for u in range(2):
                        body(base + 2 * i + u, 2 * i + u, u, P)
                if between:
                    between()
                body(base + NT, NT, 0, NB)

            with nc.Block() as block:
                @block.sync
                def _(sp):
                    sp.sem_inc(su_free, 3)
                    sp.sem_inc(sd_free, 2)
                    for j, v in ((0, ln2_g), (1, ln2_b)):
                        sp.dma_start(LNP[:, j], v.broadcast_to([P, D])).then_inc(ln_in, 16)
                    sp.dma_start(conv_s[0, :, 0], state_conv[0, :, 1]).then_inc(y_out, 16)

                    def load(c, u, l, final):
                        if not final:
                            sp.wait_ge(su_free, BASE + c + 2)
                            for x in range(2):
                                sp.dma_start(SU[:, 1 - u, :, x * P:(x + 1) * P],
                                             w_up_v[:, :, x, ds((c + 1) * P, P)]).then_inc(u_in[1 - u], 16)
                        sp.wait_ge(sd_free, BASE + c + 1)
                        sp.dma_start(SD[:, u], w_down[0, ds(c * P, P)]).then_inc(d_in[u], 16)

                    groups(sp, lambda g, n, last: chunk_loop(sp, g, n, last, load))
                    with sp.Fori(0, NT) as t:
                        sp.wait_ge(y_ready, BASE + t + 1)
                        sp.dma_start(y_prompt[0, ds(t * P, P)], Y[:]).then_inc(y_out, 16)
                    sp.wait_ge(y_ready, BASE + NT + 1)
                    sp.dma_start(y_sample[:, 0], Y[:NB]).then_inc(y_out, 16)
                    sp.wait_ge(last_read, BASE + 1)
                    for r in range(2):
                        sp.dma_start(conv_p[0, 0, r].rearrange("(c f) -> c f", f=P), UO[:2 * NCH, r]).then_inc(y_out, 16)
                    for b in range(NB):
                        sp.dma_start(conv_s[0, b, 1].rearrange("(c f) -> c f", f=P), UO[:2 * NCH, 2 + b]).then_inc(y_out, 16)
                    sp.wait_ge(y_out, BASE + 16 * (1 + NT + 1 + 2 + NB))
                    clear_before(sp)

                @block.tensor
                def _(pe):
                    def up(c, u, l, final):
                        for x, ready in ((0, a_ready), (1, g_ready)):
                            if x == 0:
                                pe.wait_ge(su_free, BASE + c + 3)
                            pe.wait_ge(conved, BASE + 2 * c + x - 1)
                            pe.wait_ge(s_conved, BASE + 2 * c + x - 1)
                            pe.sem_inc(pe_go, 1)
                            for half in range(2):
                                for k in range(KD):
                                    for a, b in PASSES:
                                        nc.tensor.matmul(PS[:, 2 * x + half], UW[:, u, a, k, x * P:(x + 1) * P],
                                                         HT[:, b, k, half * 512:(half + 1) * 512],
                                                         start=(k == 0 and (a, b) == (0, 0)), stop=(k == KD - 1 and (a, b) == (1, 0)))
                            for k in range(KD):
                                for a, b in PASSES:
                                    mm = nc.tensor.matmul(PS[:, 4 + x, 0:NB], UW[:, u, a, k, x * P:(x + 1) * P], HT[:, b, k, SEQ:T],
                                                          start=(k == 0 and (a, b) == (0, 0)), stop=(k == KD - 1 and (a, b) == (1, 0)))
                            mm.then_inc(ready, 1)

                    def down(g, n, last):
                        def tile(count, t, u, rows):
                            pe.wait_ge(lo_ready, BASE + GROUP * g + n - 1)
                            pe.wait_ge(added, BASE + count - 1)
                            if u == 1:
                                pe.wait_ge(s_conved, BASE + 2 * (GROUP * g + n))
                            pe.sem_inc(pe_go, 1)
                            for l in range(n):
                                if l == n - 1:
                                    pe.wait_ge(lo_ready, BASE + GROUP * g + n)
                                    pe.wait_ge(sd_free, BASE + GROUP * g + n + 2)
                                    pe.sem_inc(pe_go, 1)
                                for half in range(2):
                                    for a, b in PASSES:
                                        mm = nc.tensor.matmul(DB[u][:rows, half], HG[:, a, l, ds(t * P, rows)],
                                                              WD[b][:, l, half * 512:(half + 1) * 512],
                                                              start=(l == 0 and (a, b) == (0, 0)), stop=(l == n - 1 and (a, b) == (1, 0)))
                            mm.then_inc(downed, 1)
                        def turn_last():
                            pe.wait_ge(kept, BASE + 4 * NCH)
                            pe.wait_ge(conved, BASE + 2 * NCH)
                            for r in range(2 + NB):
                                mm = nc.tensor.transpose(PS[:2 * NCH, r // 4, (r % 4) * P:(r % 4 + 1) * P], UC[:, r], IDENT[:])
                            mm.then_inc(last_turned, 1)

                        tile_loop(pe, g, tile, turn_last if last else None)

                    def group(g, n, last):
                        pe.wait_ge(added, BASE + (NT + 1) * g - 1)
                        pe.sem_inc(pe_go, 1)
                        chunk_loop(pe, g, n, last, up)
                        pe.wait_ge(added, BASE + (NT + 1) * g)
                        pe.sem_inc(pe_go, 1)
                        down(g, n, last)
                    groups(pe, group)

                @block.scalar
                def _(act):
                    def up_high(c, u):
                        act.wait_ge(u_in[u], BASE + 16 * (c + u))
                        act.wait_ge(g_ready, BASE + c - 1)
                        nc.scalar.activation(UW[:, u, 0], SU[:, u], ACT.Copy, scale=S_W).then_inc(uhi, 1)

                    def step(c, u, l, final, g):
                        if not final:
                            up_high(c + 1, 1 - u)
                        for x, ready in ((0, a_ready), (1, g_ready)):
                            act.wait_ge(ready, BASE + c + 1)
                            if x == 0:
                                act.wait_ge(prod_ready, BASE + c)
                            ch = ds(c + x * NCH, 1)
                            nc.scalar.activation(C[:, x, 0:SEQ], PS[:, 2 * x:2 * x + 2].rearrange("p b n -> p (b n)"), ACT.Identity,
                                                 scale=CWS[:, 2, ch], bias=CW[:, 3, ch])
                            nc.scalar.activation(C[:, x, SEQ:T], PS[:, 4 + x, 0:NB], ACT.Identity, scale=CWS[:, 2, ch],
                                                 bias=CW[:, 3, ch]).then_inc(first_tap, 1)
                            if x == 0:
                                act.wait_ge(d_in[u], BASE + 8 * (c - u) + 16)
                                act.wait_ge(downed, BASE + (NT + 1) * g)
                                nc.scalar.activation(WD[0][:, l], SD[:, u], ACT.Copy, scale=S_W).then_inc(dhi, 1)
                        act.wait_ge(conved, BASE + 2 * c + 2)
                        act.wait_ge(s_conved, BASE + 2 * c + 2)
                        nc.scalar.activation(C[:, 1], C[:, 1], ACT.Gelu_apprx_tanh).then_inc(gelu_done, 1)
                        act.wait_ge(prod_ready, BASE + c + 1)
                        nc.scalar.activation(HG[:, 0, l], PRD[:], ACT.Copy).then_inc(hi_ready, 1)

                    groups(act, lambda g, n, last: chunk_loop(act, g, n, last, lambda c, u, l, f: step(c, u, l, f, g)))
                    act.wait_ge(last_turned, BASE + 1)
                    for b, k in ((0, 4), (1, 4), (2, 2)):
                        mm = nc.scalar.activation(UO[:2 * NCH, 4 * b:4 * b + k], PS[:2 * NCH, b, 0:k * P].rearrange("p (r n) -> p r n", r=k),
                                                  ACT.Copy)
                    mm.then_inc(last_read, 1)

                @block.gpsimd
                def _(pool):
                    count_from_base(pool)
                    def low(c, u, l, final):
                        pool.wait_ge(hi_ready, BASE + c + 1)
                        nc.gpsimd.tensor_tensor(HG[:, 1, l, :], PRD[:], HG[:, 0, l, :], ALU.subtract).then_inc(lo_ready, 1)

                    groups(pool, lambda g, n, last: chunk_loop(pool, g, n, last, low))
                    pool.wait_ge(ln_in, BASE + 32)

                    def shift(t, n):
                        pool.wait_ge(var_ready, BASE + t + 1)
                        nc.gpsimd.tensor_tensor(RSTD[:n], VE[:n], EPSC[:n, 0:1], ALU.pow).then_inc(rstd_ready, 1)
                        pool.wait_ge(gained, BASE + t + 1)
                        pool.wait_ge(y_out, BASE + 16 * t + 16)
                        nc.gpsimd.tensor_tensor(Y[:n], R[:n], LNP[:n, 1], ALU.add).then_inc(y_ready, 1)

                    with pool.Fori(0, NT) as t:
                        shift(t, P)
                    shift(NT, NB)

                @block.vector
                def _(dve):
                    def up_low(c, u):
                        dve.wait_ge(uhi, BASE + c)
                        nc.vector.scalar_tensor_tensor(UW[:, u, 1].rearrange("p k n -> p (k n)"), SU[:, u].rearrange("p k n -> p (k n)"),
                                                       S_W, UW[:, u, 0].rearrange("p k n -> p (k n)"), ALU.mult,
                                                       ALU.subtract).then_inc(su_free, 1)

                    def step(c, u, l, final):
                        if not final:
                            up_low(c + 1, 1 - u)
                        for x in range(2):
                            ch = ds(c + x * NCH, 1)
                            dve.wait_ge(first_tap, BASE + 2 * c + x + 1)
                            U = PS[:, 2 * x:2 * x + 2].rearrange("p b n -> p (b n)")
                            nc.vector.tensor_scalar(UC[:, 0:2, ch], U[:, SEQ - 2:SEQ].unsqueeze(2), UNSCALE, None, ALU.mult).then_inc(kept, 1)
                            nc.vector.tensor_scalar(UC[:, 2:, ch], PS[:, 4 + x, 0:NB].unsqueeze(2), UNSCALE, None, ALU.mult).then_inc(kept, 1)
                            nc.vector.scalar_tensor_tensor(C[:, x, 1:SEQ], U[:, 0:SEQ - 1], CWS[:, 1, ch], C[:, x, 1:SEQ],
                                                           ALU.mult, ALU.add).then_inc(tap1, 1)
                            nc.vector.scalar_tensor_tensor(C[:, x, SEQ:T].unsqueeze(2), ST[:, 1::2, ch], CW[:, 1, ch], C[:, x, SEQ:T].unsqueeze(2),
                                                           ALU.mult, ALU.add).then_inc(s_tap1, 1)
                            dve.wait_ge(tap1, BASE + 2 * c + x + 1)
                            nc.vector.scalar_tensor_tensor(C[:, x, 2:SEQ], U[:, 0:SEQ - 2], CWS[:, 0, ch], C[:, x, 2:SEQ],
                                                           ALU.mult, ALU.add).then_inc(conved, 1)
                            dve.wait_ge(s_tap1, BASE + 2 * c + x + 1)
                            nc.vector.scalar_tensor_tensor(C[:, x, SEQ:T].unsqueeze(2), ST[:, 0::2, ch], CW[:, 0, ch], C[:, x, SEQ:T].unsqueeze(2),
                                                           ALU.mult, ALU.add).then_inc(s_conved, 1)
                            if x == 0:
                                dve.wait_ge(dhi, BASE + c + 1)
                                nc.vector.scalar_tensor_tensor(WD[1][:, l, :], SD[:, u], S_W, WD[0][:, l, :], ALU.mult,
                                                               ALU.subtract).then_inc(sd_free, 1)
                        dve.wait_ge(gelu_done, BASE + c + 1)
                        dve.wait_ge(lo_ready, BASE + c)
                        nc.vector.scalar_tensor_tensor(PRD[:], C[:, 0], S_G, C[:, 1], ALU.mult, ALU.mult).then_inc(prod_ready, 1)

                    def add(count, t, u, n):
                        dve.wait_ge(downed, BASE + count + 1)
                        nc.vector.scalar_tensor_tensor(HRES[:n, t], DB[u][:n].rearrange("p b n -> p (b n)"), UNDOWN, HRES[:n, t],
                                                       ALU.mult, ALU.add).then_inc(added, 1)

                    def norm(count, t, u, n):
                        dve.wait_ge(downed, BASE + count + 1)
                        dve.wait_ge(y_ready, BASE + t)
                        nc.vector.scalar_tensor_tensor(R[:n], DB[u][:n].rearrange("p b n -> p (b n)"), UNDOWN, HRES[:n, t],
                                                       ALU.mult, ALU.add).then_inc(added, 1)
                        dve.wait_ge(added, BASE + count + 1)
                        for c in range(2):
                            nc.vector.bn_stats(BST[:n, c], R[:n, c * 512:(c + 1) * 512]).then_inc(stats, 1)
                        dve.wait_ge(stats, BASE + 2 * t + 2)
                        dve.sem_inc(stats_go, 1)
                        nc.vector.bn_aggr(MV[:n], BST[:n].rearrange("p a b -> p (a b)")).then_inc(aggr, 1)
                        dve.wait_ge(aggr, BASE + t + 1)
                        nc.vector.tensor_scalar(VE[:n], MV[:n, 1:2], EPS, None, ALU.add).then_inc(var_ready, 1)
                        dve.wait_ge(rstd_ready, BASE + t + 1)
                        nc.vector.tensor_scalar(R[:n], R[:n], MV[:n, 0:1], RSTD[:n], ALU.subtract, ALU.mult).then_inc(xn_ready, 1)
                        dve.wait_ge(xn_ready, BASE + t + 1)
                        nc.vector.tensor_tensor(R[:n], R[:n], LNP[:n, 0], ALU.mult).then_inc(gained, 1)

                    def group(g, n, last):
                        chunk_loop(dve, g, n, last, step)
                        tile_loop(dve, g, norm if last else add)

                    dve.wait_ge(ln_in, BASE + 32)
                    groups(dve, group)


def constants():
    f = np.float32

    def angles(pos, n_rot, base):
        half = n_rot // 2
        inv = (base ** (-np.arange(half, dtype=f) / f(half)).astype(np.float64)).astype(f)
        ang = (pos.astype(f)[:, None] * inv[None, :]).astype(np.float64)
        return np.stack([np.cos(ang), np.sin(ang)], 1)

    pos = np.concatenate([np.arange(SEQ), np.full(P, PAST)])
    rope_ret = (angles(pos, E, 10000.0) * UNSCALE).reshape(NT + 1, P, 2, E // 2).transpose(1, 0, 2, 3)
    rope_att = (angles(pos, E // 4, 500000.0) * UNSCALE).reshape(NT + 1, P, 2, E // 8).transpose(1, 0, 2, 3)
    lg = np.log(1.0 - 2.0 ** (-5.0 - np.arange(H)))
    i = np.arange(P)
    rel = i[None, :] - i[:, None]
    decay = np.where(rel[:, None, :] >= 0, np.exp(lg[None, :, None] * np.maximum(rel, 0)[:, None, :]), 0.0) * E ** -0.5
    head = 2 * np.arange(HP)[None, :] + (np.arange(P) // E)[:, None]
    gq = np.exp(lg[head][:, :, None] * (i + 1.0)[None, None, :])
    kdec = np.repeat(np.exp(lg[None, :] * (P - 1.0 - i[:, None])) * E ** -0.5, E, axis=1)
    gchunk = np.exp(lg[head] * P)
    dist = i[:, None] + (SEQ - P) - np.arange(SEQ)[None, :]
    count = sum(((dist >= 0) & (dist <= w) & (dist % d == 0)).astype(int) for w, d in ((128, 1), (512, 4), (2048, 16)))
    mask = np.where(count > 0, np.log(np.maximum(count, 1)) / ATT_SCALE, NEG)
    gsample = np.tile(np.exp(lg), NB)[:, None]
    own_head = np.tile(np.eye(H), (NB, 1))
    return [np.ascontiguousarray(a, dtype=f) for a in
            (np.eye(P), rope_ret, rope_att, decay, gq, kdec, gchunk, mask, gsample, own_head)]


_INS = ['x_prompt', 'x_sample', 'cache_k_win', 'cache_v_win', 'state_ret', 'state_conv', 'p_prompt', 'p_sample',
        'ln_in_g', 'ln_in_b', 'w_in', 'w_out', 'ln1_g', 'ln1_b', 'w_up', 'conv_w', 'conv_b', 'w_down',
        'w_ple_gate', 'w_ple_proj', 'ln2_g', 'ln2_b']
_CONSTS = ['ident', 'rope_ret', 'rope_att', 'decay', 'gq', 'kdec', 'gchunk', 'mask', 'gsample', 'own_head']
_OUTS = [(1, SEQ, D), (NB, 1, D), (1, 1, SEQ, H, E), (1, 1, SEQ, H, E), (1, 1, H, E, E), (1, 1, 2, 2 * D_FF),
         (1, NB, 1, H, E), (1, NB, 1, H, E), (1, NB, H, E, E), (1, NB, 2, 2 * D_FF)]


def kernel(**inputs):
    import concourse.bacc as bacc
    from concourse.bass_utils import run_bass_kernel_spmd

    nc = bacc.Bacc("TRN2", target_bir_lowering=False, num_devices=1)
    arrays, args = {}, []
    for name in _INS:
        arrays[f"in_{name}"] = np.ascontiguousarray(inputs[name])
    for name, table in zip(_CONSTS, constants()):
        arrays[f"table_{name}"] = table
    for name, a in arrays.items():
        args.append(nc.dram_tensor(name, a.shape, mybir.dt.from_np(a.dtype), kind="ExternalInput").ap())
    for i, shape in enumerate(_OUTS):
        args.append(nc.dram_tensor(f"out_{i}", shape, F32, kind="ExternalOutput").ap())
    build(nc, *args)
    r = run_bass_kernel_spmd(nc, [arrays], core_ids=[0])
    return tuple(r.results[0][f"out_{i}"] for i in range(len(_OUTS)))
```

```python
from contextlib import ExitStack

import numpy as np
import concourse.bass as bass
from concourse import mybir

F32 = mybir.dt.float32
F16 = mybir.dt.float16
ALU = mybir.AluOpType
ACT = mybir.ActivationFunctionType
AX_X = mybir.AxisListType.X
ds = bass.ds

P = 128
D = 1024
SEQ = 1024
NB = 8
NT = SEQ // P
KD = D // P
H = 8
E = 64
HP = H // 2
HW = H * E
PAST = 8192
WIN = 2048
D_FF = 2816
NCH = D_FF // P
PLE = 256
EPS = 1e-5
ALPHA = 2.0 ** 0.25
S_ACT = 16.0
S_W = 64.0
UNSCALE = 1.0 / (S_ACT * S_W)
ATT_SCALE = E ** -0.5
NEG = -1e30
BASE = 4
PASSES = ((0, 0), (0, 1), (1, 0))


Q_ORDER = [(h, q) for h in range(2) for q in (7, 3, 6, 2, 5, 1, 4, 0)]


def build(nc, x_prompt, x_sample, cache_k, cache_v, state_ret, state_conv, p_prompt, p_sample,
          ln_in_g, ln_in_b, w_in, w_out, ln1_g, ln1_b, w_up, conv_w, conv_b, w_down,
          w_ple_gate, w_ple_proj, ln2_g, ln2_b,
          c_ident, c_rope_ret, c_rope_att, c_decay, c_gq, c_kdec, c_gchunk, c_mask, c_gsample, c_own,
          y_prompt, y_sample, kwin_p, vwin_p, ret_p, conv_p, kwin_s, vwin_s, ret_s, conv_s, debug=None):
    outer = ExitStack()
    with outer:
        stage = ["all"]

        def sb(stack, name, shape, dt=F32):
            return stack.enter_context(nc.sbuf_tensor(f"{stage[0]}_{name}", shape, dt))

        own, before = [], []

        def sems(names):
            made = [nc.alloc_semaphore(name=f"{stage[0]}_{n}") for n in names.split()]
            own.extend(made)
            return made

        def count_from_base(pool):
            for s in own:
                pool.sem_inc(s, BASE)

        def clear_before(sp):
            for s in before:
                sp.sem_clear(s)

        def product(out, n, lhs, w, c, kd):
            for k in range(kd):
                for a, b in PASSES:
                    mm = nc.tensor.matmul(out[:n], lhs(a, k), w(b, k, c), start=(k == 0 and (a, b) == (0, 0)),
                                          stop=(k == kd - 1 and (a, b) == (1, 0)))
            return mm

        def mix_product(u, n, row):
            for c in range(2):
                mm = product(M[u][:, c], n, (lambda a, k: MT[:, a, k, ds(row, P)]) if n == P else (lambda a, k: MTS[:, a, k]),
                             lambda b, k, c: WS[:, k // 4, b, 2 * (k % 4) + c], c, KD)
            return mm

        def end_stage():
            for s in before:
                nc.release_semaphore(s)
            before[:] = own
            own.clear()

        PS = outer.enter_context(nc.psum_tensor("PS", [P, 8, 512], F32))
        HRES = sb(outer, "HRES", [P, NT + 1, D])
        HT = sb(outer, "HT", [P, 2, KD, SEQ + NB], F16)
        M = (PS[:, 0:2], PS[:, 2:4])
        IDENT = sb(outer, "IDENT", [P, P])
        EPSC = sb(outer, "EPSC", [P, 2])
        MTS = sb(outer, "MTS", [P, 2, KD, NB], F16)
        CW = sb(outer, "CW", [P, 4, 2 * NCH])
        CWS = sb(outer, "CWS", [P, 3, 2 * NCH])
        ST = sb(outer, "ST", [P, 2 * NB, 2 * NCH])
        scratch = nc.dram_tensor("scratch", (7, NB, HW), F32, kind="Internal").ap()

        WS = sb(outer, "WS", [P, 2, 2, KD, 512], F16)

        mid = outer.enter_context(ExitStack())
        MT = sb(mid, "MT", [P, 2, KD, SEQ], F16)

        w_in_v = w_in.rearrange("a (k p) (j h n) -> p (a k) j h n", p=P, j=7, n=P)

        proj = outer.enter_context(ExitStack())
        STG = sb(proj, "STG", [P, 2, 2, 512])
        stage[0] = "norm_in"
        tables = outer.enter_context(ExitStack())
        ROPE = sb(tables, "R_ROPE", [P, NT + 1, 2, E // 2])
        DEC = sb(tables, "R_DEC", [P, H, P])
        GQ = sb(tables, "R_GQ", [P, HP, P])
        KDEC = sb(tables, "R_KDEC", [P, HW])
        GCH = sb(tables, "R_GCH", [P, HP])
        with ExitStack() as st:
            HS = sb(st, "HS", [P, 2, D])
            XN = sb(st, "XN", [P, 2, D])
            LNP = sb(st, "LNP", [P, 2, D])
            BST = sb(st, "BST", [P, 2, 2, 6])
            MV = sb(st, "MV", [P, 2, 2])
            VE = sb(st, "VE", [P, 2])
            RSTD = sb(st, "RSTD", [P, 2])
            (const_in, stats_done, aggr_done, var_ready, rstd_ready, xn_ready, gained,
             h_ready, h_copied, turned, hi_ready, lo_ready, w_free, whi, tab_in) = sems(
                "const_in stats_done aggr_done var_ready rstd_ready xn_ready gained "
                    "h_ready h_copied turned hi_ready lo_ready w_free whi tab_in")
            stats_seen, = sems("stats_seen")
            CRAW = sb(st, "CRAW", [P, 4, P])
            SRAW = sb(st, "SRAW", [P, 2 * NB, P])
            par_in, par_turned = sems("par_in par_turned")
            x_in = sems("x_in0 x_in1 x_in2")
            w_in_s = sems("w_in_s0 w_in_s1")
            with nc.Block() as block:
                @block.sync
                def _(sp):
                    sp.sem_inc(w_free, 2)
                    def load_x(t, u, first=False):
                        if not first:
                            sp.wait_ge(x_in[u], BASE + 8 * (t - u))
                        sp.dma_start(HRES[:, t], x_prompt[0, ds(t * P, P), :]).then_inc(x_in[u], 16)

                    def load_w(c):
                        sp.wait_ge(w_free, BASE + c + 1)
                        for k in range(2):
                            sp.dma_start(STG[:, c % 2, k].rearrange("p (j n) -> p j n", j=4),
                                         w_in_v[:, 2 * c + k, 0:4, 0, :]).then_inc(w_in_s[c % 2], 16)

                    for t in range(2):
                        load_x(t, t, first=True)
                    for j, v in ((0, ln_in_g), (1, ln_in_b)):
                        sp.dma_start(LNP[:, j], v.rearrange("(a n) -> a n", a=1).broadcast_to([P, D])).then_inc(const_in, 16)
                    sp.dma_start(IDENT[:], c_ident).then_inc(const_in, 16)
                    load_w(0)
                    load_w(1)
                    sp.dma_start(CRAW[:2 * NCH, 0:3], conv_w.rearrange("a j (c f) -> c (a j) f", f=P)).then_inc(par_in, 16)
                    sp.dma_start(CRAW[:2 * NCH, 3], conv_b.rearrange("a (c f) -> (a c) f", f=P)).then_inc(par_in, 16)
                    sp.dma_start(SRAW[:2 * NCH], state_conv.rearrange("a b j (c f) -> c (a b j) f", f=P)).then_inc(par_in, 16)
                    for t in range(2, 4):
                        load_x(t, t % 2)
                    load_w(2)
                    load_w(3)
                    with sp.Fori(2, NT // 2) as i:
                        for u in range(2):
                            load_x(2 * i + u, u)
                    sp.dma_start(HRES[:NB, NT], x_sample[:, 0, :]).then_inc(x_in[2], 16)
                    for dst, src in ((ROPE, c_rope_ret), (DEC, c_decay), (GQ, c_gq), (KDEC, c_kdec), (GCH, c_gchunk)):
                        sp.dma_start(dst[:], src).then_inc(tab_in, 16)
                    sp.wait_ge(tab_in, BASE + 80)
                    clear_before(sp)

                @block.vector
                def _(dve):
                    nc.vector.memset(EPSC[:], -0.5).then_inc(stats_seen, 1)
                    def stats(t, u, n, sem, count):
                        dve.wait_ge(sem, BASE + count)
                        for c in range(2):
                            nc.vector.bn_stats(BST[:n, u, c], HRES[:n, t, c * 512:(c + 1) * 512]).then_inc(stats_done, 1)
                        dve.wait_ge(stats_done, BASE + 2 * t + 2)
                        dve.sem_inc(stats_seen, 1)
                        nc.vector.bn_aggr(MV[:n, u], BST[:n, u].rearrange("p a b -> p (a b)")).then_inc(aggr_done, 1)
                        dve.wait_ge(aggr_done, BASE + t + 1)
                        nc.vector.tensor_scalar(VE[:n, u:u + 1], MV[:n, u, 1:2], EPS, None, ALU.add).then_inc(var_ready, 1)

                    def norm(t, u, n):
                        dve.wait_ge(rstd_ready, BASE + t + 1)
                        dve.wait_ge(h_ready, BASE + t - 1)
                        nc.vector.tensor_scalar(XN[:n, u], HRES[:n, t], MV[:n, u, 0:1], RSTD[:n, u:u + 1], ALU.subtract,
                                                ALU.mult).then_inc(xn_ready, 1)
                        dve.wait_ge(xn_ready, BASE + t + 1)
                        nc.vector.tensor_tensor(XN[:n, u], XN[:n, u], LNP[:n, 0], ALU.mult).then_inc(gained, 1)

                    def low(t, n, b):
                        dve.wait_ge(hi_ready, BASE + t + 1)
                        nc.vector.scalar_tensor_tensor(
                            HT[:, 1, :, ds(t * P, n)], PS[:, b:b + 2].rearrange("p b (k n) -> p (b k) n", k=4)[:, :, :n],
                            S_ACT, HT[:, 0, :, ds(t * P, n)], ALU.mult, ALU.subtract).then_inc(lo_ready, 1)

                    def split(c):
                        dve.wait_ge(whi, BASE + c + 1)
                        nc.vector.scalar_tensor_tensor(WS[:, 0, 1, 2 * c:2 * c + 2], STG[:, c % 2], S_W,
                                                       WS[:, 0, 0, 2 * c:2 * c + 2], ALU.mult, ALU.subtract).then_inc(w_free, 1)

                    stats(0, 0, P, x_in[0], 16)
                    stats(1, 1, P, x_in[1], 16)
                    dve.wait_ge(const_in, BASE + 48)
                    norm(0, 0, P)
                    stats(2, 0, P, x_in[0], 32)
                    norm(1, 1, P)
                    split(0)
                    split(1)
                    with dve.Fori(1, NT // 2 - 1) as i:
                        for u in range(2):
                            stats(2 * i + u + 1, 1 - u, P, x_in[1 - u], 16 * i + 16 + 16 * u)
                            norm(2 * i + u, u, P)
                            low(2 * i + u - 2, P, 2 * u)
                    stats(NT - 1, 1, P, x_in[1], 8 * NT)
                    norm(NT - 2, 0, P)
                    low(NT - 4, P, 0)
                    stats(NT, 0, NB, x_in[2], 16)
                    norm(NT - 1, 1, P)
                    low(NT - 3, P, 2)
                    norm(NT, 0, NB)
                    low(NT - 2, P, 0)
                    split(2)
                    split(3)
                    low(NT - 1, P, 2)
                    low(NT, NB, 0)

                @block.gpsimd
                def _(pool):
                    count_from_base(pool)
                    pool.wait_ge(const_in, BASE + 48)
                    pool.wait_ge(stats_seen, BASE + 1)

                    def scale(t, u, n):
                        pool.wait_ge(var_ready, BASE + t + 1)
                        nc.gpsimd.tensor_tensor(RSTD[:n, u:u + 1], VE[:n, u:u + 1], EPSC[:n, 0:1], ALU.pow).then_inc(rstd_ready, 1)

                    def shift(t, u, n):
                        pool.wait_ge(gained, BASE + t + 1)
                        pool.wait_ge(turned, BASE + t - 1)
                        pool.wait_ge(h_copied, BASE + t - 1)
                        nc.gpsimd.tensor_tensor(HS[:n, u], XN[:n, u], LNP[:n, 1], ALU.add).then_inc(h_ready, 1)

                    scale(0, 0, P)
                    with pool.Fori(0, NT // 2 - 1) as i:
                        for u in range(2):
                            scale(2 * i + u + 1, 1 - u, P)
                            shift(2 * i + u, u, P)
                    scale(NT - 1, 1, P)
                    shift(NT - 2, 0, P)
                    scale(NT, 0, NB)
                    shift(NT - 1, 1, P)
                    shift(NT, 0, NB)

                @block.tensor
                def _(pe):
                    pe.wait_ge(const_in, BASE + 48)

                    def turn(t, u, n):
                        pe.wait_ge(h_ready, BASE + t + 1)
                        for k in range(KD):
                            last = nc.tensor.transpose(PS[:, 2 * u + k // 4, (k % 4) * P:(k % 4) * P + n],
                                                       HS[:n, u, k * P:(k + 1) * P], IDENT[:n, :n])
                        last.then_inc(turned, 1)

                    turn(0, 0, P)
                    turn(1, 1, P)
                    with pe.Fori(0, NT // 2 - 1) as i:
                        for u in range(2):
                            pe.wait_ge(lo_ready, BASE + 2 * i + u + 1)
                            turn(2 * i + u + 2, u, P)
                    pe.wait_ge(lo_ready, BASE + NT - 1)
                    turn(NT, 0, NB)
                    pe.wait_ge(par_in, BASE + 48)
                    for j in range(4 + 2 * NB):
                        src = CRAW[:2 * NCH, j] if j < 4 else SRAW[:2 * NCH, j - 4]
                        mm = nc.tensor.transpose(PS[:, 4 + j // 10, (j % 10) * 2 * NCH:(j % 10 + 1) * 2 * NCH],
                                                 src, IDENT[:2 * NCH, :2 * NCH])
                    mm.then_inc(par_turned, 1)

                @block.scalar
                def _(act):
                    def high(t, u, n):
                        act.wait_ge(h_ready, BASE + t + 1)
                        nc.scalar.activation(HRES[:n, t], HS[:n, u], ACT.Copy).then_inc(h_copied, 1)
                        act.wait_ge(turned, BASE + t + 1)
                        nc.scalar.activation(HT[:, 0, :, ds(t * P, n)],
                                             PS[:, 2 * u:2 * u + 2].rearrange("p b (k n) -> p (b k) n", k=4)[:, :, :n],
                                             ACT.Copy, scale=S_ACT).then_inc(hi_ready, 1)

                    def split(c):
                        act.wait_ge(w_in_s[c % 2], BASE + 32 * (c // 2) + 32)
                        nc.scalar.activation(WS[:, 0, 0, 2 * c:2 * c + 2], STG[:, c % 2], ACT.Copy,
                                             scale=S_W).then_inc(whi, 1)

                    split(0)
                    split(1)
                    with act.Fori(0, NT // 2) as i:
                        for u in range(2):
                            high(2 * i + u, u, P)
                    split(2)
                    split(3)
                    high(NT, 0, NB)
                    act.wait_ge(par_turned, BASE + 1)
                    n = 2 * NCH
                    nc.scalar.activation(CW[:].rearrange("p j c -> p (j c)"), PS[:, 4, 0:4 * n], ACT.Copy)
                    nc.scalar.activation(CWS[:].rearrange("p j c -> p (j c)"), PS[:, 4, 0:3 * n], ACT.Copy, scale=UNSCALE)
                    st_rows = ST[:].rearrange("p j c -> p (j c)")
                    nc.scalar.activation(st_rows[:, 0:6 * n], PS[:, 4, 4 * n:10 * n], ACT.Copy)
                    nc.scalar.activation(st_rows[:, 6 * n:16 * n], PS[:, 5, 0:10 * n], ACT.Copy)
        end_stage()
        stage[0] = "retention"
        with ExitStack() as st:
            STATE = sb(st, "STATE", [P, HP, P])
            T1 = sb(st, "T1", [P, 256])
            T2 = sb(st, "T2", [P, 256])
            QK = sb(st, "QK", [P, 2, 256])
            QKT = sb(st, "QKT", [P, 2, 256])
            V = sb(st, "V", [P, NT, P])
            G = sb(st, "G", [P, NT, P])
            QG = sb(st, "QG", [P, 4, P])
            KG = sb(st, "KG", [P, 4, P])
            SD = sb(st, "SD", [P, 2, 2, P])
            BST = sb(st, "BST", [P, 2, 6])
            MV = sb(st, "MV", [P, 2, 2])
            VE = sb(st, "VE", [P, 2])
            RSTD = sb(st, "RSTD", [P, 2])
            RN = sb(st, "RN", [P, P])
            R = sb(st, "R", [P, 2, P])
            ZS = sb(st, "ZS", [P, 512])
            TB, SB, OB, UB, RB = PS[:, 2, 0:256], PS[:, 3:5, 0:P], PS[:, 7, 0:P], PS[:, 7, P:2 * P], PS[:, 6, 0:P]

            def Z(s):
                return PS[:, 5] if s == NT else PS[:, s % 2]
            (z_ready, z_turned, v_ready, halves, rotated, qkt_ready, qg_ready, kg_ready, scored, sd_ready,
             out_ready, stats, stats_seen, aggr, var_ready, rstd_ready, state_ready, normed, r_ready, r_turned, rhi,
             rlo, pe_go, zs_out, w_free, whi, state_zero) = sems(
                "z_ready z_turned v_ready halves rotated qkt_ready qg_ready kg_ready scored sd_ready "
                    "out_ready stats stats_seen aggr var_ready rstd_ready state_ready normed r_ready r_turned rhi "
                    "rlo pe_go zs_out w_free whi state_zero")
            w_in_s = sems("w_in_s0 w_in_s1")

            def steps(body):
                def run(eng):
                    with eng.Fori(0, HP - 1) as p:
                        body(eng, p, False)
                    body(eng, HP - 1, True)
                return run

            def staggered(body):
                def run(eng):
                    body(eng, 0, "first")
                    with eng.Fori(1, HP - 1) as p:
                        body(eng, p, "middle")
                    body(eng, HP - 1, "last")
                    body(eng, HP, "after")
                return run

            def nsteps(kind):
                return 3 if kind == "after" else NT + 1

            def tile_at(s, lag, p, kind):
                t = s - lag
                if t >= 0:
                    return (p, t) if kind != "after" and t < NT else (p, None)
                t += NT + 1
                return (p - 1, t) if kind != "first" and t < NT else (p, None)

            with nc.Block() as block:
                @block.sync
                def _(sp):
                    sp.sem_inc(w_free, 2)

                    def body(sp, p, last):
                        for c in range(4):
                            sp.wait_ge(w_free, BASE + 4 * p + c + 1)
                            for k in range(2):
                                if last:
                                    sp.dma_start(STG[:, c % 2, k, 0:384].rearrange("p (j n) -> p j n", j=3),
                                                 w_in_v[:, 2 * c + k, 4:7, 0, :]).then_inc(w_in_s[c % 2], 16)
                                else:
                                    sp.dma_start(STG[:, c % 2, k].rearrange("p (j n) -> p j n", j=4),
                                                 w_in_v[:, 2 * c + k, 0:4, p + 1, :]).then_inc(w_in_s[c % 2], 16)
                        sp.wait_ge(rotated, BASE + 18 * p + 18)
                        sp.wait_ge(v_ready, BASE + 9 * p + 9)
                        sp.dma_start(scratch[0:4, :, ds(p * P, P)].rearrange("j b n -> b j n"),
                                     ZS[:NB].rearrange("b (j n) -> b j n", j=4)).then_inc(zs_out, 16)
                    steps(body)(sp)
                    sp.wait_ge(state_ready, BASE + HP * NT)
                    for hh in range(2):
                        sp.dma_start(ret_p.rearrange("a b (p t) d e -> (a b t) d p e", t=2)[hh],
                                     STATE[hh * E:(hh + 1) * E, :, hh * E:(hh + 1) * E]).then_inc(zs_out, 16)
                    sp.wait_ge(zs_out, BASE + 16 * HP + 32)
                    clear_before(sp)

                @block.tensor
                def _(pe):
                    def body(pe, p, kind):
                        slot = p % 2
                        for s in range(nsteps(kind)):
                            if kind != "after":
                                n = P if s < NT else NB
                                if s == 0:
                                    pe.wait_ge(w_free, BASE + 4 * p + 2)
                                done = 9 * p + (s - 2 if s < 2 else 0 if s == NT else s - 1)
                                if s >= 2 and s < NT or kind != "first":
                                    pe.wait_ge(halves, BASE + 2 * done)
                                    pe.wait_ge(v_ready, BASE + done)
                                if s == NT:
                                    pe.sem_inc(pe_go, 1)
                                for k in range(KD):
                                    for a, b in PASSES:
                                        mm = nc.tensor.matmul(Z(s)[:n], HT[:, a, k, s * P:s * P + n],
                                                              WS[:, slot, b, k, :], start=(k == 0 and (a, b) == (0, 0)),
                                                              stop=(k == KD - 1 and (a, b) == (1, 0)))
                                mm.then_inc(z_ready, 1)
                            q, t = tile_at(s, 1, p, kind)
                            if t is not None:
                                pe.wait_ge(rotated, BASE + 18 * q + 2 * t + 2)
                                pe.wait_ge(qkt_ready, BASE + 8 * q + t)
                                for j in range(2):
                                    mm = nc.tensor.transpose(TB[:, j * P:(j + 1) * P], QK[:, t % 2, j * P:(j + 1) * P], IDENT[:])
                                mm.then_inc(z_turned, 1)
                            q, t = tile_at(s, 2, p, kind)
                            if t is not None:
                                pe.wait_ge(qkt_ready, BASE + 8 * q + t + 1)
                                pe.wait_ge(sd_ready, BASE + 8 * q + t)
                                for h in range(2):
                                    r = slice(h * E, (h + 1) * E)
                                    mm = nc.tensor.matmul(SB[:, h], QKT[r, t % 2, P:2 * P],
                                                          QKT[r, t % 2, 0:P], start=True, stop=True)
                                mm.then_inc(scored, 1)
                            q, t = tile_at(s, 3, p, kind)
                            if t is not None:
                                pe.wait_ge(sd_ready, BASE + 8 * q + t + 1)
                                pe.wait_ge(qg_ready, BASE + 8 * q + t + 1)
                                pe.wait_ge(kg_ready, BASE + 8 * q + t + 1)
                                pe.wait_ge(state_ready, BASE + 8 * q + t)
                                pe.wait_ge(normed, BASE + 16 * q + 2 * t)
                                if t == 0:
                                    pe.wait_ge(state_zero, BASE + 1)
                                nc.tensor.matmul(OB, QG[:, t % 4], STATE[:, q, :], start=True, stop=False)
                                for h in range(2):
                                    nc.tensor.matmul(OB[:, h * E:(h + 1) * E], SD[:, t % 2, h], V[:, t, h * E:(h + 1) * E],
                                                     start=False, stop=(h == 1))
                                nc.tensor.matmul(UB, KG[:, t % 4], V[:, t], start=True, stop=True).then_inc(out_ready, 1)
                            q, t = tile_at(s, 4, p, kind)
                            if t is not None:
                                pe.wait_ge(r_ready, BASE + 8 * q + t + 1)
                                pe.wait_ge(rlo, BASE + 8 * q + t)
                                nc.tensor.transpose(RB, R[:, t % 2], IDENT[:]).then_inc(r_turned, 1)
                    staggered(body)(pe)

                @block.scalar
                def _(act):
                    def body(act, p, kind):
                        cols = 384 if kind == "last" else 512
                        for s in range(nsteps(kind)):
                            if kind != "after":
                                act.wait_ge(halves, BASE + 18 * p + 2 * s + 2)
                                if s < NT:
                                    if kind != "first":
                                        act.wait_ge(out_ready, BASE + 8 * (p - 1) + s + 1)
                                        act.wait_ge(r_ready, BASE + 8 * (p - 1) + s + 1)
                                    nc.scalar.activation(V[:, s], Z(s)[:, 256:384], ACT.Copy, scale=UNSCALE)
                                    nc.scalar.activation(G[:, s], Z(s)[:, 384:512], ACT.Silu, scale=UNSCALE).then_inc(v_ready, 1)
                                else:
                                    act.wait_ge(zs_out, BASE + 16 * p)
                                    nc.scalar.activation(ZS[:NB, 256:384], Z(s)[:NB, 256:384], ACT.Copy, scale=UNSCALE)
                                    nc.scalar.activation(ZS[:NB, 384:512], Z(s)[:NB, 384:512], ACT.Silu,
                                                         scale=UNSCALE).then_inc(v_ready, 1)
                            q, t = tile_at(s, 1, p, kind)
                            if t is not None:
                                act.wait_ge(z_turned, BASE + 8 * q + t + 1)
                                act.wait_ge(scored, BASE + 8 * q + t - 1)
                                act.wait_ge(qg_ready, BASE + 8 * q + t - 1)
                                nc.scalar.activation(QKT[:, t % 2], TB, ACT.Copy).then_inc(qkt_ready, 1)
                            q, t = tile_at(s, 4, p, kind)
                            if t is not None:
                                act.wait_ge(r_turned, BASE + 8 * q + t + 1)
                                nc.scalar.activation(MT[:, 0, q, t * P:(t + 1) * P], RB, ACT.Copy, scale=S_ACT).then_inc(rhi, 1)
                            if s in (1, 3, 5, 7) and kind != "after":
                                c = s // 2
                                act.wait_ge(w_in_s[c % 2], BASE + 64 * p + 32 * (c // 2) + 32)
                                if c == 0:
                                    act.wait_ge(z_ready, BASE + 9 * p)
                                nc.scalar.activation(WS[:, (p + 1) % 2, 0, 2 * c:2 * c + 2, 0:cols], STG[:, c % 2, :, 0:cols],
                                                     ACT.Copy, scale=S_W).then_inc(whi, 1)
                    staggered(body)(act)

                @block.vector
                def _(dve):
                    nc.vector.memset(STATE[:], 0.0).then_inc(state_zero, 1)
                    dve.wait_ge(state_zero, BASE + 1)

                    def turn_pairs(p, s, n, out):
                        dve.wait_ge(z_ready, BASE + 9 * p + s + 1)
                        dve.wait_ge(rotated, BASE + 18 * p + 2 * s)
                        z = Z(s)[:n, 0:256].rearrange("p (g e) -> p g e", e=E // 2)
                        for j, dst in ((0, T1), (1, T2)):
                            nc.vector.tensor_tensor(dst[:n].rearrange("p (g e) -> p g e", e=E // 2), z,
                                                    ROPE[:n, s, j].unsqueeze(1).broadcast_to([n, 8, E // 2]),
                                                    ALU.mult).then_inc(halves, 1)
                        dve.wait_ge(halves, BASE + 18 * p + 2 * s + 2)
                        c, d, o = (x[:n].rearrange("p (g a e) -> p g a e", a=2, e=E // 2) for x in (T1, T2, out))
                        nc.vector.tensor_tensor(o[:, :, 0], c[:, :, 0], d[:, :, 1], ALU.subtract).then_inc(rotated, 1)
                        nc.vector.tensor_tensor(o[:, :, 1], c[:, :, 1], d[:, :, 0], ALU.add).then_inc(rotated, 1)

                    def body(dve, p, kind):
                        cols = 384 if kind == "last" else 512
                        for s in range(nsteps(kind)):
                            if kind == "after":
                                pass
                            elif s < NT:
                                dve.wait_ge(z_turned, BASE + 8 * p + s - 1)
                                turn_pairs(p, s, P, QK[:, s % 2])
                            else:
                                dve.wait_ge(zs_out, BASE + 16 * p)
                                turn_pairs(p, s, NB, ZS[:, 0:256])
                            q, t = tile_at(s, 1, p, kind)
                            if t is not None:
                                dve.wait_ge(out_ready, BASE + 8 * q + t - 3)
                                dve.wait_ge(qkt_ready, BASE + 8 * q + t + 1)
                                dve.wait_ge(rotated, BASE + 18 * q + 2 * t + 2)
                                nc.vector.tensor_tensor(QG[:, t % 4], QKT[:, t % 2, 0:P], GQ[:, q, :], ALU.mult).then_inc(qg_ready, 1)
                                nc.vector.tensor_tensor(KG[:, t % 4], QK[:, t % 2, P:2 * P], KDEC[:, ds(q * P, P)],
                                                        ALU.mult).then_inc(kg_ready, 1)
                            q, t = tile_at(s, 2, p, kind)
                            if t is not None:
                                dve.wait_ge(scored, BASE + 8 * q + t + 1)
                                dve.wait_ge(out_ready, BASE + 8 * q + t - 1)
                                nc.vector.tensor_tensor(SD[:, t % 2], SB,
                                                        DEC[:, ds(2 * q, 2), :], ALU.mult).then_inc(sd_ready, 1)
                            q, t = tile_at(s, 3, p, kind)
                            if t is not None:
                                dve.wait_ge(out_ready, BASE + 8 * q + t + 1)
                                for h in range(2):
                                    r = slice(h * E, (h + 1) * E)
                                    mm = nc.vector.scalar_tensor_tensor(STATE[r, q, h * E:(h + 1) * E], STATE[r, q, h * E:(h + 1) * E],
                                                                        GCH[r, q:q + 1] if isinstance(q, int) else GCH[r, ds(q, 1)],
                                                                        UB[r, h * E:(h + 1) * E], ALU.mult, ALU.add)
                                mm.then_inc(state_ready, 1)
                                for h in range(2):
                                    nc.vector.bn_stats(BST[:, h], OB[:, h * E:(h + 1) * E]).then_inc(stats, 1)
                                dve.wait_ge(stats, BASE + 16 * q + 2 * t + 2)
                                dve.sem_inc(stats_seen, 1)
                                for h in range(2):
                                    nc.vector.bn_aggr(MV[:, h], BST[:, h]).then_inc(aggr, 1)
                                dve.wait_ge(aggr, BASE + 16 * q + 2 * t + 2)
                                nc.vector.tensor_scalar(VE[:], MV[:, :, 1], EPS, None, ALU.add).then_inc(var_ready, 1)
                            qu, u = tile_at(s, 4, p, kind)
                            if u is not None:
                                dve.wait_ge(rhi, BASE + 8 * qu + u + 1)
                                nc.vector.scalar_tensor_tensor(MT[:, 1, qu, u * P:(u + 1) * P], RB, S_ACT,
                                                               MT[:, 0, qu, u * P:(u + 1) * P], ALU.mult, ALU.subtract).then_inc(rlo, 1)
                            if s in (1, 3, 5, 7) and kind != "after":
                                c = s // 2
                                dve.wait_ge(whi, BASE + 4 * p + c + 1)
                                nc.vector.scalar_tensor_tensor(WS[:, (p + 1) % 2, 1, 2 * c:2 * c + 2, 0:cols], STG[:, c % 2, :, 0:cols],
                                                               S_W, WS[:, (p + 1) % 2, 0, 2 * c:2 * c + 2, 0:cols],
                                                               ALU.mult, ALU.subtract).then_inc(w_free, 1)
                            if t is not None:
                                dve.wait_ge(rstd_ready, BASE + 8 * q + t + 1)
                                for h in range(2):
                                    nc.vector.tensor_scalar(RN[:, h * E:(h + 1) * E], OB[:, h * E:(h + 1) * E], MV[:, h, 0:1],
                                                            RSTD[:, h:h + 1], ALU.subtract, ALU.mult).then_inc(normed, 1)
                                dve.wait_ge(normed, BASE + 16 * q + 2 * t + 2)
                                dve.wait_ge(r_turned, BASE + 8 * q + t - 1)
                                nc.vector.tensor_tensor(R[:, t % 2], RN[:], G[:, t], ALU.mult).then_inc(r_ready, 1)
                    staggered(body)(dve)

                @block.gpsimd
                def _(pool):
                    count_from_base(pool)
                    with pool.Fori(0, HP * NT) as n:
                        pool.wait_ge(var_ready, BASE + n + 1)
                        nc.gpsimd.tensor_tensor(RSTD[:], VE[:], EPSC[:], ALU.pow).then_inc(rstd_ready, 1)
        tables.close()
        end_stage()
        stage[0] = "attention"
        with ExitStack() as st:
            ROPE = sb(st, "ROPE", [P, NT + 1, 2, E // 8])
            MASK = sb(st, "MASK", [P, SEQ])
            T1 = sb(st, "T1", [P, 64])
            T2 = sb(st, "T2", [P, 64])
            QKV = sb(st, "QKV", [P, NT + 1, 384])
            QKT = sb(st, "QKT", [P, 2, 2, SEQ], F16)
            V16 = sb(st, "V16", [P, 2, NT, P], F16)
            PR = sb(st, "PR", [P, 3, SEQ])
            PRT = sb(st, "PRT", [P, 3, 2, NT, P], F16)
            MX = sb(st, "MX", [P, 2])
            NMX = sb(st, "NMX", [P, 3])
            SUM = sb(st, "SUM", [P, 8])
            RCP = sb(st, "RCP", [P, 2])
            ATT = sb(st, "ATT", [P, NT, P])
            Z, TB, OB, MB = PS[:, 0:2], PS[:, 2, 0:256], PS[:, 6:8, 0:E], PS[:, 3:5]
            SB = (PS[:, 0:2], PS[:, 2:3])
            PT = (PS[:, 3:5], PS[:, 5:6])
            NQ = len(Q_ORDER)
            LOG_S_P = float(np.log(1024.0))
            (tab_in, z_ready, z_turned, copied, halves, rotated, qkt_ready, scored, masked, neg_ready, exp_ready,
             p_turned, prt_ready, o_ready, rcp_ready, att_ready, att_turned, qkt_low, prt_low, v_hi, v_lo, mhi, mlo, out_st, w_free, whi,
             pe_go, dve_go, pool_go) = sems(
                "tab_in z_ready z_turned copied halves rotated qkt_ready scored masked neg_ready exp_ready "
                    "p_turned prt_ready o_ready rcp_ready att_ready att_turned qkt_low prt_low v_hi v_lo mhi mlo "
                    "out_st w_free whi pe_go dve_go pool_go")
            w_in_s = sems("w_in_s0 w_in_s1")

            with nc.Block() as block:
                @block.sync
                def _(sp):
                    sp.sem_inc(w_free, 2)
                    for dst, src in ((ROPE, c_rope_att), (MASK, c_mask)):
                        sp.dma_start(dst[:], src).then_inc(tab_in, 16)

                    def body(sp, p, last):
                        for c in range(0 if last else 4):
                            sp.wait_ge(w_free, BASE + 4 * p + c + 1)
                            for k in range(2):
                                sp.dma_start(STG[:, c % 2, k, 0:384].rearrange("p (j n) -> p j n", j=3),
                                             w_in_v[:, 2 * c + k, 4:7, p + 1, :]).then_inc(w_in_s[c % 2], 16)
                        for k in range(KD if last else 0):
                            sp.wait_ge(w_free, BASE + 4 * p + k + 1)
                            sp.dma_start(STG[:, k % 2], w_out[0, k * P:(k + 1) * P].rearrange("p (c n) -> p c n", c=2)).then_inc(w_in_s[k % 2], 16)
                        sp.wait_ge(rotated, BASE + 18 * p + 18)
                        for j, pr, sm in ((1, kwin_p, kwin_s), (2, vwin_p, vwin_s)):
                            cols = slice(j * P, (j + 1) * P)
                            sp.dma_start(pr.rearrange("a b (t p) h e -> p (a b t) (h e)", p=P)[:, :, ds(p * P, P)],
                                         QKV[:, 0:NT, cols]).then_inc(out_st, 16)
                            sp.dma_start(sm.rearrange("a b t h e -> (a b t) (h e)")[:, ds(p * P, P)],
                                         QKV[:NB, NT, cols]).then_inc(out_st, 16)
                        sp.dma_start(scratch[4:7, :, ds(p * P, P)].rearrange("j b n -> b j n"),
                                     QKV[:NB, NT].rearrange("b (j n) -> b j n", j=3)).then_inc(out_st, 16)
                    steps(body)(sp)
                    sp.wait_ge(out_st, BASE + 80 * HP)
                    clear_before(sp)

                @block.gpsimd
                def _(pool):
                    count_from_base(pool)

                    def body(pool, p, last):
                        pool.wait_ge(o_ready, BASE + NQ * p)
                        pool.wait_ge(copied, BASE + 9 * p + 8)
                        pool.sem_inc(pool_go, 1)
                        nc.gpsimd.tensor_scalar(V16[:, 0], QKV[:, 0:NT, 256:384], 1.0, None, ALU.mult).then_inc(v_hi, 1)
                        pool.wait_ge(v_hi, BASE + p + 1)
                        nc.gpsimd.tensor_tensor(V16[:, 1], QKV[:, 0:NT, 256:384], V16[:, 0], ALU.subtract).then_inc(v_lo, 1)
                    steps(body)(pool)

                @block.tensor
                def _(pe):
                    def attend(n, p):
                        if n < NQ:
                            h, q = Q_ORDER[n]
                            r = slice(h * E, (h + 1) * E)
                            if n == 0:
                                pe.wait_ge(qkt_low, BASE + 8 * p + 8)
                                pe.wait_ge(rotated, BASE + 18 * p + 18)
                            pe.wait_ge(masked, BASE + NQ * p + n - 1)
                            for c in range(q // 4 + 1):
                                w = min(512, (q + 1) * P - c * 512)
                                for a, b in PASSES:
                                    mm = nc.tensor.matmul(SB[n % 2][:, c, 0:w], QKT[r, a, 0, q * P:(q + 1) * P],
                                                          QKT[r, b, 1, c * 512:c * 512 + w], start=(a, b) == (0, 0), stop=(a, b) == (1, 0))
                            mm.then_inc(scored, 1)
                        m = n - 2
                        if 0 <= m < NQ:
                            pe.wait_ge(exp_ready, BASE + NQ * p + m + 1)
                            if m == 0:
                                pe.wait_ge(mlo, BASE + p)
                            pe.wait_ge(prt_low, BASE + NQ * p + m - 1)
                            q = Q_ORDER[m][1]
                            for kb in range(q + 1):
                                mm = nc.tensor.transpose(PT[m % 2][:, kb // 4, (kb % 4) * P:(kb % 4 + 1) * P],
                                                         PR[:, m % 3, kb * P:(kb + 1) * P], IDENT[:])
                            mm.then_inc(p_turned, 1)
                        m = n - 4
                        if 0 <= m < NQ:
                            h, q = Q_ORDER[m]
                            pe.wait_ge(prt_low, BASE + NQ * p + m + 1)
                            pe.wait_ge(att_ready, BASE + NQ * p + m - 1)
                            if m == 0:
                                pe.wait_ge(v_lo, BASE + p + 1)
                            for kb in range(q + 1):
                                for a, b in PASSES:
                                    mm = nc.tensor.matmul(OB[:, m % 2], PRT[:, m % 3, a, kb], V16[:, b, kb, h * E:(h + 1) * E],
                                                          start=(kb == 0 and (a, b) == (0, 0)), stop=(kb == q and (a, b) == (1, 0)))
                            mm.then_inc(o_ready, 1)

                    def body(pe, p, kind):
                        slot = p % 2
                        if kind != "after":
                            pe.wait_ge(masked, BASE + NQ * p)
                            pe.wait_ge(w_free, BASE + 4 * p + 2)
                        for s in range(NT + 2):
                            if s <= NT and kind != "after":
                                n = P if s < NT else NB
                                if s >= 2:
                                    pe.wait_ge(rotated, BASE + 18 * p + 2 * s - 2)
                                if s == NT:
                                    pe.sem_inc(pe_go, 1)
                                for k in range(KD):
                                    for a, b in PASSES:
                                        mm = nc.tensor.matmul(Z[:n, s % 2, 0:384], HT[:, a, k, s * P:s * P + n],
                                                              WS[:, slot, b, k, 0:384], start=(k == 0 and (a, b) == (0, 0)),
                                                              stop=(k == KD - 1 and (a, b) == (1, 0)))
                                mm.then_inc(z_ready, 1)
                            t = s - 1
                            if 0 <= t < NT and kind != "after":
                                pe.wait_ge(rotated, BASE + 18 * p + 2 * t + 2)
                                pe.wait_ge(qkt_low, BASE + 8 * p + t)
                                for j in range(2):
                                    mm = nc.tensor.transpose(TB[:, j * P:(j + 1) * P], QKV[:, t, j * P:(j + 1) * P], IDENT[:])
                                mm.then_inc(z_turned, 1)
                            if kind != "first" and s < 4:
                                attend(NQ + s, p - 1)
                            if kind != "first" and s == 5:
                                pe.wait_ge(att_ready, BASE + NQ * p)
                                for t in range(NT):
                                    mm = nc.tensor.transpose(MB[:, t // 4, (t % 4) * P:(t % 4 + 1) * P], ATT[:, t], IDENT[:])
                                mm.then_inc(att_turned, 1)
                        if kind != "after":
                            for n in range(NQ):
                                attend(n, p)
                    staggered(body)(pe)

                @block.scalar
                def _(act):
                    def split_out(k):
                        act.wait_ge(w_in_s[k % 2], BASE + 64 * (HP - 1) + 16 * (k // 2) + 16)
                        if k == 4:
                            act.wait_ge(z_ready, BASE + 9 * HP)
                        nc.scalar.activation(WS[:, k // 4, 0, 2 * (k % 4):2 * (k % 4) + 2], STG[:, k % 2], ACT.Copy,
                                             scale=S_W).then_inc(whi, 1)

                    def attend(n, p, last):
                        if last and n % 4 == 2 and n < NQ:
                            split_out(4 + n // 4)
                        m = n - 2
                        if 0 <= m < NQ:
                            q = Q_ORDER[m][1]
                            act.wait_ge(p_turned, BASE + NQ * p + m + 1)
                            act.wait_ge(o_ready, BASE + NQ * p + m - 2)
                            nc.scalar.activation(PRT[:, m % 3, 0, 0:q + 1],
                                                 PT[m % 2].rearrange("p b (k n) -> p (b k) n", k=4)[:, 0:q + 1], ACT.Copy).then_inc(prt_ready, 1)
                        if n < NQ:
                            w = (Q_ORDER[n][1] + 1) * P
                            act.wait_ge(neg_ready, BASE + NQ * p + n + 1)
                            if n >= 8:
                                act.wait_ge(rcp_ready, BASE + NQ * p + n - 7)
                            else:
                                act.wait_ge(rcp_ready, BASE + NQ * p)
                            nc.scalar.activation(PR[:, n % 3, 0:w], PR[:, n % 3, 0:w], ACT.Exp, scale=ATT_SCALE,
                                                 bias=NMX[:, n % 3:n % 3 + 1], accum_out=SUM[:, n % 8:n % 8 + 1]).then_inc(exp_ready, 1)

                    def body(act, p, kind):
                        last = kind == "last"
                        if kind != "after":
                            act.wait_ge(out_st, BASE + 80 * p)
                            act.wait_ge(v_lo, BASE + p)
                            act.wait_ge(scored, BASE + NQ * p)
                        for s in range(NT + 2):
                            if kind != "first" and s < 2:
                                attend(NQ + s, p - 1, False)
                            if kind != "first" and s == 6:
                                act.wait_ge(att_turned, BASE + p)
                                nc.scalar.activation(MT[:, 0, HP + p - 1, :], MB.rearrange("p b n -> p (b n)"), ACT.Copy,
                                                     scale=S_ACT).then_inc(mhi, 1)
                            if kind == "after":
                                continue
                            if s <= NT:
                                n = P if s < NT else NB
                                act.wait_ge(halves, BASE + 18 * p + 2 * s + 2)
                                nc.scalar.activation(QKV[:n, s], Z[:n, s % 2, 0:384], ACT.Copy, scale=UNSCALE).then_inc(copied, 1)
                            t = s - 1
                            if 0 <= t < NT:
                                act.wait_ge(z_turned, BASE + 8 * p + t + 1)
                                nc.scalar.activation(QKT[:, 0, :, t * P:(t + 1) * P], TB.rearrange("p (j n) -> p j n", j=2),
                                                     ACT.Copy).then_inc(qkt_ready, 1)
                            if kind in ("first", "middle") and s in (1, 3, 5, 7):
                                c = s // 2
                                act.wait_ge(w_in_s[c % 2], BASE + 64 * p + 32 * (c // 2) + 32)
                                nc.scalar.activation(WS[:, (p + 1) % 2, 0, 2 * c:2 * c + 2, 0:384], STG[:, c % 2, :, 0:384],
                                                     ACT.Copy, scale=S_W).then_inc(whi, 1)
                            if last and s in (1, 3, 5, 7):
                                split_out(s // 2)
                        if kind != "after":
                            for n in range(NQ):
                                attend(n, p, last)
                    staggered(body)(act)

                @block.vector
                def _(dve):
                    dve.wait_ge(tab_in, BASE + 32)

                    def split_out(k):
                        dve.wait_ge(whi, BASE + 4 * (HP - 1) + k + 1)
                        w = WS[:, k // 4, :, 2 * (k % 4):2 * (k % 4) + 2]
                        nc.vector.scalar_tensor_tensor(w[:, 1], STG[:, k % 2], S_W, w[:, 0], ALU.mult,
                                                       ALU.subtract).then_inc(w_free, 1)

                    def attend(n, p, last):
                        m = n - 3
                        if 0 <= m < NQ:
                            q = Q_ORDER[m][1]
                            dve.wait_ge(prt_ready, BASE + NQ * p + m + 1)
                            nc.vector.tensor_tensor(PRT[:, m % 3, 1, 0:q + 1],
                                                    PT[m % 2].rearrange("p b (k n) -> p (b k) n", k=4)[:, 0:q + 1],
                                                    PRT[:, m % 3, 0, 0:q + 1], ALU.subtract).then_inc(prt_low, 1)
                        if n < NQ:
                            q = Q_ORDER[n][1]
                            w = (q + 1) * P
                            dve.wait_ge(scored, BASE + NQ * p + n + 1)
                            dve.wait_ge(p_turned, BASE + NQ * p + n - 2)
                            dve.wait_ge(neg_ready, BASE + NQ * p + n - 1)
                            dve.sem_inc(dve_go, 1)
                            nc.vector.tensor_tensor_reduce(
                                out=PR[:, n % 3, 0:w], in0=SB[n % 2].rearrange("p b n -> p (b n)")[:, 0:w],
                                in1=MASK[:, SEQ - w:SEQ], scale=1.0, scalar=3 * NEG, op0=ALU.add, op1=ALU.max,
                                accum_out=MX[:, n % 2:n % 2 + 1]).then_inc(masked, 1)
                            dve.wait_ge(masked, BASE + NQ * p + n + 1)
                            nc.vector.tensor_scalar(NMX[:, n % 3:n % 3 + 1], MX[:, n % 2:n % 2 + 1], -ATT_SCALE, LOG_S_P,
                                                    ALU.mult, ALU.add).then_inc(neg_ready, 1)
                        m = n - 5
                        if 0 <= m < NQ:
                            h, q = Q_ORDER[m]
                            nc.vector.reciprocal(RCP[:, m % 2:m % 2 + 1], SUM[:, m % 8:m % 8 + 1]).then_inc(rcp_ready, 1)
                            dve.wait_ge(rcp_ready, BASE + NQ * p + m + 1)
                            dve.wait_ge(o_ready, BASE + NQ * p + m + 1)
                            nc.vector.tensor_scalar(ATT[:, q, h * E:(h + 1) * E], OB[:, m % 2], RCP[:, m % 2:m % 2 + 1], None,
                                                    ALU.mult).then_inc(att_ready, 1)
                        if last and n % 4 == 2 and n < NQ:
                            split_out(4 + n // 4)

                    def body(dve, p, kind):
                        last = kind == "last"
                        for s in range(NT + 1):
                            if kind != "first" and s < 5:
                                attend(NQ + s, p - 1, False)
                            if kind != "first" and s == 6:
                                dve.wait_ge(mhi, BASE + p)
                                nc.vector.scalar_tensor_tensor(MT[:, 1, HP + p - 1, :], MB.rearrange("p b n -> p (b n)"), S_ACT,
                                                               MT[:, 0, HP + p - 1, :], ALU.mult, ALU.subtract).then_inc(mlo, 1)
                            if kind == "after":
                                continue
                            n = P if s < NT else NB
                            dve.wait_ge(z_ready, BASE + 9 * p + s + 1)
                            dve.wait_ge(rotated, BASE + 18 * p + 2 * s)
                            z = Z[:n, s % 2, 0:256].rearrange("p (g e) -> p g e", g=4)[:, :, 0:16].rearrange("p g (a e) -> p g a e", a=2)
                            c, d = (x[:n].rearrange("p (g a e) -> p g a e", a=2, e=8) for x in (T1, T2))
                            for j, dst in ((0, c), (1, d)):
                                nc.vector.tensor_tensor(dst, z, ROPE[:n, s, j].unsqueeze(1).unsqueeze(1).broadcast_to([n, 4, 2, 8]),
                                                        ALU.mult).then_inc(halves, 1)
                            dve.wait_ge(halves, BASE + 18 * p + 2 * s + 2)
                            dve.wait_ge(copied, BASE + 9 * p + s + 1)
                            o = QKV[:n, s, 0:256].rearrange("p (g e) -> p g e", g=4)
                            nc.vector.tensor_tensor(o[:, :, 0:8], c[:, :, 0], d[:, :, 1], ALU.subtract).then_inc(rotated, 1)
                            nc.vector.tensor_tensor(o[:, :, 8:16], c[:, :, 1], d[:, :, 0], ALU.add).then_inc(rotated, 1)
                            if s >= 1:
                                dve.wait_ge(qkt_ready, BASE + 8 * p + s)
                                w = QKT[:, :, :, (s - 1) * P:s * P]
                                nc.vector.tensor_tensor(w[:, 1], TB.rearrange("p (j n) -> p j n", j=2), w[:, 0], ALU.subtract).then_inc(qkt_low, 1)
                            if not last and s in (1, 3, 5, 7):
                                k = s // 2
                                dve.wait_ge(whi, BASE + 4 * p + k + 1)
                                w = WS[:, (p + 1) % 2, :, 2 * k:2 * k + 2, 0:384]
                                nc.vector.scalar_tensor_tensor(w[:, 1], STG[:, k % 2, :, 0:384], S_W, w[:, 0],
                                                               ALU.mult, ALU.subtract).then_inc(w_free, 1)
                            if last and s in (1, 3, 5, 7):
                                split_out(s // 2)
                        if kind != "after":
                            for n in range(NQ):
                                attend(n, p, last)
                    staggered(body)(dve)
        proj.close()
        end_stage()
        stage[0] = "samples"
        R8 = NB * H
        PAT = 3
        LOG3 = float(np.log(3.0)) / ATT_SCALE
        with ExitStack() as st:
            ROW = sb(st, "ROW", [P, 7, E])
            GAM = sb(st, "GAM", [P, 1])
            OWN = sb(st, "OWN", [P, H])
            QKH = sb(st, "QKH", [P, 2, E // 2])
            SS = sb(st, "SS", [P, E // 2, E])
            OUTER = sb(st, "OUTER", [P, E // 2, E])
            MIX = sb(st, "MIX", [P, 2, 2, E])
            RO = sb(st, "RO", [P, E])
            BST = sb(st, "BST", [P, 6])
            MV = sb(st, "MV", [P, 2])
            VE = sb(st, "VE", [P, 1])
            RSTD = sb(st, "RSTD", [P, 1])
            QB = sb(st, "QB", [P, NB, HW])
            KC = sb(st, "KC", [P, 2, PAT, HW])
            VC = sb(st, "VC", [P, 2, PAT, HW])
            PRD = sb(st, "PRD", [P, PAT, HW])
            SC = sb(st, "SC", [P, PAT, R8])
            SR = sb(st, "SR", [P, PAT * P + 1])
            QN = sb(st, "QN", [P, E])
            MX = sb(st, "MX", [P, 2])
            SUM = sb(st, "SUM", [P, 2])
            PBD = PRD[:].rearrange("p a n -> p (a n)").rearrange("p (b a r) -> p b a r", a=PAT, r=R8)
            AO = sb(st, "AO", [P, E])
            OM = OUTER[:, 0:H]
            (tab_in, row_in, ss_in, k_free, v_free, s_done, s_turned, sr_ready, chain, exp_done, p_turned, pbd_ready,
             pv_done, var_ready, rstd_ready, ret_done, att_done, state_out, ms_turned, mhi, new_ready,
             half_sums, summed, pbd_zero, pool_c) = sems(
                "tab_in row_in ss_in k_free v_free s_done s_turned sr_ready chain exp_done p_turned pbd_ready "
                    "pv_done var_ready rstd_ready ret_done att_done state_out ms_turned mhi new_ready "
                    "half_sums summed pbd_zero pool_c")
            k_in = sems("k_in0 k_in1")
            v_in = sems("v_in0 v_in1 v_in2 v_in3")

            def mix_parts(odd, j):
                r = slice(odd * E, (odd + 1) * E)
                src = MPS[r, j * R8:(j + 1) * R8].rearrange("p (b k t) -> p t k b", b=NB, t=2)[:, odd]
                return src, MTS[r, :, j * HP:(j + 1) * HP]

            def v_slot(b):
                return (VC if b % 4 < 2 else KC)[:, b % 2]

            SPS, PTS, OPS = PS[:R8, 4, 0:PAT * P], PS[:, 5, 0:PAT * R8], PS[:R8, 6]
            MPS = PS[:, 4, 0:2 * R8]
            RPS = PS[:R8, 7, 0:E]

            def cached(src, b, pat):
                step = (1, 4, 16)[pat]
                return src[0, b, WIN - P * step:WIN].rearrange("(i d) h e -> i d (h e)", d=step)[:, 0]

            with nc.Block() as block:
                @block.sync
                def _(sp):
                    def load_k(b):
                        sp.wait_ge(k_free, BASE + b - 1)
                        for pat in range(PAT):
                            sp.dma_start(KC[:, b % 2, pat], cached(cache_k, b, pat)).then_inc(k_in[b % 2], 16)
                        sp.dma_start(QB[:, b], scratch[4, b:b + 1].broadcast_to([P, HW])).then_inc(k_in[b % 2], 16)

                    def load_v(b):
                        if b < 2:
                            pass
                        elif b < 4:
                            sp.wait_ge(k_free, BASE + NB - 4 + b + 1)
                        else:
                            sp.wait_ge(v_free, BASE + b - 3)
                        for pat in range(PAT):
                            sp.dma_start(v_slot(b)[:, pat], cached(cache_v, b, pat)).then_inc(v_in[b % 4], 16)

                    load_k(0)
                    load_k(1)
                    sp.dma_start(OWN[:R8], c_own).then_inc(tab_in, 16)
                    for half in range(2):
                        r = slice(half * R8, (half + 1) * R8)
                        d = slice(half * E // 2, (half + 1) * E // 2)
                        sp.dma_start(GAM[r], c_gsample, allow_slow_non_contiguous=True).then_inc(ss_in, 16)
                        sp.dma_start(ROW[r], scratch.rearrange("j b (h e) -> (b h) j e", e=E)).then_inc(row_in, 16)
                        sp.dma_start(QKH[r], scratch[0:2].rearrange("j b (h e) -> (b h) j e", e=E)[:, :, d]).then_inc(ss_in, 16)
                        sp.dma_start(SS[r], state_ret.rearrange("a b h d e -> (a b h) d e")[:, d]).then_inc(ss_in, 16)
                    for b in range(2, NB):
                        load_k(b)
                    for b in range(NB):
                        load_v(b)
                    sp.wait_ge(new_ready, BASE + 1)
                    for half in range(2):
                        sp.dma_start(ret_s.rearrange("a b h d e -> (a b h) d e")[:, half * E // 2:(half + 1) * E // 2],
                                     SS[half * R8:(half + 1) * R8]).then_inc(state_out, 16)
                    sp.wait_ge(state_out, BASE + 32)
                    clear_before(sp)

                @block.gpsimd
                def _(pool):
                    count_from_base(pool)
                    done = [0]

                    def then(ins):
                        done[0] += 1
                        ins.then_inc(pool_c, 1)
                        pool.wait_ge(pool_c, BASE + done[0])

                    pool.wait_ge(row_in, BASE + 32)
                    pool.wait_ge(ss_in, BASE + 96)
                    whole = [P, E // 2, E]
                    then(nc.gpsimd.tensor_scalar(QKH[:, 1], QKH[:, 1], E ** -0.5, None, ALU.mult))
                    then(nc.gpsimd.tensor_tensor(OUTER[:], QKH[:, 1].unsqueeze(2).broadcast_to(whole),
                                                 ROW[:, 2].unsqueeze(1).broadcast_to(whole), ALU.mult))
                    then(nc.gpsimd.tensor_tensor(SS[:], SS[:], GAM[:].unsqueeze(2).broadcast_to(whole), ALU.mult))
                    nc.gpsimd.tensor_tensor(SS[:], SS[:], OUTER[:], ALU.add).then_inc(new_ready, 1)
                    pool.wait_ge(new_ready, BASE + 1)
                    then(nc.gpsimd.tensor_tensor(OUTER[:], SS[:], QKH[:, 0].unsqueeze(2).broadcast_to(whole), ALU.mult))
                    w = E // 4
                    while w > 1:
                        then(nc.gpsimd.tensor_tensor(OUTER[:, 0:w], OUTER[:, 0:w], OUTER[:, w:2 * w], ALU.add))
                        w //= 2
                    nc.gpsimd.tensor_tensor(OUTER[:, 0], OUTER[:, 0], OUTER[:, 1], ALU.add).then_inc(half_sums, 1)
                    pool.wait_ge(s_done, BASE + NB)
                    nc.gpsimd.memset(PBD, 0.0).then_inc(pbd_zero, 1)
                    pool.wait_ge(var_ready, BASE + 1)
                    nc.gpsimd.tensor_tensor(RSTD[:R8], VE[:R8], EPSC[:R8, 0:1], ALU.pow).then_inc(rstd_ready, 1)

                @block.vector
                def _(dve):
                    done = [0]

                    def then(ins):
                        done[0] += 1
                        ins.then_inc(chain, 1)
                        dve.wait_ge(chain, BASE + done[0])

                    for b in range(NB):
                        dve.wait_ge(k_in[b % 2], BASE + 64 * (b // 2 + 1))
                        dve.wait_ge(s_done, BASE + b)
                        nc.vector.tensor_tensor(PRD[:], KC[:, b % 2], QB[:, b].unsqueeze(1).broadcast_to([P, PAT, HW]),
                                                ALU.mult).then_inc(k_free, 1)
                        dve.wait_ge(k_free, BASE + b + 1)
                        nc.vector.reduce_sum(SC[:, :, b * H:(b + 1) * H], PRD[:].rearrange("p a (h e) -> p a h e", e=E),
                                             AX_X).then_inc(s_done, 1)
                    dve.wait_ge(row_in, BASE + 32)
                    then(nc.vector.tensor_tensor(QN[:R8], ROW[:R8, 4], ROW[:R8, 5], ALU.mult))
                    then(nc.vector.reduce_sum(MX[:R8, 1:2], QN[:R8], AX_X))
                    then(nc.vector.tensor_scalar(SR[:R8, PAT * P:], MX[:R8, 1:2], LOG3, None, ALU.add))
                    dve.wait_ge(s_turned, BASE + 1)
                    then(nc.vector.tensor_copy(SR[:R8, 0:PAT * P], SPS))
                    then(nc.vector.reduce_max(MX[:R8, 0:1], SR[:R8], AX_X))
                    nc.vector.tensor_scalar(SUM[:R8, 1:2], MX[:R8, 0:1], -ATT_SCALE, None, ALU.mult).then_inc(sr_ready, 1)
                    dve.wait_ge(exp_done, BASE + 1)
                    then(nc.vector.reciprocal(MX[:R8, 0:1], SUM[:R8, 0:1]))
                    nc.vector.tensor_scalar(SR[:R8], SR[:R8], MX[:R8, 0:1], None, ALU.mult).then_inc(sr_ready, 1)
                    dve.wait_ge(p_turned, BASE + 1)
                    dve.wait_ge(pbd_zero, BASE + 1)
                    for b in range(NB):
                        nc.vector.tensor_copy(PBD[:, b, :, b * H:(b + 1) * H],
                                              PTS.rearrange("p (a r) -> p a r", a=PAT)[:, :, b * H:(b + 1) * H]).then_inc(pbd_ready, 1)
                    dve.wait_ge(summed, BASE + 1)
                    then(nc.vector.bn_stats(BST[:R8], RPS))
                    then(nc.vector.bn_aggr(MV[:R8], BST[:R8]))
                    nc.vector.tensor_scalar(VE[:R8], MV[:R8, 1:2], EPS, None, ALU.add).then_inc(var_ready, 1)
                    dve.wait_ge(rstd_ready, BASE + 1)
                    then(nc.vector.tensor_scalar(RO[:R8], RPS, MV[:R8, 0:1], RSTD[:R8], ALU.subtract, ALU.mult))
                    nc.vector.tensor_tensor(MIX[:R8, 0], RO[:R8].unsqueeze(1).broadcast_to([R8, 2, E]),
                                            ROW[:R8, 3].unsqueeze(1).broadcast_to([R8, 2, E]), ALU.mult).then_inc(ret_done, 1)
                    dve.wait_ge(pv_done, BASE + 1)
                    dve.wait_ge(tab_in, BASE + 16)
                    then(nc.vector.tensor_tensor(OM[:R8], OPS.rearrange("p (h e) -> p h e", h=H),
                                                 OWN[:R8].unsqueeze(2).broadcast_to([R8, H, E]), ALU.mult))
                    then(nc.vector.reduce_sum(AO[:R8], OM[:R8].rearrange("p h e -> p e h"), AX_X))
                    for twice in range(2):
                        nc.vector.scalar_tensor_tensor(MIX[:R8, 1, twice], ROW[:R8, 6], SR[:R8, PAT * P:], AO[:R8], ALU.mult,
                                                       ALU.add).then_inc(att_done, 1)
                    dve.wait_ge(mhi, BASE + 4)
                    for odd in range(2):
                        for j in range(2):
                            src, dst = mix_parts(odd, j)
                            nc.vector.scalar_tensor_tensor(dst[:, 1], src, S_ACT, dst[:, 0], ALU.mult, ALU.subtract)

                @block.scalar
                def _(act):
                    act.wait_ge(sr_ready, BASE + 1)
                    nc.scalar.activation(SR[:R8], SR[:R8], ACT.Exp, scale=ATT_SCALE, bias=SUM[:R8, 1:2],
                                         accum_out=SUM[:R8, 0:1]).then_inc(exp_done, 1)
                    act.wait_ge(ms_turned, BASE + 1)
                    for odd in range(2):
                        for j in range(2):
                            src, dst = mix_parts(odd, j)
                            nc.scalar.activation(dst[:, 0], src, ACT.Copy, scale=S_ACT).then_inc(mhi, 1)

                @block.tensor
                def _(pe):
                    for u in range(2):
                        mix_product(u, P, u * P)
                    pe.wait_ge(half_sums, BASE + 1)
                    for half in range(2):
                        mm = nc.tensor.matmul(RPS, IDENT[:, half * R8:(half + 1) * R8], OUTER[:, 0], start=(half == 0), stop=(half == 1))
                    mm.then_inc(summed, 1)
                    pe.wait_ge(s_done, BASE + NB)
                    for a in range(PAT):
                        mm = nc.tensor.transpose(SPS[:, a * P:(a + 1) * P], SC[:, a], IDENT[:])
                    mm.then_inc(s_turned, 1)
                    pe.wait_ge(sr_ready, BASE + 2)
                    for a in range(PAT):
                        mm = nc.tensor.transpose(PTS[:, a * R8:(a + 1) * R8], SR[:R8, a * P:(a + 1) * P], IDENT[:R8, :R8])
                    mm.then_inc(p_turned, 1)
                    for b in range(NB):
                        pe.wait_ge(pbd_ready, BASE + b + 1)
                        pe.wait_ge(v_in[b % 4], BASE + 48 * (b // 4 + 1))
                        for a in range(PAT):
                            mm = nc.tensor.matmul(OPS, PBD[:, b, a], v_slot(b)[:, a], start=(b == 0 and a == 0),
                                                  stop=(b == NB - 1 and a == PAT - 1))
                        mm.then_inc(v_free, 1)
                    pe.wait_ge(v_free, BASE + NB)
                    pe.sem_inc(pv_done, 1)
                    pe.wait_ge(ret_done, BASE + 1)
                    pe.wait_ge(att_done, BASE + 2)
                    for j in range(2):
                        mm = nc.tensor.transpose(MPS[:, j * R8:(j + 1) * R8], MIX[:R8, j].rearrange("p c e -> p (c e)"), IDENT[:R8, :R8])
                    mm.then_inc(ms_turned, 1)
        end_stage()
        stage[0] = "mixer"
        UW = WS[:, 0].rearrange("p a (c k) (d n) -> p c a (k d) n", c=2, d=2)
        w_up_v = w_up.rearrange("a (k p) (x n) -> p (a k) x n", p=P, x=2)
        with ExitStack() as st:
            WG = sb(st, "WG", [P, 2, KD + PLE // P, D], F16)
            STG = sb(st, "STG", [P, 2, D])
            LNP = sb(st, "LNP", [P, 2, D])
            R = sb(st, "R", [P, D])
            H1 = sb(st, "H1", [P, D])
            PR = sb(st, "PR", [P, 2, PLE])
            PT = sb(st, "PT", [P, 2, 2, PLE // P, P], F16)
            BST = sb(st, "BST", [P, 2, 6])
            MV = sb(st, "MV", [P, 2])
            VE = sb(st, "VE", [P, 1])
            RSTD = sb(st, "RSTD", [P, 1])
            (ln_in, whi, wlo, mixed, r_ready, stats, stats_go, aggr, var_ready, rstd_ready, xn_ready, gained,
             h1_ready, h1_kept, turned, hi_ready, lo_ready, p_turned, phi, plo, gated, embedded, sig_ready,
             e_ready, row_ready, pe_go, up_in, up_hi) = sems(
                "ln_in whi wlo mixed r_ready stats stats_go aggr var_ready rstd_ready xn_ready gained "
                    "h1_ready h1_kept turned hi_ready lo_ready p_turned phi plo gated embedded sig_ready "
                    "e_ready row_ready pe_go up_in up_hi")
            w_in_s = sems("w_in_s0 w_in_s1")
            p_in = sems("p_in0 p_in1 p_in2")
            TB, GB, EB, PB = PS[:, 4:6], PS[:, 2:4], PS[:, 0:2], PS[:, 6, 0:PLE]
            chunks = [w_ple_gate[0, k * P:(k + 1) * P] for k in range(KD)] + [w_ple_proj[0, k * P:(k + 1) * P] for k in range(PLE // P)]
            NW = len(chunks)
            UP = STG[:].rearrange("p a (k n) -> p (a k) n", n=2 * P)

            with nc.Block() as block:
                @block.sync
                def _(sp):
                    for j, v in ((0, ln1_g), (1, ln1_b)):
                        sp.dma_start(LNP[:, j], v.broadcast_to([P, D])).then_inc(ln_in, 16)
                    for c, src in enumerate(chunks):
                        if c >= 2:
                            sp.wait_ge(wlo, BASE + c - 1)
                        sp.dma_start(STG[:, c % 2], src).then_inc(w_in_s[c % 2], 16)
                    for u in range(2):
                        sp.dma_start(PR[:, u], p_prompt[0, 0, u * P:(u + 1) * P]).then_inc(p_in[u], 16)
                    sp.wait_ge(wlo, BASE + NW)
                    for x in range(2):
                        sp.dma_start(UP[:, :, x * P:(x + 1) * P], w_up_v[:, :, x, 0:P]).then_inc(up_in, 16)
                    with sp.Fori(1, NT // 2) as i:
                        for u in range(2):
                            sp.wait_ge(p_turned, BASE + 2 * i + u - 1)
                            sp.dma_start(PR[:, u], p_prompt[0, 0, ds((2 * i + u) * P, P)]).then_inc(p_in[u], 16)
                    sp.wait_ge(p_turned, BASE + NT - 1)
                    sp.dma_start(PR[:NB, 0], p_sample[0, :, 0]).then_inc(p_in[2], 16)
                    clear_before(sp)

                @block.tensor
                def _(pe):
                    def mix(t, u, n):
                        pe.wait_ge(r_ready, BASE + t - 1)
                        pe.sem_inc(pe_go, 1)
                        mix_product(u, n, t * P).then_inc(mixed, 1)

                    def turn(t, n):
                        pe.wait_ge(h1_ready, BASE + t + 1)
                        pe.wait_ge(lo_ready, BASE + t)
                        for k in range(KD):
                            mm = nc.tensor.transpose(TB[:, k // 4, (k % 4) * P:(k % 4) * P + n], H1[:n, k * P:(k + 1) * P],
                                                     IDENT[:n, :n])
                        mm.then_inc(turned, 1)

                    def turn_p(t, u, n, sem, count):
                        pe.wait_ge(sem, BASE + count)
                        pe.wait_ge(plo, BASE + t)
                        for k in range(PLE // P):
                            mm = nc.tensor.transpose(PB[:, k * P:k * P + n], PR[:n, u, k * P:(k + 1) * P], IDENT[:n, :n])
                        mm.then_inc(p_turned, 1)

                    def embed(t, u, n, between=None):
                        pe.wait_ge(lo_ready, BASE + t + 1)
                        pe.wait_ge(sig_ready, BASE + t)
                        pe.sem_inc(pe_go, 1)
                        for c in range(2):
                            mm = product(GB[:, c], n, lambda a, k: HT[:, a, k, ds(t * P, n)],
                                         lambda b, k, c: WG[:, b, k, c * 512:(c + 1) * 512], c, KD)
                        mm.then_inc(gated, 1)
                        if between:
                            between()
                        pe.wait_ge(plo, BASE + t + 1)
                        pe.wait_ge(e_ready, BASE + t)
                        pe.sem_inc(pe_go, 1)
                        for c in range(2):
                            mm = product(EB[:, c], n, lambda a, k: PT[:, u, a, k, 0:n],
                                         lambda b, k, c: WG[:, b, KD + k, c * 512:(c + 1) * 512], c, PLE // P)
                        mm.then_inc(embedded, 1)

                    pe.sem_inc(mixed, 2)
                    with pe.Fori(1, NT // 2) as i:
                        for u in range(2):
                            mix(2 * i + u, u, P)
                            turn(2 * i + u - 2, P)
                    mix(NT, 0, NB)
                    turn(NT - 2, P)
                    turn_p(0, 0, P, p_in[0], 16)
                    pe.wait_ge(wlo, BASE + KD)
                    pe.wait_ge(r_ready, BASE + NT)

                    def finish_mix():
                        turn(NT - 1, P)
                        turn_p(1, 1, P, p_in[1], 16)
                        pe.wait_ge(wlo, BASE + NW)
                        pe.wait_ge(r_ready, BASE + NT + 1)

                    embed(0, 0, P, finish_mix)
                    with pe.Fori(0, NT // 2 - 1) as i:
                        for u in range(2):
                            turn_p(2 * i + u + 2, u, P, p_in[u], 16 * i + 32)
                            embed(2 * i + u + 1, 1 - u, P)
                    turn_p(NT, 0, NB, p_in[2], 16)
                    turn(NT, NB)
                    embed(NT - 1, 1, P)
                    embed(NT, 0, NB)

                @block.scalar
                def _(act):
                    def split(c, u, i):
                        act.wait_ge(w_in_s[u], BASE + 16 * i + 16)
                        nc.scalar.activation(WG[:, 0, c], STG[:, u], ACT.Copy, scale=S_W).then_inc(whi, 1)

                    def high(t, n):
                        act.wait_ge(h1_ready, BASE + t + 1)
                        nc.scalar.activation(HRES[:n, t], H1[:n], ACT.Copy).then_inc(h1_kept, 1)
                        act.wait_ge(turned, BASE + t + 1)
                        nc.scalar.activation(HT[:, 0, :, ds(t * P, n)], TB.rearrange("p b (k n) -> p (b k) n", k=4)[:, :, :n],
                                             ACT.Copy, scale=S_ACT).then_inc(hi_ready, 1)

                    def high_p(t, u, n):
                        act.wait_ge(p_turned, BASE + t + 1)
                        nc.scalar.activation(PT[:, u, 0, :, 0:n], PB.rearrange("p (k n) -> p k n", k=2)[:, :, :n], ACT.Copy,
                                             scale=S_ACT).then_inc(phi, 1)

                    def gate(t, n):
                        act.wait_ge(gated, BASE + t + 1)
                        act.wait_ge(e_ready, BASE + t)
                        nc.scalar.activation(R[:n], GB[:n].rearrange("p b n -> p (b n)"), ACT.Sigmoid, scale=UNSCALE).then_inc(sig_ready, 1)

                    split(0, 0, 0)
                    split(1, 1, 0)
                    with act.Fori(0, NT // 2) as i:
                        for u in range(2):
                            high(2 * i + u, P)
                            split(2 * i + u + 2, u, i + 1)
                    high_p(0, 0, P)
                    act.wait_ge(up_in, BASE + 32)
                    nc.scalar.activation(UW[:, 0, 0], UP, ACT.Copy, scale=S_W).then_inc(up_hi, 1)
                    act.wait_ge(h1_ready, BASE + NT + 1)
                    with act.Fori(0, NT // 2 - 1) as i:
                        for u in range(2):
                            high_p(2 * i + u + 1, 1 - u, P)
                            gate(2 * i + u, P)
                    high_p(NT - 1, 1, P)
                    gate(NT - 2, P)
                    high_p(NT, 0, NB)
                    high(NT, NB)
                    gate(NT - 1, P)
                    gate(NT, NB)

                @block.gpsimd
                def _(pool):
                    count_from_base(pool)
                    pool.wait_ge(ln_in, BASE + 32)

                    def shift(t, n):
                        pool.wait_ge(var_ready, BASE + t + 1)
                        nc.gpsimd.tensor_tensor(RSTD[:n], VE[:n], EPSC[:n, 0:1], ALU.pow).then_inc(rstd_ready, 1)
                        pool.wait_ge(gained, BASE + t + 1)
                        pool.wait_ge(turned, BASE + t)
                        pool.wait_ge(h1_kept, BASE + t)
                        nc.gpsimd.tensor_tensor(H1[:n], R[:n], LNP[:n, 1], ALU.add).then_inc(h1_ready, 1)

                    with pool.Fori(0, NT) as t:
                        shift(t, P)
                    shift(NT, NB)

                @block.vector
                def _(dve):
                    def split(c):
                        dve.wait_ge(whi, BASE + c + 1)
                        nc.vector.scalar_tensor_tensor(WG[:, 1, c], STG[:, c % 2], S_W, WG[:, 0, c], ALU.mult,
                                                       ALU.subtract).then_inc(wlo, 1)

                    def norm(t, u, n):
                        dve.wait_ge(mixed, BASE + t + 1)
                        dve.wait_ge(h1_ready, BASE + t)
                        nc.vector.scalar_tensor_tensor(R[:n], HRES[:n, t], ALPHA / UNSCALE, M[u][:n].rearrange("p b n -> p (b n)"),
                                                       ALU.mult, ALU.add).then_inc(r_ready, 1)
                        dve.wait_ge(r_ready, BASE + t + 1)
                        for c in range(2):
                            nc.vector.bn_stats(BST[:n, c], R[:n, c * 512:(c + 1) * 512]).then_inc(stats, 1)
                        dve.wait_ge(stats, BASE + 2 * t + 2)
                        dve.sem_inc(stats_go, 1)
                        nc.vector.bn_aggr(MV[:n], BST[:n].rearrange("p a b -> p (a b)")).then_inc(aggr, 1)
                        dve.wait_ge(aggr, BASE + t + 1)
                        nc.vector.tensor_scalar(VE[:n], MV[:n, 1:2], EPS / UNSCALE ** 2, None, ALU.add).then_inc(var_ready, 1)
                        dve.wait_ge(rstd_ready, BASE + t + 1)
                        nc.vector.tensor_scalar(R[:n], R[:n], MV[:n, 0:1], RSTD[:n], ALU.subtract, ALU.mult).then_inc(xn_ready, 1)
                        dve.wait_ge(xn_ready, BASE + t + 1)
                        dve.wait_ge(ln_in, BASE + 32)
                        nc.vector.tensor_tensor(R[:n], R[:n], LNP[:n, 0], ALU.mult).then_inc(gained, 1)

                    def low(t, n):
                        dve.wait_ge(hi_ready, BASE + t + 1)
                        nc.vector.scalar_tensor_tensor(HT[:, 1, :, ds(t * P, n)], TB.rearrange("p b (k n) -> p (b k) n", k=4)[:, :, :n],
                                                       S_ACT, HT[:, 0, :, ds(t * P, n)], ALU.mult, ALU.subtract).then_inc(lo_ready, 1)

                    def low_p(t, u, n):
                        dve.wait_ge(phi, BASE + t + 1)
                        nc.vector.scalar_tensor_tensor(PT[:, u, 1, :, 0:n], PB.rearrange("p (k n) -> p k n", k=2)[:, :, :n],
                                                       S_ACT, PT[:, u, 0, :, 0:n], ALU.mult, ALU.subtract).then_inc(plo, 1)

                    def add(t, n):
                        dve.wait_ge(embedded, BASE + t + 1)
                        dve.wait_ge(sig_ready, BASE + t + 1)
                        nc.vector.scalar_tensor_tensor(R[:n], EB[:n].rearrange("p b n -> p (b n)"), UNSCALE, R[:n],
                                                       ALU.mult, ALU.mult).then_inc(row_ready, 1)
                        dve.wait_ge(row_ready, BASE + t + 1)
                        nc.vector.scalar_tensor_tensor(HRES[:n, t], HRES[:n, t], ALPHA, R[:n], ALU.mult, ALU.add).then_inc(e_ready, 1)

                    norm(0, 0, P)
                    split(0)
                    split(1)
                    norm(1, 1, P)
                    low(0, P)
                    split(2)
                    with dve.Fori(1, NT // 2) as i:
                        for u in range(2):
                            norm(2 * i + u, u, P)
                            low(2 * i + u - 1, P)
                            split(2 * i + u + 1)
                    norm(NT, 0, NB)
                    low(NT - 1, P)
                    split(NW - 1)
                    low_p(0, 0, P)
                    dve.wait_ge(up_hi, BASE + 1)
                    nc.vector.scalar_tensor_tensor(UW[:, 0, 1], UP, S_W, UW[:, 0, 0], ALU.mult, ALU.subtract)
                    dve.wait_ge(h1_ready, BASE + NT + 1)
                    with dve.Fori(0, NT // 2 - 1) as i:
                        for u in range(2):
                            low_p(2 * i + u + 1, 1 - u, P)
                            add(2 * i + u, P)
                    low_p(NT - 1, 1, P)
                    add(NT - 2, P)
                    low_p(NT, 0, NB)
                    low(NT, NB)
                    add(NT - 1, P)
                    add(NT, NB)
        mid.close()
        end_stage()
        stage[0] = "ffn"
        GROUP = 6
        FULL = NCH // GROUP
        S_G = 8.0
        UNDOWN = 1.0 / (S_G * S_W)
        T = SEQ + NB
        T3 = T // 3
        assert T == 3 * T3 and T3 <= 512 and NB + 2 <= T3
        with ExitStack() as st:
            SU = sb(st, "SU", [P, 2, KD, 2 * P])
            SD = sb(st, "SD", [P, 2, D])
            WD = (WS[:, 1].rearrange("p a (k c) n -> p (a k) (c n)", c=2)[:, 0:GROUP], sb(st, "WD", [P, GROUP, D], F16))
            HG = sb(st, "HG", [P, 2, GROUP, T], F16)
            C = sb(st, "C", [P, 2, T + 2])
            CB = sb(st, "CB", [P, 2, NB])
            PRD = sb(st, "PRD", [P, T])
            UC = sb(st, "UC", [P, 2 + NB, 2 * NCH])
            UO = sb(st, "UO", [P, 2 + NB, P])
            LNP = sb(st, "LNP", [P, 2, D])
            Y = sb(st, "Y", [P, 2, D])
            BST = sb(st, "BST", [P, 2, 2, 6])
            MV = sb(st, "MV", [P, 2, 2])
            VE = sb(st, "VE", [P, 2])
            RSTD = sb(st, "RSTD", [P, 2])
            (ln_in, su_free, sd_free, uhi, dhi, a_ready, g_ready, first_tap, tap1, conved, kept, s_tap1, s_conved, gelu_done, prod_ready,
             hi_ready, lo_ready, downed, added, stats, stats_go, aggr, var_ready, rstd_ready, xn_ready, gained,
             y_ready, y_out, last_turned, last_read, pe_go, c_zero) = sems(
                "ln_in su_free sd_free uhi dhi a_ready g_ready first_tap tap1 conved kept s_tap1 s_conved gelu_done prod_ready "
                    "hi_ready lo_ready downed added stats stats_go aggr var_ready rstd_ready xn_ready gained "
                    "y_ready y_out last_turned last_read pe_go c_zero")
            u_in = sems("u_in0 u_in1")
            d_in = sems("d_in0 d_in1")
            y_st = sems("y_st0 y_st1")
            DB = (PS[:, 6:8], PS[:, 4:6])

            def U(x):
                return PS[:, 3 * x:3 * x + 3, 0:T3]

            def C_from(x, first):
                return C[:, x, first:first + T].rearrange("p (b n) -> p b n", b=3)

            def groups(eng, body):
                with eng.Fori(0, FULL) as g:
                    body(g, GROUP, False)
                body(FULL, NCH - GROUP * FULL, True)

            def chunk_loop(eng, g, n, last, body):
                if last:
                    for l in range(n):
                        body(GROUP * g + l, l % 2, l, l == n - 1)
                else:
                    with eng.Fori(0, n // 2) as i:
                        for u in range(2):
                            body(GROUP * g + 2 * i + u, u, 2 * i + u, False)

            def ln_tiles(eng, first, second):
                first(0, 0, P)
                with eng.Fori(0, NT // 2 - 1) as i:
                    for u in range(2):
                        first(2 * i + u + 1, 1 - u, P)
                        second(2 * i + u, u, P)
                first(NT - 1, 1, P)
                second(NT - 2, 0, P)
                first(NT, 0, NB)
                second(NT - 1, 1, P)
                second(NT, 0, NB)

            def tile_loop(eng, g, body):
                base = (NT + 1) * g
                with eng.Fori(0, NT // 2) as i:
                    for u in range(2):
                        body(base + 2 * i + u, 2 * i + u, u, P)
                body(base + NT, NT, 0, NB)

            with nc.Block() as block:
                @block.sync
                def _(sp):
                    sp.sem_inc(su_free, 3)
                    sp.sem_inc(sd_free, 2)
                    for j, v in ((0, ln2_g), (1, ln2_b)):
                        sp.dma_start(LNP[:, j], v.broadcast_to([P, D])).then_inc(ln_in, 16)
                    sp.dma_start(conv_s[0, :, 0], state_conv[0, :, 1]).then_inc(y_out, 16)

                    def load(c, u, l, final):
                        if not final:
                            sp.wait_ge(su_free, BASE + c + 2)
                            for x in range(2):
                                sp.dma_start(SU[:, 1 - u, :, x * P:(x + 1) * P],
                                             w_up_v[:, :, x, ds((c + 1) * P, P)]).then_inc(u_in[1 - u], 16)
                        sp.wait_ge(sd_free, BASE + c + 1)
                        sp.dma_start(SD[:, u], w_down[0, ds(c * P, P)]).then_inc(d_in[u], 16)

                    groups(sp, lambda g, n, last: chunk_loop(sp, g, n, last, load))
                    with sp.Fori(0, NT // 2) as i:
                        for u in range(2):
                            sp.wait_ge(y_ready, BASE + 2 * i + u + 1)
                            sp.dma_start(y_prompt[0, ds((2 * i + u) * P, P)], Y[:, u]).then_inc(y_st[u], 16)
                    sp.wait_ge(last_read, BASE + 1)
                    sp.dma_start(conv_p[0, 0].rearrange("r (c f) -> c r f", f=P), UO[:2 * NCH, 0:2]).then_inc(y_out, 16)
                    sp.dma_start(conv_s[0, :, 1].rearrange("b (c f) -> c b f", f=P), UO[:2 * NCH, 2:]).then_inc(y_out, 16)
                    sp.wait_ge(y_ready, BASE + NT + 1)
                    sp.dma_start(y_sample[:, 0], Y[:NB, 0]).then_inc(y_out, 16)
                    sp.wait_ge(y_out, BASE + 16 * 4)
                    for u in range(2):
                        sp.wait_ge(y_st[u], BASE + 8 * NT)
                    clear_before(sp)

                @block.tensor
                def _(pe):
                    def up(c, u, l, final):
                        for x, ready in ((0, a_ready), (1, g_ready)):
                            if x == 0:
                                pe.wait_ge(su_free, BASE + c + 3)
                            pe.wait_ge(conved, BASE + 2 * c + x - 1)
                            pe.wait_ge(s_conved, BASE + 2 * c + x - 1)
                            pe.sem_inc(pe_go, 1)
                            for third in range(3):
                                for k in range(KD):
                                    for a, b in PASSES:
                                        mm = nc.tensor.matmul(U(x)[:, third], UW[:, u, a, k, x * P:(x + 1) * P],
                                                              HT[:, b, k, third * T3:(third + 1) * T3],
                                                              start=(k == 0 and (a, b) == (0, 0)), stop=(k == KD - 1 and (a, b) == (1, 0)))
                            mm.then_inc(ready, 1)

                    def down(g, n, last):
                        def part(t, u, rows, chunks):
                            for l in chunks:
                                for half in range(2):
                                    for a, b in PASSES:
                                        mm = nc.tensor.matmul(DB[u][:rows, half], HG[:, a, l, ds(t * P, rows)],
                                                              WD[b][:, l, half * 512:(half + 1) * 512],
                                                              start=(l == 0 and (a, b) == (0, 0)), stop=(l == n - 1 and (a, b) == (1, 0)))
                            return mm

                        def tile(count, t, u, rows):
                            pe.wait_ge(added, BASE + count - 1)
                            pe.sem_inc(pe_go, 1)
                            part(t, u, rows, range(n)).then_inc(downed, 1)

                        pe.wait_ge(lo_ready, BASE + GROUP * g + n - 1)
                        pe.wait_ge(sd_free, BASE + GROUP * g + n + 1)
                        pe.sem_inc(pe_go, 1)
                        part(0, 0, P, range(n - 1))
                        pe.wait_ge(conved, BASE + 2 * (GROUP * g + n))
                        pe.wait_ge(s_conved, BASE + 2 * (GROUP * g + n))
                        pe.sem_inc(pe_go, 1)
                        part(1, 1, P, range(n - 1))
                        pe.wait_ge(lo_ready, BASE + GROUP * g + n)
                        pe.wait_ge(sd_free, BASE + GROUP * g + n + 2)
                        pe.sem_inc(pe_go, 1)
                        for t in range(2):
                            part(t, t, P, [n - 1]).then_inc(downed, 1)
                        with pe.Fori(1, NT // 2) as i:
                            for u in range(2):
                                tile((NT + 1) * g + 2 * i + u, 2 * i + u, u, P)
                        if last:
                            pe.wait_ge(kept, BASE + 2 * NCH)
                            pe.wait_ge(conved, BASE + 2 * NCH)
                            for r in range(2 + NB):
                                mm = nc.tensor.transpose(PS[:2 * NCH, r // 4, (r % 4) * P:(r % 4 + 1) * P], UC[:, r], IDENT[:])
                            mm.then_inc(last_turned, 1)
                        tile((NT + 1) * g + NT, NT, 0, NB)

                    def group(g, n, last):
                        pe.wait_ge(added, BASE + (NT + 1) * g - 1)
                        pe.sem_inc(pe_go, 1)
                        chunk_loop(pe, g, n, last, up)
                        pe.wait_ge(added, BASE + (NT + 1) * g)
                        pe.sem_inc(pe_go, 1)
                        down(g, n, last)
                    groups(pe, group)

                @block.scalar
                def _(act):
                    def up_high(c, u):
                        act.wait_ge(u_in[u], BASE + 16 * (c + u))
                        act.wait_ge(g_ready, BASE + c - 1)
                        nc.scalar.activation(UW[:, u, 0], SU[:, u], ACT.Copy, scale=S_W).then_inc(uhi, 1)

                    def step(c, u, l, final, g):
                        if not final:
                            up_high(c + 1, 1 - u)
                        for x, ready in ((0, a_ready), (1, g_ready)):
                            act.wait_ge(ready, BASE + c + 1)
                            if x == 0:
                                act.wait_ge(prod_ready, BASE + c)
                            ch = ds(c + x * NCH, 1)
                            nc.scalar.activation(C_from(x, 0), U(x), ACT.Identity, scale=CWS[:, 2, ch], bias=CW[:, 3, ch])
                            nc.scalar.activation(CB[:, x], U(x)[:, 2, T3 - NB:], ACT.Identity, scale=CWS[:, 2, ch],
                                                 bias=CW[:, 3, ch]).then_inc(first_tap, 1)
                            if x == 0:
                                act.wait_ge(d_in[u], BASE + 8 * (c - u) + 16)
                                act.wait_ge(downed, BASE + (NT + 1) * g)
                                nc.scalar.activation(WD[0][:, l], SD[:, u], ACT.Copy, scale=S_W).then_inc(dhi, 1)
                        act.wait_ge(conved, BASE + 2 * c + 2)
                        act.wait_ge(s_conved, BASE + 2 * c + 2)
                        nc.scalar.activation(C[:, 1, 0:SEQ], C[:, 1, 0:SEQ], ACT.Gelu_apprx_tanh)
                        nc.scalar.activation(CB[:, 1], CB[:, 1], ACT.Gelu_apprx_tanh).then_inc(gelu_done, 1)
                        act.wait_ge(prod_ready, BASE + c + 1)
                        nc.scalar.activation(HG[:, 0, l], PRD[:], ACT.Copy).then_inc(hi_ready, 1)

                    groups(act, lambda g, n, last: chunk_loop(act, g, n, last, lambda c, u, l, f: step(c, u, l, f, g)))
                    act.wait_ge(last_turned, BASE + 1)
                    for b, k in ((0, 4), (1, 4), (2, 2)):
                        mm = nc.scalar.activation(UO[:2 * NCH, 4 * b:4 * b + k], PS[:2 * NCH, b, 0:k * P].rearrange("p (r n) -> p r n", r=k),
                                                  ACT.Copy)
                    mm.then_inc(last_read, 1)

                @block.gpsimd
                def _(pool):
                    count_from_base(pool)
                    def low(c, u, l, final):
                        pool.wait_ge(hi_ready, BASE + c + 1)
                        nc.gpsimd.tensor_tensor(HG[:, 1, l, :], PRD[:], HG[:, 0, l, :], ALU.subtract).then_inc(lo_ready, 1)

                    groups(pool, lambda g, n, last: chunk_loop(pool, g, n, last, low))
                    pool.wait_ge(ln_in, BASE + 32)

                    def scale(t, u, n):
                        pool.wait_ge(var_ready, BASE + t + 1)
                        nc.gpsimd.tensor_tensor(RSTD[:n, u:u + 1], VE[:n, u:u + 1], EPSC[:n, 0:1], ALU.pow).then_inc(rstd_ready, 1)

                    def shift(t, u, n):
                        pool.wait_ge(gained, BASE + t + 1)
                        pool.wait_ge(y_st[u], BASE + 8 * (t - u))
                        nc.gpsimd.tensor_tensor(Y[:n, u], HRES[:n, t], LNP[:n, 1], ALU.add).then_inc(y_ready, 1)

                    ln_tiles(pool, scale, shift)

                @block.vector
                def _(dve):
                    def up_low(c, u):
                        dve.wait_ge(uhi, BASE + c)
                        nc.vector.scalar_tensor_tensor(UW[:, u, 1].rearrange("p k n -> p (k n)"), SU[:, u].rearrange("p k n -> p (k n)"),
                                                       S_W, UW[:, u, 0].rearrange("p k n -> p (k n)"), ALU.mult,
                                                       ALU.subtract).then_inc(su_free, 1)

                    def step(c, u, l, final):
                        if not final:
                            up_low(c + 1, 1 - u)
                        for x in range(2):
                            ch = ds(c + x * NCH, 1)
                            dve.wait_ge(first_tap, BASE + 2 * c + x + 1)
                            nc.vector.tensor_scalar(UC[:, :, ch], U(x)[:, 2, T3 - NB - 2:].unsqueeze(2), UNSCALE, None, ALU.mult).then_inc(kept, 1)
                            nc.vector.scalar_tensor_tensor(C_from(x, 1), U(x), CWS[:, 1, ch], C_from(x, 1), ALU.mult, ALU.add).then_inc(tap1, 1)
                            nc.vector.scalar_tensor_tensor(CB[:, x].unsqueeze(2), ST[:, 1::2, ch], CW[:, 1, ch], CB[:, x].unsqueeze(2),
                                                           ALU.mult, ALU.add).then_inc(s_tap1, 1)
                            dve.wait_ge(tap1, BASE + 2 * c + x + 1)
                            nc.vector.scalar_tensor_tensor(C_from(x, 2), U(x), CWS[:, 0, ch], C_from(x, 2), ALU.mult, ALU.add).then_inc(conved, 1)
                            dve.wait_ge(s_tap1, BASE + 2 * c + x + 1)
                            nc.vector.scalar_tensor_tensor(CB[:, x].unsqueeze(2), ST[:, 0::2, ch], CW[:, 0, ch], CB[:, x].unsqueeze(2),
                                                           ALU.mult, ALU.add).then_inc(s_conved, 1)
                            if x == 0:
                                dve.wait_ge(dhi, BASE + c + 1)
                                nc.vector.scalar_tensor_tensor(WD[1][:, l, :], SD[:, u], S_W, WD[0][:, l, :], ALU.mult,
                                                               ALU.subtract).then_inc(sd_free, 1)
                        dve.wait_ge(gelu_done, BASE + c + 1)
                        dve.wait_ge(lo_ready, BASE + c)
                        nc.vector.scalar_tensor_tensor(PRD[:, SEQ:], CB[:, 0], S_G, CB[:, 1], ALU.mult, ALU.mult)
                        nc.vector.scalar_tensor_tensor(PRD[:, 0:SEQ], C[:, 0, 0:SEQ], S_G, C[:, 1, 0:SEQ], ALU.mult,
                                                       ALU.mult).then_inc(prod_ready, 1)

                    def add(count, t, u, n):
                        dve.wait_ge(downed, BASE + count + 1)
                        nc.vector.scalar_tensor_tensor(HRES[:n, t], DB[u][:n].rearrange("p b n -> p (b n)"), UNDOWN, HRES[:n, t],
                                                       ALU.mult, ALU.add).then_inc(added, 1)

                    def stats_of(t, u, n):
                        count = (NT + 1) * FULL + t
                        dve.wait_ge(downed, BASE + count + 1)
                        nc.vector.scalar_tensor_tensor(HRES[:n, t], DB[u][:n].rearrange("p b n -> p (b n)"), UNDOWN, HRES[:n, t],
                                                       ALU.mult, ALU.add).then_inc(added, 1)
                        dve.wait_ge(added, BASE + count + 1)
                        dve.sem_inc(stats_go, 1)
                        for c in range(2):
                            nc.vector.bn_stats(BST[:n, u, c], HRES[:n, t, c * 512:(c + 1) * 512]).then_inc(stats, 1)
                        dve.wait_ge(stats, BASE + 2 * t + 2)
                        dve.sem_inc(stats_go, 1)
                        nc.vector.bn_aggr(MV[:n, u], BST[:n, u].rearrange("p a b -> p (a b)")).then_inc(aggr, 1)
                        dve.wait_ge(aggr, BASE + t + 1)
                        nc.vector.tensor_scalar(VE[:n, u:u + 1], MV[:n, u, 1:2], EPS, None, ALU.add).then_inc(var_ready, 1)

                    def norm(t, u, n):
                        dve.wait_ge(rstd_ready, BASE + t + 1)
                        nc.vector.tensor_scalar(HRES[:n, t], HRES[:n, t], MV[:n, u, 0:1], RSTD[:n, u:u + 1], ALU.subtract,
                                                ALU.mult).then_inc(xn_ready, 1)
                        dve.wait_ge(xn_ready, BASE + t + 1)
                        nc.vector.tensor_tensor(HRES[:n, t], HRES[:n, t], LNP[:n, 0], ALU.mult).then_inc(gained, 1)

                    def group(g, n, last):
                        chunk_loop(dve, g, n, last, step)
                        if last:
                            ln_tiles(dve, stats_of, norm)
                        else:
                            tile_loop(dve, g, add)

                    dve.wait_ge(ln_in, BASE + 32)
                    nc.vector.memset(C[:, :, T:], 0.0).then_inc(c_zero, 1)
                    dve.wait_ge(c_zero, BASE + 1)
                    groups(dve, group)




def constants():
    f = np.float32

    def angles(pos, n_rot, base):
        half = n_rot // 2
        inv = (base ** (-np.arange(half, dtype=f) / f(half)).astype(np.float64)).astype(f)
        ang = (pos.astype(f)[:, None] * inv[None, :]).astype(np.float64)
        return np.stack([np.cos(ang), np.sin(ang)], 1)

    pos = np.concatenate([np.arange(SEQ), np.full(P, PAST)])
    rope_ret = (angles(pos, E, 10000.0) * UNSCALE).reshape(NT + 1, P, 2, E // 2).transpose(1, 0, 2, 3)
    rope_att = (angles(pos, E // 4, 500000.0) * UNSCALE).reshape(NT + 1, P, 2, E // 8).transpose(1, 0, 2, 3)
    lg = np.log(1.0 - 2.0 ** (-5.0 - np.arange(H)))
    i = np.arange(P)
    rel = i[None, :] - i[:, None]
    decay = np.where(rel[:, None, :] >= 0, np.exp(lg[None, :, None] * np.maximum(rel, 0)[:, None, :]), 0.0) * E ** -0.5
    head = 2 * np.arange(HP)[None, :] + (np.arange(P) // E)[:, None]
    gq = np.exp(lg[head][:, :, None] * (i + 1.0)[None, None, :])
    kdec = np.repeat(np.exp(lg[None, :] * (P - 1.0 - i[:, None])) * E ** -0.5, E, axis=1)
    gchunk = np.exp(lg[head] * P)
    dist = i[:, None] + (SEQ - P) - np.arange(SEQ)[None, :]
    count = sum(((dist >= 0) & (dist <= w) & (dist % d == 0)).astype(int) for w, d in ((128, 1), (512, 4), (2048, 16)))
    mask = np.where(count > 0, np.log(np.maximum(count, 1)) / ATT_SCALE, NEG)
    gsample = np.tile(np.exp(lg), NB)[:, None]
    own_head = np.tile(np.eye(H), (NB, 1))
    return [np.ascontiguousarray(a, dtype=f) for a in
            (np.eye(P), rope_ret, rope_att, decay, gq, kdec, gchunk, mask, gsample, own_head)]


_INS = ['x_prompt', 'x_sample', 'cache_k_win', 'cache_v_win', 'state_ret', 'state_conv', 'p_prompt', 'p_sample',
        'ln_in_g', 'ln_in_b', 'w_in', 'w_out', 'ln1_g', 'ln1_b', 'w_up', 'conv_w', 'conv_b', 'w_down',
        'w_ple_gate', 'w_ple_proj', 'ln2_g', 'ln2_b']
_CONSTS = ['ident', 'rope_ret', 'rope_att', 'decay', 'gq', 'kdec', 'gchunk', 'mask', 'gsample', 'own_head']
_OUTS = [(1, SEQ, D), (NB, 1, D), (1, 1, SEQ, H, E), (1, 1, SEQ, H, E), (1, 1, H, E, E), (1, 1, 2, 2 * D_FF),
         (1, NB, 1, H, E), (1, NB, 1, H, E), (1, NB, H, E, E), (1, NB, 2, 2 * D_FF)]


def kernel(**inputs):
    import concourse.bacc as bacc
    from concourse.bass_utils import run_bass_kernel_spmd

    nc = bacc.Bacc("TRN2", target_bir_lowering=False, num_devices=1)
    arrays, args = {}, []
    for name in _INS:
        arrays[f"in_{name}"] = np.ascontiguousarray(inputs[name])
    for name, table in zip(_CONSTS, constants()):
        arrays[f"table_{name}"] = table
    for name, a in arrays.items():
        args.append(nc.dram_tensor(name, a.shape, mybir.dt.from_np(a.dtype), kind="ExternalInput").ap())
    for i, shape in enumerate(_OUTS):
        args.append(nc.dram_tensor(f"out_{i}", shape, F32, kind="ExternalOutput").ap())
    build(nc, *args)
    r = run_bass_kernel_spmd(nc, [arrays], core_ids=[0])
    return tuple(r.results[0][f"out_{i}"] for i in range(len(_OUTS)))
```
